# Optimizing a Trainium2 kernel written in Bass

```python
import jax
import jax.numpy as jnp
from jax import lax
import numpy as np

D_MODEL = 1024
BATCH = 1
SEQ = 1024
DEPTH = 1
DEC_BATCH = 8
DEC_SEQ = 4
PAST_LEN = 512
PAGE_SIZE = 128

NSA_HEADS = 8
NSA_KV_HEADS = 2
NSA_GROUP = NSA_HEADS // NSA_KV_HEADS
NSA_HEAD_DIM = 64
NSA_WIDTH = NSA_HEADS * NSA_HEAD_DIM
NSA_KV_WIDTH = NSA_KV_HEADS * NSA_HEAD_DIM
CMP_BLOCK = 32
CMP_STRIDE = 16
CMP_HIDDEN = 2 * NSA_HEAD_DIM
SEL_BLOCK = 64
SEL_TOPN = 16
WINDOW = 512
GLA_HEADS = 4
GLA_KEY_WIDTH = D_MODEL // 2
GLA_VAL_WIDTH = D_MODEL
GLA_DK = GLA_KEY_WIDTH // GLA_HEADS
GLA_DV = GLA_VAL_WIDTH // GLA_HEADS
GLA_GATE_RANK = 16
GLA_GATE_TAU = 16.0
GLA_CHUNK = 32
Q_BLOCK = 128
NORM_EPS = 1e-6
NEG_INF = -1e30
TINY = 1e-30
FORCE_BONUS = 1e4
IN_SIZES = (NSA_WIDTH, 6 * NSA_KV_WIDTH, 3 * NSA_HEADS, NSA_WIDTH, GLA_KEY_WIDTH, GLA_KEY_WIDTH, GLA_VAL_WIDTH, GLA_GATE_RANK, GLA_VAL_WIDTH, 2 * D_MODEL)
D_IN = NSA_WIDTH * 2 + 6 * NSA_KV_WIDTH + 3 * NSA_HEADS + 2 * GLA_KEY_WIDTH + 2 * GLA_VAL_WIDTH + GLA_GATE_RANK + 2 * D_MODEL

kernel_name = 'hybrid_nsa_gla_gated_merge_step'

F32 = jnp.float32

def _split_offsets():
    return tuple(int(o) for o in np.cumsum(np.array(IN_SIZES))[:-1])

def rms_norm(x, g):
    xf = x.astype(F32)
    xf = xf * lax.rsqrt(jnp.mean(xf * xf, axis=-1, keepdims=True) + NORM_EPS)
    return xf.astype(x.dtype) * g

def alibi_slopes():
    h = jnp.arange(1, NSA_HEADS + 1, dtype=F32)
    return jnp.exp2(-8.0 * h / NSA_HEADS).reshape(NSA_KV_HEADS, NSA_GROUP)

def alibi_bias(slopes, dist):
    return -slopes[:, :, None, None] * dist[..., None, None, :, :].astype(F32)

def masked_softmax(s, mask):
    s = jnp.where(mask, s, NEG_INF)
    p = jnp.where(mask, jnp.exp(s - jnp.max(s, axis=-1, keepdims=True)), 0.0)
    return p / jnp.maximum(jnp.sum(p, axis=-1, keepdims=True), TINY)

def attend(q, k, v, bias, mask):
    scale = q.shape[-1] ** -0.5
    s = jnp.einsum('...qgrd,...kgd->...grqk', q.astype(F32), k.astype(F32)) * scale + bias
    p = masked_softmax(s, mask)
    o = jnp.einsum('...grqk,...kgd->...qgrd', p, v.astype(F32))
    return o, p

def compress_blocks(x, pe, w1, w2):
    B, L, G, hd = x.shape
    n_cmp = (L - CMP_BLOCK) // CMP_STRIDE + 1
    idx = np.arange(n_cmp)[:, None] * CMP_STRIDE + np.arange(CMP_BLOCK)[None, :]
    blocks = x[:, idx] + pe[:, None, :]
    flat = blocks.transpose(0, 1, 3, 2, 4).reshape(B, n_cmp, G, CMP_BLOCK * hd)
    return jax.nn.silu(flat @ w1) @ w2

def cmp_block_end(L):
    n_cmp = (L - CMP_BLOCK) // CMP_STRIDE + 1
    return np.arange(n_cmp) * CMP_STRIDE + CMP_BLOCK - 1

def sel_overlap(n_cmp, n_sel):
    cs = np.arange(n_cmp)[:, None] * CMP_STRIDE
    ss = np.arange(n_sel)[None, :] * SEL_BLOCK
    ov = np.clip(np.minimum(cs + CMP_BLOCK, ss + SEL_BLOCK) - np.maximum(cs, ss), 0, None)
    return jnp.asarray((ov / CMP_BLOCK).astype(np.float32))

def to_sel_blocks(x):
    B, L, G, hd = x.shape
    n_sel = -(-L // SEL_BLOCK)
    xp = jnp.pad(x, ((0, 0), (0, n_sel * SEL_BLOCK - L), (0, 0), (0, 0)))
    return xp.reshape(B, n_sel, SEL_BLOCK, G, hd)

def nsa_cmp_slc(q, q_pos, kc, vc, cmp_end, ks_blocks, vs_blocks, slopes):
    B, Tq, G, R, hd = q.shape
    dist_c = q_pos[:, None] - cmp_end[None, :]
    o_cmp, p_cmp = attend(q, kc, vc, alibi_bias(slopes, dist_c), (dist_c >= 0)[None, None])
    n_sel = ks_blocks.shape[1]
    imp = jnp.einsum('bgrqc,cs->bgqs', p_cmp, sel_overlap(kc.shape[1], n_sel))
    blk = np.arange(n_sel)
    valid = blk[None, :] * SEL_BLOCK <= q_pos[:, None]
    forced = (blk[None, :] == 0) | (blk[None, :] == q_pos[:, None] // SEL_BLOCK)
    score = jnp.where(valid, imp + jnp.where(forced, FORCE_BONUS, 0.0), NEG_INF)
    _, idx = lax.top_k(score, min(SEL_TOPN, n_sel))
    n = idx.shape[-1]
    bi = jnp.arange(B)[:, None, None, None]
    gi = jnp.arange(G)[None, :, None, None]
    kg = ks_blocks.transpose(0, 3, 1, 2, 4)[bi, gi, idx].reshape(B, G, Tq, n * SEL_BLOCK, hd)
    vg = vs_blocks.transpose(0, 3, 1, 2, 4)[bi, gi, idx].reshape(B, G, Tq, n * SEL_BLOCK, hd)
    kpos = (idx[..., None] * SEL_BLOCK + jnp.arange(SEL_BLOCK)).reshape(B, G, Tq, n * SEL_BLOCK)
    dist_s = q_pos[None, None, :, None] - kpos
    s = (jnp.einsum('bqgrd,bgqkd->bgrqk', q.astype(F32), kg.astype(F32)) * hd ** -0.5
         - slopes[None, :, :, None, None] * dist_s[:, :, None].astype(F32))
    p = masked_softmax(s, (dist_s >= 0)[:, :, None])
    o_slc = jnp.einsum('bgrqk,bgqkd->bqgrd', p, vg.astype(F32))
    return o_cmp, o_slc

def window_attend(q, k, v, q_pos, k_pos, slopes):
    dist = q_pos[..., :, None] - k_pos[..., None, :]
    mask = (dist >= 0) & (dist < WINDOW) & (k_pos[..., None, :] >= 0)
    o, _ = attend(q, k, v, alibi_bias(slopes, dist), mask[..., None, None, :, :])
    return o

def window_prompt(q, k, v, slopes):
    B, T = k.shape[:2]
    nqb = T // Q_BLOCK
    band = np.arange(nqb)[:, None] * Q_BLOCK + np.arange(WINDOW + Q_BLOCK)[None, :]
    pad = ((0, 0), (WINDOW, 0), (0, 0), (0, 0))
    kb = jnp.pad(k, pad)[:, band]
    vb = jnp.pad(v, pad)[:, band]
    qb = q.reshape(B, nqb, Q_BLOCK, NSA_KV_HEADS, NSA_GROUP, NSA_HEAD_DIM)
    o = window_attend(qb, kb, vb, np.arange(T).reshape(nqb, Q_BLOCK), band - WINDOW, slopes)
    return o.reshape(B, T, NSA_KV_HEADS, NSA_GROUP, NSA_HEAD_DIM)

def gla_chunked(q, k, v, log_a, s0, chunk):
    B, T, H, dk = q.shape
    dv = v.shape[-1]
    n = T // chunk

    def to_chunks(a):
        return a.astype(F32).reshape(B, n, chunk, H, a.shape[-1]).transpose(1, 0, 2, 3, 4)

    qc, kc, vc, gc = to_chunks(q), to_chunks(k), to_chunks(v), to_chunks(log_a)
    b = jnp.cumsum(gc, axis=2)
    b_last = b[:, :, -1:]
    q_dec = qc * jnp.exp(b)
    k_inv = kc * jnp.exp(-b)
    k_tail = kc * jnp.exp(b_last - b)
    causal = np.tril(np.ones((chunk, chunk), dtype=bool))
    a_intra = jnp.where(causal, jnp.einsum('nbihd,nbjhd->nbhij', q_dec, k_inv), 0.0)
    o_intra = jnp.einsum('nbhij,nbjhv->nbihv', a_intra, vc)

    def step(S, xs):
        qd, kt, vv, bl = xs
        o_inter = jnp.einsum('bihd,bhdv->bihv', qd, S)
        S = jnp.exp(bl[:, 0])[..., None] * S + jnp.einsum('bjhd,bjhv->bhdv', kt, vv)
        return S, o_inter

    s_final, o_inter = lax.scan(step, s0.astype(F32), (q_dec, k_tail, vc, b_last))
    o = (o_intra + o_inter).transpose(1, 0, 2, 3, 4).reshape(B, T, H, dv)
    return o, s_final

def mixer_inputs(h, w_in, a_up, a_b):
    B, T, _ = h.shape
    (q, kv, gate, z_a, q_g, k_g, v_g, a_low, z_b, merge) = jnp.split(h @ w_in, _split_offsets(), axis=-1)
    q = q.reshape(B, T, NSA_KV_HEADS, NSA_GROUP, NSA_HEAD_DIM)
    kv = kv.reshape(B, T, 6, NSA_KV_HEADS, NSA_HEAD_DIM)
    gate = jax.nn.sigmoid(gate.astype(F32)).reshape(B, T, 3, NSA_KV_HEADS, NSA_GROUP)
    q_g = q_g.reshape(B, T, GLA_HEADS, GLA_DK) * GLA_DK ** -0.5
    k_g = k_g.reshape(B, T, GLA_HEADS, GLA_DK)
    v_g = v_g.reshape(B, T, GLA_HEADS, GLA_DV)
    log_a = (jax.nn.log_sigmoid((a_low @ a_up + a_b).astype(F32)) / GLA_GATE_TAU).reshape(B, T, GLA_HEADS, GLA_DK)
    return (q, kv[:, :, 0], kv[:, :, 1], kv[:, :, 2], kv[:, :, 3], kv[:, :, 4], kv[:, :, 5],
            gate, z_a, q_g, k_g, v_g, log_a, z_b, merge)

def mixer_outputs(x, o_cmp, o_slc, o_win, gate, z_a, o_gla, z_b, merge, gla_g, w_ba, w_bb, w_out):
    B, T, _ = x.shape
    o_nsa = gate[:, :, 0, :, :, None] * o_cmp + gate[:, :, 1, :, :, None] * o_slc + gate[:, :, 2, :, :, None] * o_win
    o_nsa = o_nsa.reshape(B, T, NSA_WIDTH).astype(x.dtype) * jax.nn.silu(z_a)
    o_g = o_gla * lax.rsqrt(jnp.mean(o_gla * o_gla, axis=-1, keepdims=True) + NORM_EPS)
    o_g = (o_g.astype(x.dtype) * gla_g).reshape(B, T, GLA_VAL_WIDTH) * jax.nn.silu(z_b)
    g_a, g_b = jnp.split(merge, 2, axis=-1)
    mix = jax.nn.sigmoid(g_a) * (o_nsa @ w_ba) + jax.nn.sigmoid(g_b) * (o_g @ w_bb)
    return x + mix @ w_out

def prompt_layer(x, lp, slopes):
    (g_norm, w_in, pk_pe, pk_w1, pk_w2, pv_pe, pv_w1, pv_w2, a_up, a_b, gla_g, w_ba, w_bb, w_out) = lp
    B, T, _ = x.shape
    h = rms_norm(x, g_norm)
    (q, k_cmp, v_cmp, k_slc, v_slc, k_win, v_win, gate, z_a, q_g, k_g, v_g, log_a, z_b, merge) = mixer_inputs(h, w_in, a_up, a_b)
    kc = compress_blocks(k_cmp, pk_pe, pk_w1, pk_w2)
    vc = compress_blocks(v_cmp, pv_pe, pv_w1, pv_w2)
    cmp_end = cmp_block_end(T)
    ks_blocks = to_sel_blocks(k_slc)
    vs_blocks = to_sel_blocks(v_slc)
    nqb = T // Q_BLOCK
    qb = q.reshape(B, nqb, Q_BLOCK, NSA_KV_HEADS, NSA_GROUP, NSA_HEAD_DIM).swapaxes(0, 1)
    posb = jnp.arange(T, dtype=jnp.int32).reshape(nqb, Q_BLOCK)

    def block_fn(args):
        qq, pp = args
        return nsa_cmp_slc(qq, pp, kc, vc, cmp_end, ks_blocks, vs_blocks, slopes)

    o_cmp, o_slc = lax.map(block_fn, (qb, posb))
    o_cmp = o_cmp.swapaxes(0, 1).reshape(B, T, NSA_KV_HEADS, NSA_GROUP, NSA_HEAD_DIM)
    o_slc = o_slc.swapaxes(0, 1).reshape(B, T, NSA_KV_HEADS, NSA_GROUP, NSA_HEAD_DIM)
    o_win = window_prompt(q, k_win, v_win, slopes)
    s0 = jnp.zeros((B, GLA_HEADS, GLA_DK, GLA_DV), F32)
    o_gla, s_gla = gla_chunked(q_g, k_g, v_g, log_a, s0, GLA_CHUNK)
    y = mixer_outputs(x, o_cmp, o_slc, o_win, gate, z_a, o_gla, z_b, merge, gla_g, w_ba, w_bb, w_out)
    keep = min(WINDOW, T)
    return y, (k_cmp, v_cmp, k_slc, v_slc, k_win[:, T - keep:], v_win[:, T - keep:], s_gla)

def gather_pages(pool, page_table):
    rows = pool[page_table]
    return rows.reshape(page_table.shape[0], page_table.shape[1] * pool.shape[1], pool.shape[2], pool.shape[3])

def sample_layer(x, lp, slopes, pk_cmp, pv_cmp, pk_slc, pv_slc, buf_k, buf_v, s_prev, page_table):
    (g_norm, w_in, pk_pe, pk_w1, pk_w2, pv_pe, pv_w1, pv_w2, a_up, a_b, gla_g, w_ba, w_bb, w_out) = lp
    DB, DS, _ = x.shape
    past = page_table.shape[1] * pk_cmp.shape[1]
    h = rms_norm(x, g_norm)
    (q, k_cmp, v_cmp, k_slc, v_slc, k_win, v_win, gate, z_a, q_g, k_g, v_g, log_a, z_b, merge) = mixer_inputs(h, w_in, a_up, a_b)
    q_pos = past + np.arange(DS)
    kc_all = jnp.concatenate([gather_pages(pk_cmp, page_table), k_cmp], axis=1)
    vc_all = jnp.concatenate([gather_pages(pv_cmp, page_table), v_cmp], axis=1)
    L = past + DS
    kc = compress_blocks(kc_all, pk_pe, pk_w1, pk_w2)
    vc = compress_blocks(vc_all, pv_pe, pv_w1, pv_w2)
    ks_blocks = to_sel_blocks(jnp.concatenate([gather_pages(pk_slc, page_table), k_slc], axis=1))
    vs_blocks = to_sel_blocks(jnp.concatenate([gather_pages(pv_slc, page_table), v_slc], axis=1))
    o_cmp, o_slc = nsa_cmp_slc(q, q_pos, kc, vc, cmp_block_end(L), ks_blocks, vs_blocks, slopes)
    w_buf = buf_k.shape[1]
    keys_w = jnp.concatenate([buf_k, k_win], axis=1)
    vals_w = jnp.concatenate([buf_v, v_win], axis=1)
    k_pos = past - w_buf + np.arange(w_buf + DS)
    o_win = window_attend(q, keys_w, vals_w, q_pos, k_pos, slopes)
    o_gla, s_gla = gla_chunked(q_g, k_g, v_g, log_a, s_prev, DS)
    y = mixer_outputs(x, o_cmp, o_slc, o_win, gate, z_a, o_gla, z_b, merge, gla_g, w_ba, w_bb, w_out)
    return y, (k_cmp, v_cmp, k_slc, v_slc, keys_w[:, DS:], vals_w[:, DS:], s_gla)

def setup_inputs(seed: int = 0) -> dict:
    key = jax.random.key(seed)
    ks = jax.random.split(key, 32)
    n_pages = PAST_LEN // PAGE_SIZE
    n_used = DEC_BATCH * n_pages
    n_pool = n_used + n_used // 4
    w_buf = min(WINDOW, PAST_LEN)
    G, hd = NSA_KV_HEADS, NSA_HEAD_DIM

    def nrm(k, shape, scale):
        return scale * jax.random.normal(k, shape, F32)

    pool_shape = (DEPTH, n_pool, PAGE_SIZE, G, hd)
    page_table = jax.random.permutation(ks[0], n_pool)[:n_used].reshape(DEC_BATCH, n_pages).astype(jnp.int32)
    return {
        'x_prompt': nrm(ks[1], (BATCH, SEQ, D_MODEL), 1.0),
        'x_sample': nrm(ks[2], (DEC_BATCH, DEC_SEQ, D_MODEL), 1.0),
        'cache_k_cmp': nrm(ks[3], pool_shape, 1.0),
        'cache_v_cmp': nrm(ks[4], pool_shape, 1.0),
        'cache_k_slc': nrm(ks[5], pool_shape, 1.0),
        'cache_v_slc': nrm(ks[6], pool_shape, 1.0),
        'cache_k_win': nrm(ks[7], (DEPTH, DEC_BATCH, w_buf, G, hd), 1.0),
        'cache_v_win': nrm(ks[8], (DEPTH, DEC_BATCH, w_buf, G, hd), 1.0),
        'state_gla': nrm(ks[9], (DEPTH, DEC_BATCH, GLA_HEADS, GLA_DK, GLA_DV), 1.0),
        'page_table': page_table,
        'norm_g': 1.0 + nrm(ks[10], (DEPTH, D_MODEL), 0.1),
        'w_in': nrm(ks[11], (DEPTH, D_MODEL, D_IN), D_MODEL ** -0.5),
        'phi_k_pe': nrm(ks[12], (DEPTH, CMP_BLOCK, hd), 0.1),
        'phi_k_w1': nrm(ks[13], (DEPTH, CMP_BLOCK * hd, CMP_HIDDEN), (CMP_BLOCK * hd) ** -0.5),
        'phi_k_w2': nrm(ks[14], (DEPTH, CMP_HIDDEN, hd), CMP_HIDDEN ** -0.5),
        'phi_v_pe': nrm(ks[15], (DEPTH, CMP_BLOCK, hd), 0.1),
        'phi_v_w1': nrm(ks[16], (DEPTH, CMP_BLOCK * hd, CMP_HIDDEN), (CMP_BLOCK * hd) ** -0.5),
        'phi_v_w2': nrm(ks[17], (DEPTH, CMP_HIDDEN, hd), CMP_HIDDEN ** -0.5),
        'gla_alpha_up': nrm(ks[18], (DEPTH, GLA_GATE_RANK, GLA_KEY_WIDTH), GLA_GATE_RANK ** -0.5),
        'gla_alpha_b': nrm(ks[19], (DEPTH, GLA_KEY_WIDTH), 0.1),
        'gla_norm_g': 1.0 + nrm(ks[20], (DEPTH, GLA_DV), 0.1),
        'w_branch_a': nrm(ks[21], (DEPTH, NSA_WIDTH, D_MODEL), NSA_WIDTH ** -0.5),
        'w_branch_b': nrm(ks[22], (DEPTH, GLA_VAL_WIDTH, D_MODEL), GLA_VAL_WIDTH ** -0.5),
        'w_out': nrm(ks[23], (DEPTH, D_MODEL, D_MODEL), D_MODEL ** -0.5),
        'final_norm_g': 1.0 + nrm(ks[24], (D_MODEL,), 0.1),
    }

def reference(x_prompt, x_sample, cache_k_cmp, cache_v_cmp, cache_k_slc, cache_v_slc, cache_k_win, cache_v_win,
              state_gla, page_table, norm_g, w_in, phi_k_pe, phi_k_w1, phi_k_w2, phi_v_pe, phi_v_w1, phi_v_w2,
              gla_alpha_up, gla_alpha_b, gla_norm_g, w_branch_a, w_branch_b, w_out, final_norm_g):
    slopes = alibi_slopes()
    y_p, y_s = x_prompt, x_sample
    prompt_new, sample_new = [], []
    for l in range(DEPTH):
        lp = (norm_g[l], w_in[l], phi_k_pe[l], phi_k_w1[l], phi_k_w2[l], phi_v_pe[l], phi_v_w1[l], phi_v_w2[l],
              gla_alpha_up[l], gla_alpha_b[l], gla_norm_g[l], w_branch_a[l], w_branch_b[l], w_out[l])
        y_p, st_p = prompt_layer(y_p, lp, slopes)
        y_s, st_s = sample_layer(y_s, lp, slopes, cache_k_cmp[l], cache_v_cmp[l], cache_k_slc[l], cache_v_slc[l],
                                 cache_k_win[l], cache_v_win[l], state_gla[l], page_table)
        prompt_new.append(st_p)
        sample_new.append(st_s)
    y_prompt = rms_norm(y_p, final_norm_g)
    y_sample = rms_norm(y_s, final_norm_g)
    (p_k_cmp, p_v_cmp, p_k_slc, p_v_slc, p_k_win, p_v_win, p_gla) = [jnp.stack(t) for t in zip(*prompt_new)]
    (s_k_cmp, s_v_cmp, s_k_slc, s_v_slc, s_k_win, s_v_win, s_gla) = [jnp.stack(t) for t in zip(*sample_new)]
    return (y_prompt, y_sample, p_k_cmp, p_v_cmp, p_k_slc, p_v_slc, p_k_win, p_v_win, p_gla,
            s_k_cmp, s_v_cmp, s_k_slc, s_v_slc, s_k_win, s_v_win, s_gla)


_drawn_inputs = setup_inputs


def setup_inputs(seed=0):
    import zlib

    import numpy as np

    out = dict(_drawn_inputs(seed))
    spreads = {}
    factors = {'cache_k_cmp': 4.797,
     'phi_k_pe': 8.0,
     'phi_k_w1': 4.198,
     'phi_k_w2': 4.131,
     'phi_v_pe': 6.509}
    for name, (base, spread) in spreads.items():
        noise = np.random.default_rng([zlib.crc32(name.encode()), seed]).standard_normal(out[name].shape)
        drawn = base * np.exp(spread * noise) if base else spread * noise
        out[name] = jnp.asarray(drawn.astype(out[name].dtype))
    for name, factor in factors.items():
        out[name] = (out[name] * factor).astype(out[name].dtype)
    return out
```

```python
from contextlib import ExitStack

import concourse.bass as bass
from concourse import mybir

F32 = mybir.dt.float32
I32 = mybir.dt.int32
ALU = mybir.AluOpType
ACT = mybir.ActivationFunctionType
AX = mybir.AxisListType.X

P = 128
D = 1024
KT = D // P
SEQ = 1024
PT = SEQ // P
DB, DS = 8, 4
ST = DB * DS
TILES = PT + 1
TOK = SEQ + ST
NF = TOK // 3
PAST, PAGE, NPAGES, NPOOL = 512, 128, 4, 40
H, G, R, HD = 8, 2, 4, 64
CB, CS, SB_POS = 32, 16, 32
NCP = (SEQ - CB) // CS + 1
NCS = (PAST + DS - CB) // CS + 1
WIN = 512
GH, DK, DV = 4, 128, 256
RANK, TAU = 16, 16.0
CH = 32
EPS, BIG, TINY = 1e-6, 1e30, 1e-30
NSLOT = 4
C_Q, C_KV, C_GATE, C_ZA = 0, 512, 1280, 1304
C_QG, C_KG, C_VG, C_AL, C_ZB, C_MRG = 1816, 2328, 2840, 3864, 3880, 4904


def rows_of(t):
    return P if t < PT else ST


def hybrid_step(nc, a, outs):
    (y_p, y_s, p_kc, p_vc, p_ks, p_vs, p_kw, p_vw, p_gla,
     s_kc, s_vc, s_ks, s_vs, s_kw, s_vw, s_gla) = outs
    w_in = a["w_in"][0]
    ctx = ExitStack()
    sem_names = {}

    def sem(name):
        if name not in sem_names:
            sem_names[name] = ctx.enter_context(nc.semaphore(name))
        return sem_names[name]

    def sb(stack, name, shape, dt=F32):
        return stack.enter_context(nc.sbuf_tensor(name, shape, dt))

    with ctx:
        hT = sb(ctx, "hT", [P, KT, TOK])
        wr = sb(ctx, "wr", [P, NSLOT, 2048])
        gaT = sb(ctx, "gaT", [48, TOK])
        gate = sb(ctx, "gate", [P, TILES, 24])
        ident = sb(ctx, "ident", [P, P])
        tri = sb(ctx, "tri", [P, P])
        small = sb(ctx, "small", [P, 256])
        idx = sb(ctx, "idx", [P, DB], I32)
        ps = ctx.enter_context(nc.psum_tensor("ps", [P, 8, 512], F32))

        o_spill = nc.dram_tensor("o_spill", [P, TILES, 512], F32, kind="Internal").ap()
        gate_spill = nc.dram_tensor("gate_spill", [DB, H, DS, 3], F32, kind="Internal").ap()
        orow_spill = nc.dram_tensor("orow_spill", [DB, H, DS, HD], F32, kind="Internal").ap()

        ng_col = small[:, 0:8]
        ab_col = small[:, 8:12]
        gn_col = small[:, 12:14]
        ssq = small[:, 16:25]
        rstd = small[:, 32:41]
        peK = small[0:HD, 64:96]
        peV = small[0:HD, 96:128]
        pt_all = small[:, 128:160].bitcast(I32)
        pbase = small[:, 160:161].bitcast(I32)

        link_count = {}

        def linker(eng, name):
            s = sem(name)

            def link(ins):
                link_count[name] = link_count.get(name, 0) + 1
                ins.then_inc(s, 1)
                eng.wait_ge(s, link_count[name])
            return link

        chunks, number = [], {}

        def chunk(name, *parts):
            number[name] = len(chunks)
            chunks.append(parts)

        def cols(src, c0, n, ks=KT, at=0, width=256):
            v = src.rearrange("(k p) c -> p k c", p=P)
            h = ks // 2
            return [(k0, h, at, n, width, v[:, k0:k0 + h, c0:c0 + n]) for k0 in (0, h)]

        def pair(src, c0, c1, n=P):
            v = src.rearrange("(k p) c -> p k c", p=P)
            return [(0, KT, at, n, 256, v[:, :, c:c + n]) for at, c in ((0, c0), (P, c1))]

        for j in range(2):
            v = w_in.rearrange("(k p) c -> p k c", p=P)
            chunk(f"q{j}", *[(0, KT, P * r + HD * g, HD, 256,
                              v[:, :, C_Q + 256 * g + P * j + HD * r:C_Q + 256 * g + P * j + HD * r + HD])
                             for r in range(2) for g in range(G)])
        chunk("cmp", *cols(w_in, C_KV, 256))
        chunk("slc", *cols(w_in, C_KV + 256, 256))
        chunk("win", *cols(w_in, C_KV + 512, 256))
        vin = w_in.rearrange("(k p) c -> p k c", p=P)
        chunk("ga", (0, KT, 0, 32, 48, vin[:, :, C_GATE:C_GATE + 32]),
              (0, KT, 32, RANK, 48, vin[:, :, C_AL:C_AL + RANK]))
        for kv in "kv":
            w1 = a[f"phi_{kv}_w1"][0].rearrange("(s d) c -> d s c", d=HD)
            for half in range(2):
                chunk(f"w1{kv}{half}", *[("w1", g, w1[:, 16 * half:16 * half + 16, :]) for g in range(G)])
        for h in range(GH):
            chunk(f"gqk{h}", *pair(w_in, C_QG + P * h, C_KG + P * h))
            chunk(f"gv{h}", *cols(w_in, C_VG + DV * h, DV))
        for j in range(2):
            chunk(f"za{j}", *cols(w_in, C_ZA + 256 * j, 256))
        for j in range(4):
            chunk(f"zb{j}", *cols(w_in, C_ZB + 256 * j, 256))
        for j in range(4):
            chunk(f"ma{j}", *cols(w_in, C_MRG + 256 * j, 256))
            chunk(f"wa{j}", *cols(a["w_branch_a"][0], 256 * j, 256, ks=4))
            chunk(f"mb{j}", *cols(w_in, C_MRG + D + 256 * j, 256))
            chunk(f"wb{j}", *cols(a["w_branch_b"][0], 256 * j, 256))
        for j in range(4):
            chunk(f"wo{j}", *cols(a["w_out"][0], 256 * j, 256))

        released = {}

        def slot(name, width=256):
            return wr[:, number[name] % NSLOT, 0:KT * width].rearrange("p (k c) -> p k c", c=width)

        def have(eng, name):
            n = number[name]
            eng.wait_ge(sem(f"w_loaded{n % NSLOT}"), 16 * sum(len(c) for c in chunks[n % NSLOT:n + 1:NSLOT]))

        def load_chunks(eng, first, last):
            for n in range(number[first], number[last] + 1):
                if n >= NSLOT:
                    eng.wait_ge(*released[n - NSLOT])
                s = n % NSLOT
                for part in chunks[n]:
                    if part[0] == "w1":
                        dst = wr[HD * part[1]:HD * part[1] + HD, s, :].rearrange("p (s c) -> p s c", c=P)
                    else:
                        k0, nk, at, w, width, _ = part
                        dst = wr[:, s, 0:KT * width].rearrange("p (k c) -> p k c", c=width)[
                            :, k0:k0 + nk, at:at + w]
                    eng.dma_start(dst, part[-1]).then_inc(sem(f"w_loaded{s}"), 16)

        out_count = [0]

        def store(eng, dst, src):
            out_count[0] += 1
            return eng.dma_start(dst, src).then_inc(sem("stored"), 16)

        def feature_major(set_, lhs, ntile, m=P):
            for n in range(3):
                for k in range(ntile):
                    mm = nc.tensor.matmul(ps[0:m, 3 * set_ + n, 0:NF], lhs(k)[0], lhs(k)[1](n),
                                          start=(k == 0), stop=(k == ntile - 1))
            return mm

        def h_cols(k):
            return lambda n: hT[:, k, NF * n:NF * n + NF]

        def banks(set_, m=P):
            return ps[0:m, 3 * set_:3 * set_ + 3, 0:NF]

        def split3(ap):
            return ap.rearrange("p (n c) -> p n c", n=3)

        nsa = ExitStack()
        qT = sb(nsa, "qT", [P, R, TOK])
        kT = sb(nsa, "kT", [P, 4, TOK])
        vtok = sb(nsa, "vtok", [P, TILES, 256])
        o_acc = sb(nsa, "o_acc", [P, TILES, 512])
        slope = sb(nsa, "slope", [P, H])
        kc = sb(nsa, "kc", [P, 64])
        vc = sb(nsa, "vc", [64, P])
        kcs = sb(nsa, "kcs", [P, DB, NCS])
        vcs = sb(nsa, "vcs", [NCS, DB, P])

        s1 = ExitStack()
        x_all = sb(s1, "x_all", [P, TILES, D])
        xn = sb(s1, "xn", [P, 2, D])
        ktok = sb(s1, "ktok", [P, TILES, 512])
        NFT = 9
        with nc.Block() as block:
            @block.tensor
            def _(pe):
                pe.wait_ge(sem("consts"), 4)
                for t in range(TILES):
                    n = rows_of(t)
                    pe.wait_ge(sem("xn_ready"), t + 1)
                    for half in range(2):
                        if t >= 1:
                            pe.wait_ge(sem("hT_ready"), 2 * t + half - 1)
                        for k in range(4):
                            mm = nc.tensor.transpose(ps[:, 6 + half, P * k:P * k + n],
                                                     xn[0:n, t % 2, P * (4 * half + k):P * (4 * half + k) + P],
                                                     ident[0:n, 0:n])
                        mm.then_inc(sem("xT_done"), 1)
                pe.wait_ge(sem("hT_ready"), 2 * TILES)

                def keys_of(name, c0, width=256, m=P):
                    w = slot(name, width)
                    return lambda k: (w[:, k, c0:c0 + m], h_cols(k))

                def q_of(r):
                    w = slot(f"q{r // 2}")
                    c0 = P * (r % 2)
                    return lambda k: (w[:, k, c0:c0 + P], h_cols(k))

                plan = [(f"q{r // 2}", q_of(r), P) for r in range(R)]
                plan += [("cmp", keys_of("cmp", 0), P), ("cmp", keys_of("cmp", P), P),
                         ("slc", keys_of("slc", 0), P), ("win", keys_of("win", 0), P)]
                for f, (name, lhs, m) in enumerate(plan):
                    have(pe, name)
                    if f >= 2:
                        pe.wait_ge(sem("f_copied"), f - 1)
                    feature_major(f % 2, lhs, KT, m).then_inc(sem("f_done"), 1)
                    released[number[name]] = (sem("f_done"), f + 1)
                for t in range(TILES):
                    n = rows_of(t)
                    if t >= 2:
                        pe.wait_ge(sem("v_copied"), t - 1)
                    for j, name in enumerate(("slc", "win")):
                        for k in range(KT):
                            mm = nc.tensor.matmul(ps[0:n, 6 + t % 2, P * j:P * j + P],
                                                  hT[:, k, P * t:P * t + n], slot(name)[:, k, P:2 * P],
                                                  start=(k == 0), stop=(k == KT - 1))
                    mm.then_inc(sem("v_done"), 1)
                for name in ("slc", "win"):
                    released[number[name]] = (sem("v_done"), TILES)
                have(pe, "ga")
                pe.wait_ge(sem("f_copied"), NFT - 2)
                feature_major(0, keys_of("ga", 0, 48, 48), KT, 48).then_inc(sem("f_done"), 1)
                released[number["ga"]] = (sem("f_done"), NFT)
                pe.wait_ge(sem("f_copied"), NFT - 1)
                pe.wait_ge(sem("v_copied"), TILES)
                for t in range(TILES):
                    n = rows_of(t)
                    if t >= 2:
                        pe.wait_ge(sem("ktok_copied"), t - 1)
                    for j in range(4):
                        mm = nc.tensor.transpose(ps[0:n, 6 + t % 2, P * j:P * j + P],
                                                 kT[:, j, P * t:P * t + n], ident[:, :])
                    mm.then_inc(sem("ktok_done"), 1)
                pe.wait_ge(sem("f_copied"), NFT)
                for t in range(TILES):
                    n = rows_of(t)
                    mm = nc.tensor.transpose(ps[0:n, 3, 24 * t:24 * t + 24],
                                             gaT[0:24, P * t:P * t + n], ident[0:24, 0:24])
                mm.then_inc(sem("gate_done"), 1)

            @block.gpsimd
            def _(pool):
                pool.dma_start(ng_col, a["norm_g"].rearrange("o (k p) -> p (o k)", p=P),
                               allow_slow_non_contiguous=True).then_inc(sem("vectors"), 16)
                pool.dma_start(ab_col, a["gla_alpha_b"].rearrange("o (k p) -> p (o k)", p=P),
                               allow_slow_non_contiguous=True).then_inc(sem("vectors"), 16)
                pool.dma_start(gn_col, a["gla_norm_g"].rearrange("o (k p) -> p (o k)", p=P),
                               allow_slow_non_contiguous=True).then_inc(sem("vectors"), 16)
                pool.dma_start(peK, a["phi_k_pe"][0].rearrange("s d -> d s"),
                               allow_slow_non_contiguous=True).then_inc(sem("vectors"), 16)
                pool.dma_start(peV, a["phi_v_pe"][0].rearrange("s d -> d s"),
                               allow_slow_non_contiguous=True).then_inc(sem("vectors"), 16)
                pool.dma_start(pt_all, a["page_table"].rearrange("b g -> (b g)").unsqueeze(0)
                               .to_broadcast([P, DB * NPAGES])).then_inc(sem("table"), 16)
                for m in (ident, tri):
                    pool.memset(m[:, :], 0.0 if m is ident else 1.0).then_inc(sem("consts0"), 1)
                pool.wait_ge(sem("consts0"), 2)
                pool.affine_select(out=ident[:, :], in_=ident[:, :], compare_op=ALU.not_equal, fill=1.0,
                                   base=0, pattern=[[-1, P]], channel_multiplier=1).then_inc(sem("consts"), 1)
                pool.affine_select(out=tri[:, :], in_=tri[:, :], compare_op=ALU.is_ge, fill=0.0,
                                   base=0, pattern=[[1, P]], channel_multiplier=-1).then_inc(sem("consts"), 1)
                for h in range(H):
                    pool.memset(slope[:, h:h + 1], 2.0 ** -(h + 1)).then_inc(sem("slopes"), 1)
                pool.wait_ge(sem("slopes"), H)
                for q in range(4):
                    pool.iota(pbase[32 * q:32 * q + 32, :], pattern=[[0, 1]], base=0,
                              channel_multiplier=1).then_inc(sem("pbase"), 1)
                    pool.wait_ge(sem("pbase"), q + 1)
                pool.memset(ssq, 1.0).then_inc(sem("consts"), 1)
                pool.memset(kc[:, :], 0.0).then_inc(sem("consts"), 1)

            @block.vector
            def _(dve):
                link = linker(dve, "dve_link")
                dve.wait_ge(sem("squares"), TILES)
                link(nc.vector.tensor_scalar(rstd, ssq, 1.0 / D, EPS, ALU.mult, ALU.add))
                dve.sem_inc(sem("var_ready"), 1)
                dve.wait_ge(sem("sd_ready"), 1)
                nc.vector.reciprocal(rstd, ssq).then_inc(sem("rstd_ready"), 1)
                dve.wait_ge(sem("vectors"), 80)
                for t in range(TILES):
                    n = rows_of(t)
                    for half in range(2):
                        dve.wait_ge(sem("xT_done"), 2 * t + half + 1)
                        nc.vector.tensor_tensor(
                            hT[:, 4 * half:4 * half + 4, P * t:P * t + n],
                            ps[:, 6 + half, :].rearrange("p (k c) -> p k c", k=4)[:, :, 0:n],
                            ng_col[:, 4 * half:4 * half + 4].unsqueeze(2).to_broadcast([P, 4, n]),
                            ALU.mult).then_inc(sem("hT_ready"), 1)
                dve.wait_ge(sem("table"), 16)
                dve.wait_ge(sem("pbase"), 4)
                for q in range(NPAGES):
                    rr = slice(32 * q, 32 * q + 32)
                    link(nc.vector.tensor_scalar(
                        idx[rr, :], pt_all[rr, :].rearrange("p (b g) -> p b g", g=NPAGES)[:, :, q],
                        32, None, ALU.mult))
                    ins = nc.vector.tensor_tensor(idx[rr, :], idx[rr, :], pbase[rr, :].to_broadcast([32, DB]),
                                                  ALU.add)
                    link(ins)
                dve.sem_inc(sem("idx_ready"), 1)
                for t in range(TILES):
                    n = rows_of(t)
                    dve.wait_ge(sem("ktok_done"), t + 1)
                    nc.vector.tensor_copy(ktok[0:n, t, :], ps[0:n, 6 + t % 2, :]).then_inc(sem("ktok_copied"), 1)

            @block.scalar
            def _(act):
                act.wait_ge(sem("consts"), 3)
                for t in range(TILES):
                    n = rows_of(t)
                    act.wait_ge(sem(f"x_loaded{t}"), 16)
                    if t >= 2:
                        act.wait_ge(sem("squares"), t - 1)
                    nc.scalar.activation(xn[0:n, t % 2, :], x_all[0:n, t, :], ACT.Square,
                                         accum_out=ssq[0:n, t:t + 1]).then_inc(sem("squares"), 1)
                act.wait_ge(sem("var_ready"), 1)
                act.wait_ge(sem("squares"), TILES)
                nc.scalar.activation(ssq, rstd, ACT.Sqrt).then_inc(sem("sd_ready"), 1)
                act.wait_ge(sem("rstd_ready"), 1)
                for t in range(TILES):
                    n = rows_of(t)
                    if t >= 2:
                        act.wait_ge(sem("xT_done"), 2 * (t - 1))
                    nc.scalar.activation(xn[0:n, t % 2, :], x_all[0:n, t, :], ACT.Copy,
                                         scale=rstd[0:n, t:t + 1]).then_inc(sem("xn_ready"), 1)
                for f in range(NFT - 1):
                    act.wait_ge(sem("f_done"), f + 1)
                    dst = qT[:, f, :] if f < R else kT[:, f - R, :]
                    nc.scalar.activation(split3(dst), banks(f % 2), ACT.Copy,
                                         scale=-HD ** -0.5 if f < R else 1.0).then_inc(sem("f_copied"), 1)
                for t in range(TILES):
                    n = rows_of(t)
                    act.wait_ge(sem("v_done"), t + 1)
                    nc.scalar.activation(vtok[0:n, t, :], ps[0:n, 6 + t % 2, 0:256], ACT.Copy)\
                        .then_inc(sem("v_copied"), 1)
                act.wait_ge(sem("f_done"), NFT)
                nc.scalar.activation(split3(gaT[:, :]), banks(0, 48), ACT.Copy).then_inc(sem("f_copied"), 1)
                act.wait_ge(sem("gate_done"), 1)
                nc.scalar.activation(gate[:, 0:PT, :], ps[:, 3, 0:24 * PT].rearrange("p (t c) -> p t c", c=24),
                                     ACT.Sigmoid).then_inc(sem("gate_ready"), 1)
                nc.scalar.activation(gate[0:ST, PT, :], ps[0:ST, 3, 24 * PT:24 * PT + 24],
                                     ACT.Sigmoid).then_inc(sem("gate_ready"), 1)

            @block.sync
            def _(sp):
                for t in range(TILES):
                    src = a["x_prompt"][0, P * t:P * t + P, :] if t < PT else \
                        a["x_sample"].rearrange("b s d -> (b s) d")
                    sp.dma_start(x_all[0:rows_of(t), t, :], src).then_inc(sem(f"x_loaded{t}"), 16)
                load_chunks(sp, "q0", "w1v1")
                for src, dst in ((a["cache_k_win"], s_kw), (a["cache_v_win"], s_vw)):
                    store(sp, dst[0, :, 0:WIN - DS].rearrange("b s g d -> b (s g d)"),
                          src[0, :, DS:WIN].rearrange("b s g d -> b (s g d)"))
                sp.wait_ge(sem("v_copied"), TILES)
                for j, (pd, sd) in enumerate(((p_vs, s_vs), (p_vw, s_vw))):
                    t0 = 0 if j == 0 else PT - WIN // P
                    store(sp, pd[0, 0].rearrange("(t p) g d -> p t (g d)", p=P), vtok[:, t0:PT, P * j:P * j + P])
                    if j == 0:
                        store(sp, sd[0].rearrange("b s g d -> (b s) (g d)"), vtok[0:ST, PT, 0:P])
                    else:
                        for b in range(DB):
                            store(sp, sd[0, b, WIN - DS:WIN].rearrange("s g d -> s (g d)"),
                                  vtok[DS * b:DS * b + DS, PT, P:2 * P])
                sp.wait_ge(sem("ktok_copied"), TILES)
                for j, (pd, sd) in enumerate(((p_kc, s_kc), (p_vc, s_vc), (p_ks, s_ks), (p_kw, s_kw))):
                    t0 = 0 if j < 3 else PT - WIN // P
                    store(sp, pd[0, 0].rearrange("(t p) g d -> p t (g d)", p=P), ktok[:, t0:PT, P * j:P * j + P])
                    if j < 3:
                        store(sp, sd[0].rearrange("b s g d -> (b s) (g d)"), ktok[0:ST, PT, P * j:P * j + P])
                    else:
                        for b in range(DB):
                            store(sp, sd[0, b, WIN - DS:WIN].rearrange("s g d -> s (g d)"),
                                  ktok[DS * b:DS * b + DS, PT, P * j:P * j + P])
                sp.wait_ge(sem("gate_ready"), 2)
                for b in range(DB):
                    sp.dma_start(gate_spill[b].rearrange("x t c -> t c x"),
                                 gate[DS * b:DS * b + DS, PT, :].rearrange("t (c x) -> t c x", c=3),
                                 allow_slow_non_contiguous=True).then_inc(sem("gate_spilled"), 16)
                sp.wait_ge(sem("stored"), 16 * out_count[0])
        s1.close()

        s2 = ExitStack()
        pages = sb(s2, "pages", [P, 4, 512])
        cT = sb(s2, "cT", [P, DB, 512])
        w2 = sb(s2, "w2", [P, 2, HD])
        hid = sb(s2, "hid", [P, 2, 2 * (64 + DB * NCS)])
        cbias = sb(s2, "cbias", [P, 2])
        NP2, NS2 = 64, DB * NCS
        with nc.Block() as block:
            @block.tensor
            def _(pe):
                for kv in range(2):
                    for b in range(DB):
                        n = DB * kv + b
                        pe.wait_ge(sem(f"page_loaded{n % 4}"), 16 * (n // 4 + 1))
                        if n >= 2:
                            pe.wait_ge(sem("cT_copied"), n - 1)
                        for j in range(4):
                            mm = nc.tensor.transpose(ps[:, 6 + n % 2, P * j:P * j + P],
                                                     pages[:, n % 4, P * j:P * j + P], ident[:, :])
                        mm.then_inc(sem("pT_done"), 1)
                    name = "kv"[kv]
                    pe.wait_ge(sem("cT_copied"), DB * (kv + 1))
                    if kv == 1:
                        pe.wait_ge(sem("hid_read"), 8)
                    for pos in range(SB_POS):
                        if pos % 16 == 0:
                            have(pe, f"w1{name}{pos // 16}")
                        flags = dict(start=(pos == 0), stop=(pos == SB_POS - 1))
                        for g in range(G):
                            w = wr[HD * g:HD * g + HD, number[f"w1{name}{pos // 16}"] % NSLOT,
                                   P * (pos % 16):P * (pos % 16) + P]
                            c0 = P * (pos % 4) + pos // 4
                            if g == 0:
                                nc.tensor.matmul(ps[:, 4, 0:1], w, (peK, peV)[kv][:, pos:pos + 1], **flags)
                            nc.tensor.matmul(ps[:, g, 0:NCP], w,
                                             kT[HD * g:HD * g + HD, kv, pos:pos + CS * (NCP - 1) + 1:CS], **flags)
                            mm = nc.tensor.matmul(ps[:, 2 + g, 0:NS2].rearrange("p (b c) -> p b c", b=DB), w,
                                                  cT[HD * g:HD * g + HD, :, c0:c0 + 4 * (NCS - 1) + 1:4], **flags)
                        if pos == 15:
                            mm.then_inc(sem("half_done"), 1)
                            released[number[f"w1{name}0"]] = (sem("half_done"), kv + 1)
                    mm.then_inc(sem("hid_done"), 1)
                    released[number[f"w1{name}1"]] = (sem("hid_done"), kv + 1)
                    pe.wait_ge(sem("w2_loaded"), 32)
                    pe.wait_ge(sem("hid_ready"), 4 * (kv + 1))
                    if kv == 0:
                        for g in range(G):
                            nc.tensor.matmul(ps[HD * g:HD * g + HD, 5, 0:NCP], w2[:, 0, :],
                                             hid[:, 0, 64 * g:64 * g + NCP], start=True, stop=True)
                        for g in range(G):
                            mm = nc.tensor.matmul(ps[HD * g:HD * g + HD, 5, 64:64 + NS2], w2[:, 0, :],
                                                  hid[:, 0, 128 + NS2 * g:128 + NS2 * g + NS2],
                                                  start=True, stop=True)
                        mm.then_inc(sem("c2_done"), 1)
                    else:
                        pe.wait_ge(sem("c2_copied"), 2)
                        for g in range(G):
                            nc.tensor.matmul(ps[0:NCP, 5, HD * g:HD * g + HD],
                                             hid[:, 0, 64 * g:64 * g + NCP], w2[:, 1, :], start=True, stop=True)
                        for b in range(DB):
                            for g in range(G):
                                c0 = 128 + NS2 * g + NCS * b
                                mm = nc.tensor.matmul(ps[0:NCS, 6 + b // 4, P * (b % 4) + HD * g:P * (b % 4) + HD * g + HD],
                                                      hid[:, 0, c0:c0 + NCS], w2[:, 1, :], start=True, stop=True)
                        mm.then_inc(sem("c2_done"), 1)

            @block.gpsimd
            def _(pool):
                pool.wait_ge(sem("idx_ready"), 1)
                for kv in range(2):
                    src = (a["cache_k_cmp"], a["cache_v_cmp"])[kv].rearrange("o n (s j) g d -> (o n s) (j g d)", j=4)
                    for b in range(DB):
                        n = DB * kv + b
                        if n >= 4:
                            pool.wait_ge(sem("pT_done"), n - 3)
                        pool.indirect_dma_start(pages[:, n % 4, :], None, src,
                                                bass.IndirectOffsetOnAxis(ap=idx[:, b:b + 1], axis=0))\
                            .then_inc(sem(f"page_loaded{n % 4}"), 16)

            @block.vector
            def _(dve):
                link = linker(dve, "dve_link")
                for kv in range(2):
                    for b in range(DB):
                        n = DB * kv + b
                        dve.wait_ge(sem("pT_done"), n + 1)
                        if b == 0 and kv == 1:
                            dve.wait_ge(sem("hid_done"), 1)
                        nc.vector.tensor_copy(cT[:, b, :], ps[:, 6 + n % 2, :]).then_inc(sem("cT_copied"), 1)
                    dve.wait_ge(sem("hid_done"), kv + 1)
                    link(nc.vector.tensor_copy(cbias[:, kv:kv + 1], ps[:, 4, 0:1]))
                    dve.sem_inc(sem("cbias_ready"), 1)
                    dve.wait_ge(sem("hid_read"), 8 * (kv + 1))
                    for g in range(G):
                        nc.vector.tensor_tensor(hid[:, 0, 64 * g:64 * g + NCP], hid[:, 0, 64 * g:64 * g + NCP],
                                                hid[:, 1, 64 * g:64 * g + NCP], ALU.mult).then_inc(sem("hid_ready"), 1)
                        c = slice(128 + NS2 * g, 128 + NS2 * g + NS2)
                        nc.vector.tensor_tensor(hid[:, 0, c], hid[:, 0, c], hid[:, 1, c], ALU.mult)\
                            .then_inc(sem("hid_ready"), 1)
                    dve.wait_ge(sem("c2_done"), kv + 1)
                    if kv == 0:
                        nc.vector.tensor_copy(kc[:, 0:NCP], ps[:, 5, 0:NCP]).then_inc(sem("c2_copied"), 1)
                        nc.vector.tensor_copy(kcs[:, :, :].rearrange("p b c -> p (b c)"), ps[:, 5, 64:64 + NS2])\
                            .then_inc(sem("c2_copied"), 1)
                    else:
                        link(nc.vector.memset(vc[:, :], 0.0))
                        nc.vector.tensor_copy(vc[0:NCP, :], ps[0:NCP, 5, 0:P]).then_inc(sem("c2_copied"), 1)
                        nc.vector.tensor_copy(vcs[:, :, :].rearrange("p (x b) c -> p x (b c)", x=2),
                                              ps[0:NCS, 6:8, :]).then_inc(sem("c2_copied"), 1)

            @block.scalar
            def _(act):
                for kv in range(2):
                    act.wait_ge(sem("cbias_ready"), kv + 1)
                    if kv == 1:
                        act.wait_ge(sem("c2_done"), 1)
                    for g in range(G):
                        for bank, c0, n in ((g, 64 * g, NCP), (2 + g, 128 + NS2 * g, NS2)):
                            for f, (i, func) in enumerate(((0, ACT.Identity), (1, ACT.Sigmoid))):
                                nc.scalar.activation(hid[:, i, c0:c0 + n], ps[:, bank, 0:n], func,
                                                     bias=cbias[:, kv:kv + 1]).then_inc(sem("hid_read"), 1)

            @block.sync
            def _(sp):
                for kv in range(2):
                    sp.dma_start(w2[:, kv, :], a[("phi_k_w2", "phi_v_w2")[kv]][0]).then_inc(sem("w2_loaded"), 16)
                load_chunks(sp, "gqk0", "gv1")
        s2.close()

        s3 = ExitStack()
        sS = sb(s3, "sS", [P, 2, 1024])
        pP = sb(s3, "pP", [P, 2, 1024])
        pPT = sb(s3, "pPT", [P, 2, 1024])
        bias = sb(s3, "bias", [P, 2, 1024 + 640])
        ndist = sb(s3, "ndist", [P, 1024])
        cdist = sb(s3, "cdist", [P, 2, 512])
        stat = sb(s3, "stat", [P, 256])
        tmp = sb(s3, "tmp", [P, 2, 512])
        mcol = stat[:, 0:16]
        wcol = stat[:, 32:48]

        def lcol(h):
            return stat[:, 64 + 16 * (h % 2):80 + 16 * (h % 2)]

        mcmp, lcmp = stat[:, 48:56], stat[:, 56:64]

        def units():
            return [(h, i, br) for h in range(H) for i in range(PT) for br in range(2)]

        U = units()

        def keys_range(i, br):
            k0 = 0 if br == 0 else max(0, i - WIN // P)
            return k0, i + 1 - k0

        with nc.Block() as block:
            @block.tensor
            def _(pe):
                for i in range(PT):
                    if i >= 1:
                        pe.wait_ge(sem("cmp_scored"), i)
                    for h in range(H):
                        g, r = h // R, h % R
                        mm = nc.tensor.matmul(ps[:, g, 64 * r:64 * r + 64], qT[HD * g:HD * g + HD, r, P * i:P * i + P],
                                              kc[HD * g:HD * g + HD, :], start=True, stop=True)
                    mm.then_inc(sem("cmp_qk"), 1)
                    pe.wait_ge(sem("cmp_probs"), i + 1)
                    if i >= 1:
                        pe.wait_ge(sem("cmp_pT"), 2 * i)
                    for h in range(H):
                        mm = nc.tensor.transpose(ps[0:64, 4 + h // 4, P * (h % 4):P * (h % 4) + P],
                                                 pP[:, 0, 64 * h:64 * h + 64], ident[:, :])
                    mm.then_inc(sem("cmp_T"), 1)
                    pe.wait_ge(sem("cmp_pT"), 2 * i + 2)
                    if i >= 1:
                        pe.wait_ge(sem("cmp_out"), i)
                    for h in range(H):
                        mm = nc.tensor.matmul(ps[:, 6, HD * h:HD * h + HD], pPT[0:64, 0, P * h:P * h + P],
                                              vc[:, HD * (h // R):HD * (h // R) + HD], start=True, stop=True)
                    mm.then_inc(sem("cmp_av"), 1)
                pe.wait_ge(sem("cmp_out"), PT)

                def scores(n):
                    h, i, br = U[n]
                    g, r = h // R, h % R
                    k0, nk = keys_range(i, br)
                    if n >= 2:
                        pe.wait_ge(sem("scored"), n - 1)
                    for c in range(0, nk, 4):
                        w = min(4, nk - c) * P
                        mm = nc.tensor.matmul(ps[:, 2 * (n % 2) + c // 4, 0:w],
                                              qT[HD * g:HD * g + HD, r, P * i:P * i + P],
                                              kT[HD * g:HD * g + HD, 2 + br, P * (k0 + c):P * (k0 + c) + w],
                                              start=True, stop=True)
                    mm.then_inc(sem("qk_done"), 1)

                def transposes(n):
                    h, i, br = U[n]
                    k0, nk = keys_range(i, br)
                    pe.wait_ge(sem("probs"), n + 1)
                    if n >= 1:
                        pe.wait_ge(sem("pT_copied"), n)
                    for k in range(nk):
                        mm = nc.tensor.transpose(ps[:, 4 + k // 4, P * (k % 4):P * (k % 4) + P],
                                                 pP[:, n % 2, P * k:P * k + P], ident[:, :])
                    mm.then_inc(sem("pT_ready"), 1)

                def values(n):
                    h, i, br = U[n]
                    g = h // R
                    k0, nk = keys_range(i, br)
                    pe.wait_ge(sem("pT_copied"), n + 1)
                    if i == 0 and h >= 1:
                        pe.wait_ge(sem("head_out"), 2 * (h - 1) + br + 1)
                    for k in range(nk):
                        mm = nc.tensor.matmul(ps[:, 6 + br, HD * i:HD * i + HD], pPT[:, n % 2, P * k:P * k + P],
                                              vtok[:, k0 + k, P * br + HD * g:P * br + HD * g + HD],
                                              start=(k == 0), stop=(k == nk - 1))
                    mm.then_inc(sem("av_done"), 1)

                scores(0)
                for n in range(len(U) + 1):
                    if n + 1 < len(U):
                        scores(n + 1)
                    if n < len(U):
                        transposes(n)
                    if n >= 1:
                        values(n - 1)

            @block.gpsimd
            def _(pool):
                link = linker(pool, "pool_link")
                pool.wait_ge(sem("slopes"), H)
                for i in range(PT):
                    if i >= 2:
                        pool.wait_ge(sem("cmp_scored"), i - 1)
                    v = cdist[:, i % 2, :].rearrange("p (h c) -> p h c", h=H)
                    link(nc.gpsimd.iota(v, pattern=[[0, H], [-CS, 64]], base=P * i - (CB - 1), channel_multiplier=1,
                                        allow_small_or_imprecise_dtypes=True))
                    link(nc.gpsimd.tensor_tensor(v, v, slope[:, :].unsqueeze(2).to_broadcast([P, H, 64]), ALU.mult))
                    nc.gpsimd.affine_select(out=v, in_=v, compare_op=ALU.is_ge, fill=BIG, base=P * i - (CB - 1),
                                            pattern=[[0, H], [-CS, 64]], channel_multiplier=1)\
                        .then_inc(sem("cbias"), 1)
                link(nc.gpsimd.iota(ndist[:, :], pattern=[[-1, 1024]], base=896, channel_multiplier=1,
                                    allow_small_or_imprecise_dtypes=True))
                for h in range(H):
                    if h >= 2:
                        pool.wait_ge(sem("scored"), 16 * (h - 1))
                    bs, bw = bias[:, h % 2, 0:1024], bias[:, h % 2, 1024:1664]
                    link(nc.gpsimd.tensor_scalar(bs, ndist[:, :], 2.0 ** -(h + 1), None, ALU.mult))
                    link(nc.gpsimd.affine_select(out=bs, in_=bs, compare_op=ALU.is_ge, fill=BIG, base=896,
                                                 pattern=[[-1, 1024]], channel_multiplier=1))
                    link(nc.gpsimd.tensor_copy(bw, bs[:, 384:1024]))
                    nc.gpsimd.affine_select(out=bw[:, 0:P], in_=bw[:, 0:P], compare_op=ALU.is_gt, fill=BIG, base=0,
                                            pattern=[[1, P]], channel_multiplier=-1).then_inc(sem("bias_ready"), 1)

            @block.vector
            def _(dve):
                link = linker(dve, "dve_link")
                v8 = lambda ap: ap.rearrange("p (h c) -> p h c", h=H)
                wide = lambda ap: ap.unsqueeze(2).to_broadcast([P, H, 64])
                for i in range(PT):
                    dve.wait_ge(sem("cmp_qk"), i + 1)
                    dve.wait_ge(sem("cbias"), i + 1)
                    s, p = v8(sS[:, 0, 0:512]), v8(pP[:, 0, 0:512])
                    nc.vector.tensor_tensor(sS[:, 0, 0:512].rearrange("p (g c) -> p g c", g=G), ps[:, 0:2, 0:256],
                                            cdist[:, i % 2, :].rearrange("p (g c) -> p g c", g=G), ALU.add)\
                        .then_inc(sem("cmp_scored"), 1)
                    dve.wait_ge(sem("cmp_scored"), i + 1)
                    link(nc.vector.tensor_reduce(mcmp, s, AX, ALU.min))
                    nc.vector.tensor_tensor(v8(sS[:, 1, 0:512]), s, wide(mcmp), ALU.subtract).then_inc(sem("cmp_sub"), 1)
                    dve.wait_ge(sem("cmp_exp"), i + 1)
                    link(nc.vector.scalar_tensor_tensor(out=pP[:, 1, 0:512], in0=sS[:, 0, 0:512], scalar=0.5 * BIG,
                                                        in1=pP[:, 1, 0:512], op0=ALU.is_lt, op1=ALU.mult))
                    link(nc.vector.tensor_reduce(lcmp, v8(pP[:, 1, 0:512]), AX, ALU.add))
                    link(nc.vector.tensor_scalar(lcmp, lcmp, TINY, None, ALU.max))
                    link(nc.vector.reciprocal(lcmp, lcmp))
                    link(nc.vector.tensor_tensor(lcmp, lcmp, gate[:, i, 0:8], ALU.mult))
                    if i >= 1:
                        dve.wait_ge(sem("cmp_T"), i)
                    nc.vector.tensor_tensor(p, v8(pP[:, 1, 0:512]), wide(lcmp), ALU.mult).then_inc(sem("cmp_probs"), 1)
                    dve.wait_ge(sem("cmp_T"), i + 1)
                    for j in range(2):
                        nc.vector.tensor_copy(pPT[0:64, 0, 512 * j:512 * j + 512], ps[0:64, 4 + j, :])\
                            .then_inc(sem("cmp_pT"), 1)
                    dve.wait_ge(sem("cmp_av"), i + 1)
                    nc.vector.tensor_copy(o_acc[:, i, :], ps[:, 6, :]).then_inc(sem("cmp_out"), 1)
                dve.wait_ge(sem("cmp_out"), PT)

                def score(n):
                    h, i, br = U[n]
                    k0, nk = keys_range(i, br)
                    dve.wait_ge(sem("qk_done"), n + 1)
                    dve.wait_ge(sem("bias_ready"), h + 1)
                    if n >= 2:
                        dve.wait_ge(sem("probs"), n - 1)
                    w = nk * P
                    b0 = (1024 if br == 0 else 1664) - w
                    nc.vector.tensor_tensor_reduce(
                        sS[:, n % 2, 0:w], ps[:, 2 * (n % 2):2 * (n % 2) + 2, :].rearrange("p a c -> p (a c)")[:, 0:w],
                        bias[:, h % 2, b0:b0 + w], 1.0, 3e38, ALU.add, ALU.min,
                        mcol[:, 2 * i + br:2 * i + br + 1]).then_inc(sem("scored"), 1)

                def copy_T(n):
                    h, i, br = U[n]
                    _, nk = keys_range(i, br)
                    dve.wait_ge(sem("pT_ready"), n + 1)
                    if n >= 2:
                        dve.wait_ge(sem("av_done"), n - 1)
                    w = nk * P
                    nc.vector.tensor_copy(pPT[:, n % 2, 0:w],
                                          ps[:, 4:6, :].rearrange("p a c -> p (a c)")[:, 0:w]).then_inc(sem("pT_copied"), 1)

                def finish(h, br):
                    dve.wait_ge(sem("av_done"), 16 * h + 15 + br)
                    pick = lambda ap: ap.rearrange("p (i b) -> p i b", b=2)[:, :, br]
                    link(nc.vector.tensor_scalar(pick(wcol), pick(lcol(h)), TINY, None, ALU.max))
                    link(nc.vector.reciprocal(pick(wcol), pick(wcol)))
                    link(nc.vector.tensor_tensor(pick(wcol), pick(wcol), gate[:, 0:PT, 8 * (1 + br) + h], ALU.mult))
                    nc.vector.tensor_tensor(v8(tmp[:, br, :]), ps[:, 6 + br, :].rearrange("p (h c) -> p h c", h=PT),
                                            pick(wcol).unsqueeze(2).to_broadcast([P, PT, HD]), ALU.mult)\
                        .then_inc(sem("head_out"), 1)
                    dve.wait_ge(sem("head_out"), 2 * h + br + 1)
                    o = o_acc[:, 0:PT, HD * h:HD * h + HD]
                    link(nc.vector.tensor_tensor(o, o, v8(tmp[:, br, :]), ALU.add))

                score(0)
                for n in range(len(U) + 1):
                    if n + 1 < len(U):
                        score(n + 1)
                    if n < len(U):
                        copy_T(n)
                    if n >= 1 and n % 16 == 0:
                        finish(n // 16 - 1, 0)
                        finish(n // 16 - 1, 1)

            @block.scalar
            def _(act):
                for i in range(PT):
                    act.wait_ge(sem("cmp_sub"), i + 1)
                    nc.scalar.activation(pP[:, 1, 0:512], sS[:, 1, 0:512], ACT.Exp, scale=-1.0).then_inc(sem("cmp_exp"), 1)
                act.wait_ge(sem("cmp_out"), PT)
                for n, (h, i, br) in enumerate(U):
                    _, nk = keys_range(i, br)
                    w = nk * P
                    act.wait_ge(sem("scored"), n + 1)
                    if n >= 2:
                        act.wait_ge(sem("pT_ready"), n - 1)
                    if h >= 2 and i == 0:
                        act.wait_ge(sem("head_out"), 2 * (h - 1))
                    c = 2 * i + br
                    nc.scalar.activation(pP[:, n % 2, 0:w], sS[:, n % 2, 0:w], ACT.Exp, bias=mcol[:, c:c + 1],
                                         scale=-1.0, accum_out=lcol(h)[:, c:c + 1]).then_inc(sem("probs"), 1)
        s3.close()


        s4 = ExitStack()
        NK = PAST + ST
        Qb = sb(s4, "Qb", [P, DB, 32])
        kp = sb(s4, "kp", [P, 2, 4, 512])
        vp = sb(s4, "vp", [P, 2, 4, 512])
        kpT = sb(s4, "kpT", [P, 4, 512])
        zS = sb(s4, "zS", [P, NK])
        zP = sb(s4, "zP", [P, NK])
        zPT = sb(s4, "zPT", [P, 5, P])
        zbias = sb(s4, "zbias", [P, 2, 2, NK])
        zcb = sb(s4, "zcb", [P, NCS])
        zx = sb(s4, "zx", [P, NK])
        zm = sb(s4, "zm", [P, NK])
        zcol = sb(s4, "zcol", [P, 64])
        orow = sb(s4, "orow", [P, 2, HD])
        grow = sb(s4, "grow", [P, 2, 3])
        pi, hi, si = (zcol[:, c:c + 1].bitcast(I32) for c in (0, 1, 2))
        t_row, b_row, sl_row, m0, m1, hf = (zcol[:, c:c + 1] for c in range(3, 9))
        zmin, zsum, w0, w1 = (zcol[:, c:c + 1] for c in range(9, 13))
        bcols = zcol[:, 16:48]
        ZU = [(gp, br) for gp in range(2) for br in range(3)]
        NB = 4
        PU = [(gp, br) for gp, br in ZU if br < 2]
        with nc.Block() as block:
            @block.tensor
            def _(pe):
                u2 = 0
                pe.wait_ge(sem("Qb_ready"), G * R)
                for u, (gp, br) in enumerate(ZU):
                    nk = NCS if br == 2 else NK
                    if br < 2:
                        pe.wait_ge(sem(f"kp_loaded{u2 % 2}"), 16 * NB * (u2 // 2 + 1))
                        for b in range(NB):
                            c = NB * u2 + b
                            if c >= 2:
                                pe.wait_ge(sem("kpT_copied"), c - 1)
                            for j in range(4):
                                mm = nc.tensor.transpose(ps[:, 4 + c % 2, P * j:P * j + P],
                                                         kp[:, u2 % 2, b, P * j:P * j + P], ident[:, :])
                            mm.then_inc(sem("kpT_done"), 1)
                        pe.wait_ge(sem("kpT_copied"), NB * (u2 + 1))
                    if u >= 1:
                        pe.wait_ge(sem("z_scored"), u)
                    for b in range(NB):
                        rows = slice(32 * b, 32 * b + 32)
                        q = Qb[:, NB * gp + b, :]
                        if br == 2:
                            mm = nc.tensor.matmul(ps[rows, 0, 0:NCS], q, kcs[:, NB * gp + b, :], start=True, stop=True)
                        else:
                            nc.tensor.matmul(ps[rows, 0, 0:PAST], q, kpT[:, b, :], start=True, stop=True)
                            mm = nc.tensor.matmul(ps[rows, 1, 0:ST], q, kT[:, 2 + br, SEQ:TOK], start=True, stop=True)
                    mm.then_inc(sem("z_qk"), 1)
                    pe.wait_ge(sem("z_probs"), u + 1)
                    if u >= 1:
                        pe.wait_ge(sem("zPT_copied"), u)
                    if br == 2:
                        mm = nc.tensor.transpose(ps[0:NCS, 2, 0:P], zP[:, 0:NCS], ident[:, :])
                    else:
                        for j in range(4):
                            nc.tensor.transpose(ps[:, 2, P * j:P * j + P], zP[:, P * j:P * j + P], ident[:, :])
                        mm = nc.tensor.transpose(ps[0:ST, 3, 0:P], zP[:, PAST:NK], ident[:, :])
                    mm.then_inc(sem("zPT_done"), 1)
                    pe.wait_ge(sem("zPT_copied"), u + 1)
                    if u >= 1:
                        pe.wait_ge(sem("z_out"), u)
                    if br < 2:
                        pe.wait_ge(sem(f"vp_loaded{u2 % 2}"), 16 * NB * (u2 // 2 + 1))
                    for b in range(NB):
                        rows = slice(32 * b, 32 * b + 32)
                        if br == 2:
                            mm = nc.tensor.matmul(ps[rows, 6, 0:P], zPT[0:NCS, 0, rows], vcs[:, NB * gp + b, :],
                                                  start=True, stop=True)
                        else:
                            for j in range(4):
                                nc.tensor.matmul(ps[rows, 6, 0:P], zPT[:, j, rows], vp[:, u2 % 2, b, P * j:P * j + P],
                                                 start=(j == 0), stop=False)
                            mm = nc.tensor.matmul(ps[rows, 6, 0:P], zPT[0:ST, 4, rows],
                                                  vtok[0:ST, PT, P * br:P * br + P], start=False, stop=True)
                    mm.then_inc(sem("z_av"), 1)
                    if br < 2:
                        u2 += 1

            @block.gpsimd
            def _(pool):
                link = linker(pool, "pool_link")
                def fetch(n):
                    gp, br = PU[n]
                    for dst, name, slc, win in ((kp, "kp", a["cache_k_slc"], a["cache_k_win"]),
                                                (vp, "vp", a["cache_v_slc"], a["cache_v_win"])):
                        for b in range(NB):
                            B = NB * gp + b
                            if br == 0:
                                ins = pool.indirect_dma_start(
                                    dst[:, n % 2, b, :], None, slc.rearrange("o n (s j) g d -> (o n s) (j g d)", j=4),
                                    bass.IndirectOffsetOnAxis(ap=idx[:, B:B + 1], axis=0))
                            else:
                                ins = pool.dma_start(dst[:, n % 2, b, :],
                                                     win[0, B].rearrange("(p j) g d -> p (j g d)", j=4))
                            ins.then_inc(sem(f"{name}_loaded{n % 2}"), 16)

                fetch(0)
                fetch(1)
                link(nc.gpsimd.memset(Qb[:, :, :], 0.0))
                pool.sem_inc(sem("Qb_zero"), 1)
                link(nc.gpsimd.iota(pi, pattern=[[0, 1]], base=0, channel_multiplier=1))
                link(nc.gpsimd.iota(zx[:, 0:PAST].rearrange("p (j c) -> p j c", j=4), pattern=[[-1, 4], [-4, P]],
                                    base=PAST, channel_multiplier=0, allow_small_or_imprecise_dtypes=True))
                link(nc.gpsimd.iota(zx[:, PAST:NK].rearrange("p (b t) -> p b t", t=DS), pattern=[[0, DB], [-1, DS]],
                                    base=0, channel_multiplier=0, allow_small_or_imprecise_dtypes=True))
                link(nc.gpsimd.iota(bcols.rearrange("p (b t) -> p b t", t=DS), pattern=[[1, DB], [0, DS]],
                                    base=0, channel_multiplier=0, allow_small_or_imprecise_dtypes=True))
                link(nc.gpsimd.iota(zcb[:, :], pattern=[[-CS, NCS]], base=PAST - (CB - 1), channel_multiplier=0,
                                    allow_small_or_imprecise_dtypes=True))
                pool.sem_inc(sem("z_iota"), 1)
                for n in range(2, len(PU)):
                    pool.wait_ge(sem("z_av"), ZU.index(PU[n - 2]) + 1)
                    fetch(n)

            @block.vector
            def _(dve):
                link = linker(dve, "dve_link")
                dve.wait_ge(sem("Qb_zero"), 1)
                for r in range(R):
                    for g in range(G):
                        rows = slice(HD * g, HD * g + HD)
                        c0 = DS * R * g + DS * r
                        nc.vector.tensor_copy(Qb[rows, :, c0:c0 + DS],
                                              qT[rows, r, SEQ:TOK].rearrange("p (b t) -> p b t", t=DS))\
                            .then_inc(sem("Qb_ready"), 1)
                dve.wait_ge(sem("z_iota"), 1)
                link(nc.vector.tensor_scalar(hi, pi, 3, None, ALU.bitwise_and))
                link(nc.vector.tensor_copy(t_row, hi))
                link(nc.vector.tensor_scalar(hi, pi, 5, None, ALU.logical_shift_right))
                link(nc.vector.tensor_copy(b_row, hi))
                link(nc.vector.tensor_scalar(hi, pi, 2, 7, ALU.logical_shift_right, ALU.bitwise_and))
                link(nc.vector.tensor_copy(hf, hi))
                link(nc.vector.tensor_scalar(m0, hf, float(R), None, ALU.is_lt))
                link(nc.vector.tensor_scalar(m1, hf, float(R), None, ALU.is_ge))
                link(nc.vector.tensor_scalar(hi, hi, -1, 126, ALU.mult, ALU.add))
                link(nc.vector.tensor_scalar(si, hi, 23, None, ALU.logical_shift_left))
                link(nc.vector.tensor_copy(sl_row, zcol[:, 2:3]))
                link(nc.vector.tensor_scalar(zcb[:, :], zcb[:, :], t_row, sl_row, ALU.add, ALU.mult))
                link(nc.vector.tensor_scalar(zx[:, :], zx[:, :], t_row, None, ALU.add))
                new = slice(PAST, NK)
                for gp in range(2):
                    for br in range(2):
                        zb = zbias[:, gp, br, :]
                        link(nc.vector.tensor_scalar(zb, zx[:, :], sl_row, None, ALU.mult))
                        link(nc.vector.tensor_scalar(zm[:, new], zx[:, new], 0.0, BIG, ALU.is_lt, ALU.mult))
                        link(nc.vector.tensor_tensor(zb[:, new], zb[:, new], zm[:, new], ALU.add))
                        link(nc.vector.tensor_scalar(zm[:, new], bcols, float(-NB * gp), b_row, ALU.add, ALU.not_equal))
                        link(nc.vector.tensor_scalar(zm[:, new], zm[:, new], BIG, None, ALU.mult))
                        link(nc.vector.tensor_tensor(zb[:, new], zb[:, new], zm[:, new], ALU.add))
                        if br == 1:
                            link(nc.vector.tensor_scalar(zm[:, :], zx[:, :], float(WIN), BIG, ALU.is_ge, ALU.mult))
                            link(nc.vector.tensor_tensor(zb, zb, zm[:, :], ALU.add))
                link(nc.vector.memset(orow[:, :, :], 0.0))
                dve.wait_ge(sem("grow_loaded"), 16)
                u2 = 0
                for u, (gp, br) in enumerate(ZU):
                    if br < 2:
                        for b in range(NB):
                            c = NB * u2 + b
                            dve.wait_ge(sem("kpT_done"), c + 1)
                            if b == 0 and u >= 1:
                                dve.wait_ge(sem("z_qk"), u)
                            nc.vector.tensor_copy(kpT[:, b, :], ps[:, 4 + c % 2, :]).then_inc(sem("kpT_copied"), 1)
                        u2 += 1
                    nk = NCS if br == 2 else NK
                    dve.wait_ge(sem("z_qk"), u + 1)
                    if u >= 1:
                        dve.wait_ge(sem("z_probs"), u)
                    nc.vector.tensor_tensor_reduce(
                        zS[:, 0:nk], ps[:, 0:2, :].rearrange("p a c -> p (a c)")[:, 0:nk],
                        zcb[:, :] if br == 2 else zbias[:, gp, br, :], 1.0, 3e38, ALU.add, ALU.min, zmin)\
                        .then_inc(sem("z_scored"), 1)
                    dve.wait_ge(sem("zPT_done"), u + 1)
                    if u >= 1:
                        dve.wait_ge(sem("z_av"), u)
                    if br == 2:
                        nc.vector.tensor_copy(zPT[0:NCS, 0, :], ps[0:NCS, 2, 0:P]).then_inc(sem("zPT_copied"), 1)
                    else:
                        link(nc.vector.tensor_copy(zPT[:, 0:4, :].rearrange("p j c -> p (j c)"), ps[:, 2, :]))
                        nc.vector.tensor_copy(zPT[0:ST, 4, :], ps[0:ST, 3, 0:P]).then_inc(sem("zPT_copied"), 1)
                    link(nc.vector.tensor_scalar(w0, zsum, TINY, None, ALU.max))
                    link(nc.vector.reciprocal(w0, w0))
                    gcol = (1, 2, 0)[br]
                    link(nc.vector.tensor_tensor(w0, w0, grow[:, gp, gcol:gcol + 1], ALU.mult))
                    link(nc.vector.tensor_tensor(w1, w0, m1, ALU.mult))
                    link(nc.vector.tensor_tensor(w0, w0, m0, ALU.mult))
                    dve.wait_ge(sem("z_av"), u + 1)
                    link(nc.vector.scalar_tensor_tensor(out=orow[:, gp, :], in0=ps[:, 6, 0:HD], scalar=w0,
                                                        in1=orow[:, gp, :], op0=ALU.mult, op1=ALU.add))
                    nc.vector.scalar_tensor_tensor(out=orow[:, gp, :], in0=ps[:, 6, HD:P], scalar=w1,
                                                   in1=orow[:, gp, :], op0=ALU.mult, op1=ALU.add)\
                        .then_inc(sem("z_out"), 1)
                    dve.wait_ge(sem("z_out"), u + 1)

            @block.scalar
            def _(act):
                for u, (gp, br) in enumerate(ZU):
                    nk = NCS if br == 2 else NK
                    act.wait_ge(sem("z_scored"), u + 1)
                    if u >= 1:
                        act.wait_ge(sem("zPT_done"), u)
                        act.wait_ge(sem("z_out"), u)
                    nc.scalar.activation(zP[:, 0:nk], zS[:, 0:nk], ACT.Exp, bias=zmin, scale=-1.0,
                                         accum_out=zsum).then_inc(sem("z_probs"), 1)

            @block.sync
            def _(sp):
                sp.wait_ge(sem("gate_spilled"), 16 * DB)
                sp.dma_start(grow[:, :, :], gate_spill.rearrange("(q b) x t c -> (b x t) q c", q=2))\
                    .then_inc(sem("grow_loaded"), 16)
                sp.wait_ge(sem("z_out"), len(ZU))
                sp.dma_start(orow_spill.rearrange("(q b) x t d -> (b x t) q d", q=2), orow[:, :, :])\
                    .then_inc(sem("orow_spilled"), 16)
                sp.wait_ge(sem("orow_spilled"), 16)
                for b in range(DB):
                    sp.dma_start(o_acc[DS * b:DS * b + DS, PT, :].rearrange("t (x d) -> t x d", d=HD),
                                 orow_spill[b].rearrange("x t d -> t x d")).then_inc(sem("o_sample"), 16)
                sp.wait_ge(sem("o_sample"), 16 * DB)
                sp.dma_start(o_spill[:, 0:PT, :], o_acc[:, 0:PT, :]).then_inc(sem("o_spilled"), 16)
                sp.dma_start(o_spill[0:ST, PT, :], o_acc[0:ST, PT, :]).then_inc(sem("o_spilled"), 16)
                sp.wait_ge(sem("o_spilled"), 32)
        s4.close()
        nsa.close()

        og = sb(ctx, "og", [P, TILES, GH * DV])
        s5 = ExitStack()
        NCH = SEQ // CH
        raw = sb(s5, "raw", [P, 3, TOK])
        e1 = sb(s5, "e1", [P, TOK])
        bsum = sb(s5, "bsum", [P, TOK])
        eb = sb(s5, "eb", [P, TOK])
        qd = sb(s5, "qd", [P, TOK])
        qi = sb(s5, "qi", [P, SEQ])
        kt = sb(s5, "kt", [P, TOK])
        Wk = sb(s5, "Wk", [P, PT, 4, P])
        W4 = sb(s5, "W4", [P, PT, P])
        vh = sb(s5, "vh", [P, 2, TILES, DV])
        S = sb(s5, "S", [P, 2, DV])
        S0 = sb(s5, "S0", [P, DB, DV])
        reset = sb(s5, "reset", [P, TOK])
        dec = sb(s5, "dec", [P, PT, 5])
        kis = sb(s5, "kis", [P, ST])
        Qm = sb(s5, "Qm", [P, DB, ST])
        bmr = sb(s5, "bmr", [P, DB, ST])
        bmt = sb(s5, "bmt", [ST, DB])
        tris = sb(s5, "tris", [ST, ST])
        ATs = sb(s5, "ATs", [ST, ST])
        aup = sb(s5, "aup", [48, GH * DK])
        AT = e1[:, 0:SEQ]
        k4 = kt[:, 0:SEQ]
        Km = bsum[0:ST, 0:DB * DK]
        ebt = eb[:, 0:SEQ].rearrange("p (t c i) -> p t c i", t=PT, c=4)
        NP_ = 3
        ncore = PT + 1
        with nc.Block() as block:
            @block.tensor
            def _(pe):
                def project(h):
                    if h >= 1:
                        pe.wait_ge(sem("raw_copied"), 3 * h)
                    name = f"gqk{h}"
                    have(pe, name)
                    w = slot(name)
                    for f, lhs in enumerate((lambda k: (w[:, k, 0:P], h_cols(k)), lambda k: (w[:, k, P:2 * P], h_cols(k)))):
                        feature_major(f % 2, lhs, KT).then_inc(sem("g_done"), 1)
                    released[number[name]] = (sem("g_done"), 3 * h + 2)
                    if h == 0:
                        pe.wait_ge(sem("aup_loaded"), 16)
                    pe.wait_ge(sem("raw_copied"), 3 * h + 1)
                    for n in range(3):
                        mm = nc.tensor.matmul(ps[:, n, 0:NF], aup[32:48, DK * h:DK * h + DK],
                                              gaT[32:48, NF * n:NF * n + NF], start=True, stop=True)
                    mm.then_inc(sem("g_done"), 1)
                    have(pe, f"gv{h}")
                    for t in range(TILES):
                        n, c = rows_of(t), TILES * h + t
                        if c >= 2:
                            pe.wait_ge(sem("gv_copied"), c - 1)
                        for k in range(KT):
                            mm = nc.tensor.matmul(ps[0:n, 6 + c % 2, 0:DV], hT[:, k, P * t:P * t + n],
                                                  slot(f"gv{h}")[:, k, :], start=(k == 0), stop=(k == KT - 1))
                        mm.then_inc(sem("gv_done"), 1)
                    released[number[f"gv{h}"]] = (sem("gv_done"), TILES * (h + 1))

                def core(h, last):
                    pe.wait_ge(sem("elem_done"), h + 1)
                    pe.wait_ge(sem("raw_copied"), 3 * min(h + 2, GH))
                    pe.wait_ge(sem("gv_copied"), TILES * min(h + 2, GH))
                    for t in range(PT):
                        for c in range(4):
                            c0 = P * (t % 4) + CH * c
                            mm = nc.tensor.matmul(ps[:, t // 4, c0:c0 + CH], Wk[:, t, c, :],
                                                  qd[:, P * t + CH * c:P * t + CH * c + CH], start=True, stop=True)
                        if t % 4 == 3:
                            mm.then_inc(sem("at_done"), 1)
                    for t in range(PT):
                        mm = nc.tensor.transpose(ps[:, 2 + t // 4, P * (t % 4):P * (t % 4) + P], W4[:, t, :], ident[:, :])
                        if t % 4 == 3:
                            mm.then_inc(sem("w4_done"), 1)
                    for t in range(PT):
                        if t % 4 == 0:
                            pe.wait_ge(sem("k4_copied"), 2 * h + t // 4 + 1)
                            pe.wait_ge(sem("at_copied"), 2 * h + t // 4 + 1)
                        c = PT * h + t
                        if t >= 2:
                            pe.wait_ge(sem("S_ready"), c - 1)
                        nc.tensor.matmul(ps[:, 4 + t % 2, 0:DV], k4[:, P * t:P * t + P], vh[:, h % 2, t, :],
                                         start=True, stop=True).then_inc(sem("u_done"), 1)
                        if t >= 2:
                            pe.wait_ge(sem("go_copied"), ncore * h + t - 1)
                        mm = nc.tensor.matmul(ps[:, 6 + t % 2, 0:DV], AT[:, P * t:P * t + P], vh[:, h % 2, t, :],
                                              start=True, stop=(t == 0))
                        if t >= 1:
                            pe.wait_ge(sem("S_ready"), c)
                            mm = nc.tensor.matmul(ps[:, 6 + t % 2, 0:DV], qi[:, P * t:P * t + P], S[:, t % 2, :],
                                                  start=False, stop=True)
                        mm.then_inc(sem("go_done"), 1)
                    nc.tensor.transpose(ps[0:ST, 2, 0:P], kt[:, SEQ:TOK], ident[:, :])
                    nc.tensor.matmul(ps[0:ST, 0, 0:ST], kis[:, :], qd[:, SEQ:TOK], start=True, stop=True)\
                        .then_inc(sem("sA_done"), 1)
                    pe.wait_ge(sem("sA_ready"), h + 1)
                    pe.wait_ge(sem("S0_loaded"), 16 * (h + 1))
                    pe.wait_ge(sem("go_copied"), ncore * h + PT - 1)
                    vs = vh[0:ST, h % 2, PT, :]
                    nc.tensor.matmul(ps[0:ST, 6, 0:DV], ATs[:, :], vs, start=True, stop=False)
                    for b in range(DB):
                        mm = nc.tensor.matmul(ps[0:ST, 6, 0:DV], Qm[:, b, :], S0[:, b, :], start=False, stop=(b == DB - 1))
                    mm.then_inc(sem("go_done"), 1)
                    pe.wait_ge(sem("S_ready"), PT * (h + 1))
                    for b in range(DB):
                        c = DB * h + b
                        if b >= 2:
                            pe.wait_ge(sem("sS_ready"), c - 1)
                        nc.tensor.matmul(ps[:, 4 + b % 2, 0:DV], Km[:, DK * b:DK * b + DK], vs, start=True, stop=True)\
                            .then_inc(sem("su_done"), 1)
                    pe.wait_ge(sem("sS_ready"), DB * (h + 1))
                    pe.wait_ge(sem("go_copied"), ncore * (h + 1))

                for h in range(GH):
                    project(h)
                    if h >= 1:
                        core(h - 1, False)
                core(GH - 1, True)

            @block.gpsimd
            def _(pool):
                link = linker(pool, "pool_link")
                pool.dma_start(aup[32:48, :], a["gla_alpha_up"][0]).then_inc(sem("aup_loaded"), 16)
                for m in (reset, bmr, bmt, Wk):
                    f = m[tuple([slice(None)] * len(m.shape))]
                    nc.gpsimd.memset(f, 0.0 if m is Wk else 1.0).then_inc(sem("g_ones"), 1)
                nc.gpsimd.tensor_copy(tris[:, :], tri[0:ST, 0:ST]).then_inc(sem("g_ones"), 1)
                nc.gpsimd.memset(dec[:, :, 0:1], 1.0).then_inc(sem("g_ones"), 1)
                pool.wait_ge(sem("g_ones"), 6)
                link(nc.gpsimd.memset(reset[:, 0:SEQ:CH], 0.0))
                link(nc.gpsimd.memset(reset[:, SEQ:TOK:DS], 0.0))
                keep = lambda out, base, pattern, cm: link(nc.gpsimd.affine_select(
                    out=out, in_=out, compare_op=ALU.is_ge, fill=0.0, base=base, pattern=pattern, channel_multiplier=cm))
                keep(bmr[:, :, :], 0, [[-DS, DB], [1, ST]], 0)
                keep(bmr[:, :, :], DS - 1, [[DS, DB], [-1, ST]], 0)
                keep(bmt[:, :], 0, [[-DS, DB]], 1)
                keep(bmt[:, :], DS - 1, [[DS, DB]], -1)
                keep(tris[:, :].rearrange("p (b t) -> p b t", t=DS), 0, [[-DS, DB], [0, DS]], 1)
                pool.sem_inc(sem("g_masks"), 1)

            @block.vector
            def _(dve):
                link = linker(dve, "dve_link")
                chunks_of = lambda ap: ap[:, 0:SEQ].rearrange("p (n i) -> p n i", i=CH)
                seqs_of = lambda ap: ap[:, SEQ:TOK].rearrange("p (b t) -> p b t", t=DS)
                tt = nc.vector.tensor_tensor

                def elementwise(h):
                    if h >= 1:
                        dve.wait_ge(sem("su_done"), DB * h)
                    dve.wait_ge(sem("raw_copied"), 3 * (h + 1))
                    q, k, z = raw[:, 0, :], raw[:, 1, :], raw[:, 2, :]
                    nc.vector.scalar_tensor_tensor(out=e1[:, :], in0=z, scalar=-1.0, in1=z, op0=ALU.mult, op1=ALU.min)\
                        .then_inc(sem("to_act"), 1)
                    dve.wait_ge(sem("from_act"), 4 * h + 1)
                    link(nc.vector.scalar_tensor_tensor(out=eb[:, :], in0=z, scalar=0.0, in1=e1[:, :],
                                                        op0=ALU.min, op1=ALU.subtract))
                    nc.vector.tensor_tensor_scan(bsum[:, :], reset[:, :], eb[:, :], 0.0, ALU.mult, ALU.add)\
                        .then_inc(sem("to_act"), 1)
                    dve.wait_ge(sem("to_act"), 3 * h + 2)
                    dve.wait_ge(sem("from_act"), 4 * h + 3)
                    link(tt(qd[:, :], q, eb[:, :], ALU.mult))
                    link(tt(diag(),
                            k[:, 0:SEQ].rearrange("p (t c i) -> p t c i", t=PT, c=4),
                            e1[:, 0:SEQ].rearrange("p (t c i) -> p t c i", t=PT, c=4), ALU.mult))
                    link(tt(kis[:, :], k[:, SEQ:TOK], e1[:, SEQ:TOK], ALU.mult))
                    link(tt(chunks_of(e1), chunks_of(bsum)[:, :, CH - 1:CH].to_broadcast([P, NCH, CH]), chunks_of(bsum),
                            ALU.subtract))
                    tt(seqs_of(e1), seqs_of(bsum)[:, :, DS - 1:DS].to_broadcast([P, DB, DS]), seqs_of(bsum),
                       ALU.subtract).then_inc(sem("to_act"), 1)
                    dve.wait_ge(sem("from_act"), 4 * h + 4)
                    link(tt(kt[:, :], k, e1[:, :], ALU.mult))
                    kc4 = kt[:, 0:SEQ].rearrange("p (t c i) -> p t c i", t=PT, c=4)
                    for c in range(1, 5):
                        dst = Wk[:, :, c, :] if c < 4 else W4[:, :, :]
                        if c > 1:
                            w = CH * (c - 1)
                            link(tt(dst[:, :, 0:w], Wk[:, :, c - 1, 0:w],
                                    ebt[:, :, c - 1, CH - 1:CH].to_broadcast([P, PT, w]), ALU.mult))
                        link(nc.vector.tensor_copy(dst[:, :, CH * (c - 1):CH * c], kc4[:, :, c - 1, :]))
                        link(tt(dec[:, :, c:c + 1], dec[:, :, c - 1:c], ebt[:, :, c - 1, CH - 1:CH], ALU.mult))
                    link(tt(qi[:, :].rearrange("p (t c i) -> p t c i", t=PT, c=4),
                            qd[:, 0:SEQ].rearrange("p (t c i) -> p t c i", t=PT, c=4),
                            dec[:, :, 0:4].unsqueeze(3).to_broadcast([P, PT, 4, CH]), ALU.mult))
                    tt(Qm[:, :, :], qd[:, SEQ:TOK].unsqueeze(1).to_broadcast([P, DB, ST]), bmr[:, :, :], ALU.mult)\
                        .then_inc(sem("elem_done"), 1)
                    dve.wait_ge(sem("elem_done"), h + 1)

                def diag():
                    v = Wk[:, :, :, :].rearrange("p t c i -> p t (c i)")
                    return bass.AP(v.tensor, v.offset, [v.ap[0], [4 * P, PT], [P + CH, 4], [1, CH]])

                def core(h):
                    for j in range(2):
                        dve.wait_ge(sem("at_done"), 2 * h + j + 1)
                        tt(AT[:, 512 * j:512 * j + 512].rearrange("p (t i) -> p t i", t=4),
                           ps[:, j, :].rearrange("p (t i) -> p t i", t=4),
                           tri[:, :].unsqueeze(1).to_broadcast([P, 4, P]), ALU.mult).then_inc(sem("at_copied"), 1)
                    for t in range(PT):
                        c = PT * h + t
                        dve.wait_ge(sem("u_done"), c + 1)
                        dst, u = S[:, (t + 1) % 2, :], ps[:, 4 + t % 2, 0:DV]
                        if t >= 1:
                            dve.wait_ge(sem("go_done"), ncore * h + t)
                            dve.wait_ge(sem("S_ready"), c)
                            ins = nc.vector.scalar_tensor_tensor(out=dst, in0=S[:, t % 2, :], scalar=dec[:, t, 4:5],
                                                                 in1=u, op0=ALU.mult, op1=ALU.add)
                        else:
                            ins = nc.vector.tensor_copy(dst, u)
                        ins.then_inc(sem("S_ready"), 1)
                        if t == 0 and h >= 1:
                            dve.wait_ge(sem("pgla_stored"), 16 * h)
                    dve.wait_ge(sem("sA_done"), h + 1)
                    if h == 0:
                        dve.wait_ge(sem("g_masks"), 1)
                    link(tt(Km.rearrange("p (b c) -> p b c", b=DB), ps[0:ST, 2, 0:P].unsqueeze(1).to_broadcast([ST, DB, P]),
                            bmt[:, :].unsqueeze(2).to_broadcast([ST, DB, P]), ALU.mult))
                    tt(ATs[:, :], ps[0:ST, 0, 0:ST], tris[:, :], ALU.mult).then_inc(sem("sA_ready"), 1)
                    dve.wait_ge(sem("go_done"), ncore * (h + 1))
                    for b in range(DB):
                        dve.wait_ge(sem("su_done"), DB * h + b + 1)
                        nc.vector.scalar_tensor_tensor(out=S0[:, b, :], in0=S0[:, b, :],
                                                       scalar=eb[:, SEQ + DS * b + DS - 1:SEQ + DS * b + DS],
                                                       in1=ps[:, 4 + b % 2, 0:DV], op0=ALU.mult, op1=ALU.add)\
                            .then_inc(sem("sS_ready"), 1)

                dve.wait_ge(sem("g_masks"), 1)
                for h in range(GH):
                    if h >= 1:
                        core(h - 1)
                    elementwise(h)
                core(GH - 1)

            @block.scalar
            def _(act):
                act.wait_ge(sem("vectors"), 80)

                def project(h):
                    if h >= 1:
                        act.wait_ge(sem("elem_done"), h)
                    for f in range(3):
                        act.wait_ge(sem("g_done"), 3 * h + f + 1)
                        if f < 2:
                            ins = nc.scalar.activation(split3(raw[:, f, :]), banks(f % 2), ACT.Copy,
                                                       scale=DK ** -0.5 if f == 0 else 1.0)
                        else:
                            ins = nc.scalar.activation(split3(raw[:, f, :]), banks(0), ACT.Identity,
                                                       bias=ab_col[:, h:h + 1])
                        ins.then_inc(sem("raw_copied"), 1)
                    for t in range(TILES):
                        n, c = rows_of(t), TILES * h + t
                        act.wait_ge(sem("gv_done"), c + 1)
                        nc.scalar.activation(vh[0:n, h % 2, t, :], ps[0:n, 6 + c % 2, 0:DV], ACT.Copy)\
                            .then_inc(sem("gv_copied"), 1)

                def elementwise(h):
                    act.wait_ge(sem("to_act"), 3 * h + 1)
                    nc.scalar.activation(e1[:, :], e1[:, :], ACT.Exp).then_inc(sem("act_link"), 1)
                    act.wait_ge(sem("act_link"), h + 1)
                    nc.scalar.activation(e1[:, :], e1[:, :], ACT.Ln, bias=1.0).then_inc(sem("from_act"), 1)
                    act.wait_ge(sem("to_act"), 3 * h + 2)
                    nc.scalar.activation(eb[:, :], bsum[:, :], ACT.Exp, scale=1.0 / TAU).then_inc(sem("from_act"), 1)
                    nc.scalar.activation(e1[:, :], bsum[:, :], ACT.Exp, scale=-1.0 / TAU).then_inc(sem("from_act"), 1)
                    act.wait_ge(sem("to_act"), 3 * h + 3)
                    nc.scalar.activation(e1[:, :], e1[:, :], ACT.Exp, scale=1.0 / TAU).then_inc(sem("from_act"), 1)

                def core(h):
                    for j in range(2):
                        act.wait_ge(sem("w4_done"), 2 * h + j + 1)
                        nc.scalar.activation(k4[:, 512 * j:512 * j + 512], ps[:, 2 + j, :], ACT.Copy)\
                            .then_inc(sem("k4_copied"), 1)
                    for t in range(TILES):
                        n = rows_of(t)
                        act.wait_ge(sem("go_done"), ncore * h + t + 1)
                        nc.scalar.activation(og[0:n, t, DV * h:DV * h + DV], ps[0:n, 6 + t % 2, 0:DV], ACT.Copy)\
                            .then_inc(sem("go_copied"), 1)

                for h in range(GH):
                    project(h)
                    if h >= 1:
                        core(h - 1)
                    elementwise(h)
                core(GH - 1)

            @block.sync
            def _(sp):
                sp.dma_start(S0[:, :, :], a["state_gla"][0, :, 0].rearrange("b k v -> k b v")).then_inc(sem("S0_loaded"), 16)
                for h in range(GH):
                    if h == 0:
                        load_chunks(sp, "gqk2", "gqk2")
                        load_chunks(sp, "gv2", "gv2")
                    if h == 1:
                        load_chunks(sp, "gqk3", "gv3")
                    sp.wait_ge(sem("S_ready"), PT * (h + 1))
                    sp.dma_start(p_gla[0, 0, h], S[:, 0, :]).then_inc(sem("pgla_stored"), 16)
                    sp.wait_ge(sem("sS_ready"), DB * (h + 1))
                    sp.dma_start(s_gla[0, :, h].rearrange("b k v -> k b v"), S0[:, :, :]).then_inc(sem("sgla_stored"), 16)
                    sp.wait_ge(sem("sgla_stored"), 16 * (h + 1))
                    if h + 1 < GH:
                        sp.dma_start(S0[:, :, :], a["state_gla"][0, :, h + 1].rearrange("b k v -> k b v"))\
                            .then_inc(sem("S0_loaded"), 16)
                    if h == 1:
                        load_chunks(sp, "za0", "za1")
                load_chunks(sp, "zb0", "zb1")
                sp.wait_ge(sem("pgla_stored"), 16 * GH)
        s5.close()

        oT = sb(ctx, "oT", [P, 4, TOK])
        ogT = sb(ctx, "ogT", [P, KT, TOK])
        s6 = ExitStack()
        oN = sb(s6, "oN", [P, TILES, 512])
        zz = sb(s6, "zz", [P, 2, TOK])
        zg = sb(s6, "zg", [P, 2, TOK])
        junk = zg[:, 0, 0:DV]
        gss = sb(s6, "gss", [P, TILES * GH])
        grs = sb(s6, "grs", [P, TILES * GH])
        ogv = og[:, :, :].rearrange("p t (h v) -> p (t h) v", h=GH)
        NZ = 12
        with nc.Block() as block:
            @block.tensor
            def _(pe):
                def gates(f):
                    name = f"za{f // 2}" if f < 4 else f"zb{(f - 4) // 2}"
                    have(pe, name)
                    if f >= 2:
                        pe.wait_ge(sem("z_copied"), 2 * (f - 1))
                    w = slot(name)
                    feature_major(f % 2, lambda k: (w[:, k, P * (f % 2):P * (f % 2) + P], h_cols(k)), KT)\
                        .then_inc(sem("z_done"), 1)
                    released[number[name]] = (sem("z_done"), f + 1)

                def turn(f):
                    src = oN[:, :, P * f:P * f + P] if f < 4 else og[:, :, P * (f - 4):P * (f - 4) + P]
                    if f == 0:
                        pe.wait_ge(sem("oN_loaded"), 32)
                    if f == 4:
                        pe.wait_ge(sem("og_normed"), 2)
                    for j in range(3):
                        last = 3 * f + (0, -1, 1)[j]
                        if last > 0:
                            pe.wait_ge(sem("oT_copied"), last)
                        for t in range(4 * j, min(4 * j + 4, TILES)):
                            n = rows_of(t)
                            mm = nc.tensor.transpose(ps[:, 6 + j % 2, P * (t % 4):P * (t % 4) + n], src[0:n, t, :],
                                                     ident[0:n, 0:n])
                        mm.then_inc(sem("oT_done"), 1)

                for f in range(NZ):
                    gates(f)
                    if f >= 1:
                        turn(f - 1)
                turn(NZ - 1)

            @block.vector
            def _(dve):
                link = linker(dve, "dve_link")
                dve.wait_ge(sem("g_squares"), GH * TILES)
                link(nc.vector.tensor_scalar(grs[:, :], gss[:, :], 1.0 / DV, EPS, ALU.mult, ALU.add))
                dve.sem_inc(sem("g_var"), 1)
                dve.wait_ge(sem("g_sd"), 1)
                link(nc.vector.reciprocal(grs[:, :], gss[:, :]))
                NG = GH * PT
                nc.vector.tensor_tensor(ogv[:, 0:NG, :], ogv[:, 0:NG, :],
                                        grs[:, 0:NG].unsqueeze(2).to_broadcast([P, NG, DV]), ALU.mult)\
                    .then_inc(sem("og_normed"), 1)
                nc.vector.tensor_tensor(ogv[0:ST, NG:, :], ogv[0:ST, NG:, :],
                                        grs[0:ST, NG:].unsqueeze(2).to_broadcast([ST, GH, DV]), ALU.mult)\
                    .then_inc(sem("og_normed"), 1)
                for f in range(NZ):
                    dve.wait_ge(sem("z_copied"), 2 * (f + 1))
                    z = zz[:, f % 2, :]
                    link(nc.vector.tensor_tensor(z, z, zg[:, f % 2, :], ALU.mult))
                    for j in range(3):
                        dve.wait_ge(sem("oT_done"), 3 * f + j + 1)
                        w = min(512, TOK - 512 * j)
                        c = slice(512 * j, 512 * j + w)
                        src = ps[:, 6 + j % 2, 0:w]
                        if f < 4:
                            ins = nc.vector.tensor_tensor(oT[:, f, c], src, z[:, c], ALU.mult)
                        else:
                            ins = nc.vector.scalar_tensor_tensor(out=ogT[:, f - 4, c], in0=src,
                                                                 scalar=gn_col[:, f % 2:f % 2 + 1], in1=z[:, c],
                                                                 op0=ALU.mult, op1=ALU.mult)
                        ins.then_inc(sem("oT_copied"), 1)

            @block.gpsimd
            def _(pool):
                pool.memset(gss[:, :], 1.0).then_inc(sem("gss_ones"), 1)

            @block.scalar
            def _(act):
                act.wait_ge(sem("gss_ones"), 1)
                for t in range(TILES):
                    n = rows_of(t)
                    for h in range(GH):
                        c = GH * t + h
                        if c >= 1:
                            act.wait_ge(sem("g_squares"), c)
                        nc.scalar.activation(junk[0:n, :], og[0:n, t, DV * h:DV * h + DV], ACT.Square,
                                             accum_out=gss[0:n, c:c + 1]).then_inc(sem("g_squares"), 1)
                act.wait_ge(sem("g_var"), 1)
                act.wait_ge(sem("g_squares"), GH * TILES)
                nc.scalar.activation(gss[:, :], grs[:, :], ACT.Sqrt).then_inc(sem("g_sd"), 1)
                for f in range(NZ):
                    act.wait_ge(sem("z_done"), f + 1)
                    if f >= 2:
                        act.wait_ge(sem("oT_copied"), 3 * (f - 1))
                    nc.scalar.activation(split3(zz[:, f % 2, :]), banks(f % 2), ACT.Copy).then_inc(sem("z_copied"), 1)
                    nc.scalar.activation(split3(zg[:, f % 2, :]), banks(f % 2), ACT.Sigmoid).then_inc(sem("z_copied"), 1)

            @block.sync
            def _(sp):
                sp.dma_start(oN[:, 0:PT, :], o_spill[:, 0:PT, :]).then_inc(sem("oN_loaded"), 16)
                sp.dma_start(oN[0:ST, PT, :], o_spill[0:ST, PT, :]).then_inc(sem("oN_loaded"), 16)
                load_chunks(sp, "zb2", "wa0")
        s6.close()

        mixT = og[:, :, :].rearrange("p t c -> p (t c)")[:, 0:KT * TOK].rearrange("p (k c) -> p k c", k=KT)
        s7 = ExitStack()
        sg = sb(s7, "sg", [P, 4, TOK])
        ta = sb(s7, "ta", [P, 2, TOK])
        tb = sb(s7, "tb", [P, TOK])
        kinds = ("ma", "wa", "mb", "wb")
        steps = [(j, kind, s) for j in range(4) for kind in kinds for s in range(2)]
        with nc.Block() as block:
            def drained(n):
                j, kind, s = steps[n]
                who = "m_gated" if kind[0] == "m" else "m_merged"
                return sem(who), sum(1 for q in steps[:n + 1] if q[1][0] == kind[0])

            @block.tensor
            def _(pe):
                for n, (j, kind, s) in enumerate(steps):
                    name = f"{kind}{j}"
                    have(pe, name)
                    if n >= 2:
                        pe.wait_ge(*drained(n - 2))
                    w = slot(name)
                    if kind == "wa":
                        rhs = lambda k: (lambda i: oT[:, k, NF * i:NF * i + NF])
                    elif kind == "wb":
                        rhs = lambda k: (lambda i: ogT[:, k, NF * i:NF * i + NF])
                    else:
                        rhs = h_cols
                    feature_major(n % 2, lambda k: (w[:, k, P * s:P * s + P], rhs(k)), 4 if kind == "wa" else KT)\
                        .then_inc(sem("m_done"), 1)
                    released[number[name]] = (sem("m_done"), n + 1)

            @block.scalar
            def _(act):
                for n, (j, kind, s) in enumerate(steps):
                    if kind[0] != "m":
                        continue
                    act.wait_ge(sem("m_done"), n + 1)
                    i = s if kind == "ma" else 2 + s
                    if j >= 1:
                        act.wait_ge(*drained(steps.index((j - 1, "w" + kind[1], s))))
                    nc.scalar.activation(split3(sg[:, i, :]), banks(n % 2), ACT.Sigmoid).then_inc(sem("m_gated"), 1)

            @block.vector
            def _(dve):
                link = linker(dve, "dve_link")
                for n, (j, kind, s) in enumerate(steps):
                    if kind[0] != "w":
                        continue
                    dve.wait_ge(sem("m_done"), n + 1)
                    i = s if kind == "wa" else 2 + s
                    dve.wait_ge(*drained(steps.index((j, "m" + kind[1], s))))
                    dst = ta[:, s, :] if kind == "wa" else tb[:, :]
                    nc.vector.tensor_tensor(split3(dst), banks(n % 2), split3(sg[:, i, :]), ALU.mult)\
                        .then_inc(sem("m_merged"), 1)
                    if kind == "wb":
                        dve.wait_ge(*drained(n))
                        link(nc.vector.tensor_tensor(mixT[:, 2 * j + s, :], ta[:, s, :], tb[:, :], ALU.add))

            @block.sync
            def _(sp):
                load_chunks(sp, "mb0", "wo3")
        s7.close()

        s8 = ExitStack()
        xr = sb(s8, "xr", [P, 3, D])
        yy = sb(s8, "yy", [P, 3, D])
        jk = sb(s8, "jk", [P, D])
        fg = sb(s8, "fg", [P, D])
        fst = sb(s8, "fst", [P, 2 * TILES])
        with nc.Block() as block:
            @block.tensor
            def _(pe):
                for t in range(TILES):
                    n = rows_of(t)
                    if t >= 4:
                        pe.wait_ge(sem("y_added"), t - 3)
                    for j in range(4):
                        have(pe, f"wo{j}")
                        for k in range(KT):
                            mm = nc.tensor.matmul(ps[0:n, 2 * (t % 4) + j // 2, 256 * (j % 2):256 * (j % 2) + 256],
                                                  mixT[:, k, P * t:P * t + n], slot(f"wo{j}")[:, k, :],
                                                  start=(k == 0), stop=(k == KT - 1))
                    mm.then_inc(sem("y_done"), 1)

            @block.vector
            def _(dve):
                link = linker(dve, "dve_link")
                dve.wait_ge(sem("fg_loaded"), 16)
                for t in range(TILES):
                    n = rows_of(t)
                    dve.wait_ge(sem("y_done"), t + 1)
                    dve.wait_ge(sem(f"xr_loaded{t % 3}"), 16 * (t // 3 + 1))
                    if t >= 3:
                        dve.wait_ge(sem(f"y_stored{t % 3}"), 16 * (t // 3))
                    y = yy[0:n, t % 3, :]
                    nc.vector.tensor_tensor(y, ps[0:n, 2 * (t % 4):2 * (t % 4) + 2, :].rearrange("p a c -> p (a c)"),
                                            xr[0:n, t % 3, :], ALU.add).then_inc(sem("y_added"), 1)
                    ss, r = fst[0:n, 2 * t:2 * t + 1], fst[0:n, 2 * t + 1:2 * t + 2]
                    dve.wait_ge(sem("y_squared"), t + 1)
                    nc.vector.tensor_scalar(r, ss, 1.0 / D, EPS, ALU.mult, ALU.add).then_inc(sem("y_var"), 1)
                    dve.wait_ge(sem("y_sd"), t + 1)
                    link(nc.vector.reciprocal(r, ss))
                    nc.vector.scalar_tensor_tensor(out=y, in0=y, scalar=r, in1=fg[0:n, :], op0=ALU.mult, op1=ALU.mult)\
                        .then_inc(sem("y_ready"), 1)

            @block.scalar
            def _(act):
                for t in range(TILES):
                    n = rows_of(t)
                    ss, r = fst[0:n, 2 * t:2 * t + 1], fst[0:n, 2 * t + 1:2 * t + 2]
                    act.wait_ge(sem("y_added"), t + 1)
                    if t >= 1:
                        act.wait_ge(sem("y_squared"), t)
                    nc.scalar.activation(jk[0:n, :], yy[0:n, t % 3, :], ACT.Square, accum_out=ss)\
                        .then_inc(sem("y_squared"), 1)
                    act.wait_ge(sem("y_var"), t + 1)
                    nc.scalar.activation(ss, r, ACT.Sqrt).then_inc(sem("y_sd"), 1)

            @block.sync
            def _(sp):
                sp.dma_start(fg[:, :], a["final_norm_g"].unsqueeze(0).to_broadcast([P, D])).then_inc(sem("fg_loaded"), 16)

                def load_x(t):
                    src = a["x_prompt"][0, P * t:P * t + P, :] if t < PT else \
                        a["x_sample"].rearrange("b s d -> (b s) d")
                    sp.dma_start(xr[0:rows_of(t), t % 3, :], src).then_inc(sem(f"xr_loaded{t % 3}"), 16)

                for t in range(3):
                    load_x(t)
                for t in range(TILES):
                    if t + 3 < TILES:
                        sp.wait_ge(sem("y_added"), t + 1)
                        load_x(t + 3)
                    sp.wait_ge(sem("y_ready"), t + 1)
                    dst = y_p[0, P * t:P * t + P, :] if t < PT else y_s.rearrange("b s d -> (b s) d")
                    sp.dma_start(dst, yy[0:rows_of(t), t % 3, :]).then_inc(sem(f"y_stored{t % 3}"), 16)
                for s in range(3):
                    sp.wait_ge(sem(f"y_stored{s}"), 16 * 3)
                sp.wait_ge(sem("stored"), 16 * out_count[0])
                sp.wait_ge(sem("sgla_stored"), 16 * GH)
        s8.close()


_INS = ["x_prompt", "x_sample", "cache_k_cmp", "cache_v_cmp", "cache_k_slc", "cache_v_slc", "cache_k_win",
        "cache_v_win", "state_gla", "page_table", "norm_g", "w_in", "phi_k_pe", "phi_k_w1", "phi_k_w2",
        "phi_v_pe", "phi_v_w1", "phi_v_w2", "gla_alpha_up", "gla_alpha_b", "gla_norm_g", "w_branch_a",
        "w_branch_b", "w_out", "final_norm_g"]
_OUTS = ([(1, SEQ, D), (DB, DS, D)] + [(1, 1, SEQ, G, HD)] * 4 + [(1, 1, WIN, G, HD)] * 2 + [(1, 1, GH, DK, DV)]
         + [(1, DB, DS, G, HD)] * 4 + [(1, DB, WIN, G, HD)] * 2 + [(1, DB, GH, DK, DV)])


def kernel(**inputs):
    import numpy as _np
    import concourse.bacc as _bacc
    from concourse import mybir as _mybir
    from concourse.bass_utils import run_bass_kernel_spmd as _run

    nc = _bacc.Bacc("TRN2", target_bir_lowering=False, num_devices=1)
    arrays, args = {}, {}
    for name in _INS:
        x = _np.ascontiguousarray(inputs[name])
        arrays[f"in_{name}"] = x
        args[name] = nc.dram_tensor(f"in_{name}", x.shape, _mybir.dt.from_np(x.dtype), kind="ExternalInput").ap()
    outs = [nc.dram_tensor(f"out_{i}", shape, F32, kind="ExternalOutput").ap() for i, shape in enumerate(_OUTS)]
    hybrid_step(nc, args, outs)
    r = _run(nc, [arrays], core_ids=[0])
    return tuple(r.results[0][f"out_{i}"] for i in range(len(_OUTS)))
```

```python
from contextlib import ExitStack

import concourse.bass as bass
from concourse import mybir

F32 = mybir.dt.float32
I32 = mybir.dt.int32
ALU = mybir.AluOpType
ACT = mybir.ActivationFunctionType
AX = mybir.AxisListType.X

P = 128
D = 1024
KT = D // P
SEQ = 1024
PT = SEQ // P
DB, DS = 8, 4
ST = DB * DS
TILES = PT + 1
TOK = SEQ + ST
NF = TOK // 3
PAST, PAGE, NPAGES, NPOOL = 512, 128, 4, 40
H, G, R, HD = 8, 2, 4, 64
CB, CS, SB_POS = 32, 16, 32
NCP = (SEQ - CB) // CS + 1
NCS = (PAST + DS - CB) // CS + 1
WIN = 512
GH, DK, DV = 4, 128, 256
RANK, TAU = 16, 16.0
CH = 32
EPS, BIG, TINY = 1e-6, 1e30, 1e-30
NSLOT = 4
C_Q, C_KV, C_GATE, C_ZA = 0, 512, 1280, 1304
C_QG, C_KG, C_VG, C_AL, C_ZB, C_MRG = 1816, 2328, 2840, 3864, 3880, 4904


def rows_of(t):
    return P if t < PT else ST


def hybrid_step(nc, a, outs):
    (y_p, y_s, p_kc, p_vc, p_ks, p_vs, p_kw, p_vw, p_gla,
     s_kc, s_vc, s_ks, s_vs, s_kw, s_vw, s_gla) = outs
    w_in = a["w_in"][0]
    ctx = ExitStack()
    sem_names = {}

    def sem(name):
        if name not in sem_names:
            sem_names[name] = ctx.enter_context(nc.semaphore(name))
        return sem_names[name]

    def sb(stack, name, shape, dt=F32):
        return stack.enter_context(nc.sbuf_tensor(name, shape, dt))

    with ctx:
        hT = sb(ctx, "hT", [P, KT, TOK])
        wr = sb(ctx, "wr", [P, NSLOT, 2048])
        gaT = sb(ctx, "gaT", [48, TOK])
        gate = sb(ctx, "gate", [P, TILES, 24])
        ident = sb(ctx, "ident", [P, P])
        tri = sb(ctx, "tri", [P, P])
        small = sb(ctx, "small", [P, 256])
        idx = sb(ctx, "idx", [P, DB], I32)
        ps = ctx.enter_context(nc.psum_tensor("ps", [P, 8, 512], F32))

        o_spill = nc.dram_tensor("o_spill", [P, TILES, 512], F32, kind="Internal").ap()
        gate_spill = nc.dram_tensor("gate_spill", [DB, H, DS, 3], F32, kind="Internal").ap()
        orow_spill = nc.dram_tensor("orow_spill", [DB, H, DS, HD], F32, kind="Internal").ap()

        ng_col = small[:, 0:8]
        ab_col = small[:, 8:12]
        gn_col = small[:, 12:14]
        ssq = small[:, 16:25]
        rstd = small[:, 32:41]
        pe2 = small[:, 64:96].rearrange("p (v s) -> p v s", v=2)
        pt_all = small[:, 128:160].bitcast(I32)
        pbase = small[:, 160:161].bitcast(I32)

        link_count = {}

        def linker(eng, name):
            s = sem(name)

            def link(ins):
                link_count[name] = link_count.get(name, 0) + 1
                ins.then_inc(s, 1)
                eng.wait_ge(s, link_count[name])
            return link

        chunks, number = [], {}

        def chunk(name, *parts):
            number[name] = len(chunks)
            chunks.append(parts)

        def cols(src, c0, n, ks=KT, at=0, width=256):
            v = src.rearrange("(k p) c -> p k c", p=P)
            h = ks // 2
            return [(k0, h, at, n, width, v[:, k0:k0 + h, c0:c0 + n]) for k0 in (0, h)]

        def pair(src, c0, c1, n=P):
            v = src.rearrange("(k p) c -> p k c", p=P)
            return [(0, KT, at, n, 256, v[:, :, c:c + n]) for at, c in ((0, c0), (P, c1))]

        for j in range(2):
            v = w_in.rearrange("(k p) c -> p k c", p=P)
            chunk(f"q{j}", *[(0, KT, P * r + HD * g, HD, 256,
                              v[:, :, C_Q + 256 * g + P * j + HD * r:C_Q + 256 * g + P * j + HD * r + HD])
                             for r in range(2) for g in range(G)])
        chunk("cmp", *cols(w_in, C_KV, 256))
        chunk("slc", *cols(w_in, C_KV + 256, 256))
        chunk("win", *cols(w_in, C_KV + 512, 256))
        vin = w_in.rearrange("(k p) c -> p k c", p=P)
        chunk("ga", (0, KT, 0, 32, 48, vin[:, :, C_GATE:C_GATE + 32]),
              (0, KT, 32, RANK, 48, vin[:, :, C_AL:C_AL + RANK]))
        for kv in "kv":
            w1 = a[f"phi_{kv}_w1"][0].rearrange("(s p) c -> p s c", p=P)
            chunk(f"w1{kv}", *[(8 * i, 8, 0, P, P, w1[:, 8 * i:8 * i + 8, :]) for i in range(2)])
        for h in range(GH):
            chunk(f"gqk{h}", *pair(w_in, C_QG + P * h, C_KG + P * h))
            chunk(f"gv{h}", *cols(w_in, C_VG + DV * h, DV))
        for j in range(2):
            chunk(f"za{j}", *cols(w_in, C_ZA + 256 * j, 256))
        for j in range(4):
            chunk(f"zb{j}", *cols(w_in, C_ZB + 256 * j, 256))
        for j in range(4):
            chunk(f"ma{j}", *cols(w_in, C_MRG + 256 * j, 256))
            chunk(f"wa{j}", *cols(a["w_branch_a"][0], 256 * j, 256, ks=4))
            chunk(f"mb{j}", *cols(w_in, C_MRG + D + 256 * j, 256))
            chunk(f"wb{j}", *cols(a["w_branch_b"][0], 256 * j, 256))
        for j in range(4):
            chunk(f"wo{j}", *cols(a["w_out"][0], 256 * j, 256))

        released = {}

        def slot(name, width=256):
            return wr[:, number[name] % NSLOT, 0:KT * width].rearrange("p (k c) -> p k c", c=width)

        def have(eng, name):
            n = number[name]
            eng.wait_ge(sem(f"w_loaded{n % NSLOT}"), 16 * sum(len(c) for c in chunks[n % NSLOT:n + 1:NSLOT]))

        def load_chunks(eng, first, last):
            for n in range(number[first], number[last] + 1):
                if n >= NSLOT:
                    eng.wait_ge(*released[n - NSLOT])
                s = n % NSLOT
                for part in chunks[n]:
                    k0, nk, at, w, width, src = part
                    dst = wr[:, s, 0:2048 // width * width].rearrange("p (k c) -> p k c", c=width)[
                        :, k0:k0 + nk, at:at + w]
                    eng.dma_start(dst, src).then_inc(sem(f"w_loaded{s}"), 16)

        out_count = [0]

        def store(eng, dst, src):
            out_count[0] += 1
            return eng.dma_start(dst, src).then_inc(sem("stored"), 16)

        def feature_major(set_, lhs, ntile, m=P):
            for n in range(3):
                for k in range(ntile):
                    mm = nc.tensor.matmul(ps[0:m, 3 * set_ + n, 0:NF], lhs(k)[0], lhs(k)[1](n),
                                          start=(k == 0), stop=(k == ntile - 1))
            return mm

        def h_cols(k):
            return lambda n: hT[:, k, NF * n:NF * n + NF]

        def banks(set_, m=P):
            return ps[0:m, 3 * set_:3 * set_ + 3, 0:NF]

        def split3(ap):
            return ap.rearrange("p (n c) -> p n c", n=3)

        nsa = ExitStack()
        qT = sb(nsa, "qT", [P, R, TOK])
        kT = sb(nsa, "kT", [P, 4, TOK])
        vtok = sb(nsa, "vtok", [P, TILES, 256])
        o_acc = sb(nsa, "o_acc", [P, TILES, 512])
        slope = sb(nsa, "slope", [P, H])
        kc = sb(nsa, "kc", [P, 64])
        vc = sb(nsa, "vc", [64, P])
        kcs = sb(nsa, "kcs", [P, DB, NCS])
        vcs = sb(nsa, "vcs", [NCS, DB, P])
        NK = PAST + ST
        zbias = sb(nsa, "zbias", [P, 2, 2, NK])
        zcb = sb(nsa, "zcb", [P, NCS])
        zcol = sb(nsa, "zcol", [P, 64])
        pi, hi, si = (zcol[:, c:c + 1].bitcast(I32) for c in (0, 1, 2))
        t_row, b_row, sl_row, m0, m1, hf = (zcol[:, c:c + 1] for c in range(3, 9))
        bcols = zcol[:, 16:48]
        NB = 4
        pgs = ExitStack()
        NPG = 6
        pages = sb(pgs, "pages", [P, NPG, 512])

        def gather_cmp(pool, n):
            if n >= NPG:
                pool.wait_ge(sem("pT_done"), n - NPG + 1)
            src = a[("cache_k_cmp", "cache_v_cmp")[n // DB]].rearrange("o n (s j) g d -> (o n s) (j g d)", j=4)
            pool.indirect_dma_start(pages[:, n % NPG, :], None, src,
                                    bass.IndirectOffsetOnAxis(ap=idx[:, n % DB:n % DB + 1], axis=0))\
                .then_inc(sem(f"page_loaded{n % NPG}"), 16)


        s1 = ExitStack()
        x_all = sb(s1, "x_all", [P, TILES, D])
        junk1 = sb(s1, "junk1", [P, 2 * (PAST + ST)])
        ktok = x_all[:, :, 0:512]
        zx, zm = junk1[:, 0:PAST + ST], junk1[:, PAST + ST:2 * (PAST + ST)]
        NFT = 9
        with nc.Block() as block:
            @block.tensor
            def _(pe):
                pe.wait_ge(sem("consts"), 4)
                for t in range(TILES):
                    n = rows_of(t)
                    pe.wait_ge(sem("xn_ready"), t + 1)
                    for half in range(2):
                        if t >= 1:
                            pe.wait_ge(sem("hT_ready"), 2 * t + half - 1)
                        for k in range(4):
                            mm = nc.tensor.transpose(ps[:, 6 + half, P * k:P * k + n],
                                                     x_all[0:n, t, P * (4 * half + k):P * (4 * half + k) + P],
                                                     ident[0:n, 0:n])
                        mm.then_inc(sem("xT_done"), 1)
                pe.wait_ge(sem("hT_ready"), 2 * TILES)

                def keys_of(name, c0, width=256, m=P):
                    w = slot(name, width)
                    return lambda k: (w[:, k, c0:c0 + m], h_cols(k))

                def q_of(r):
                    w = slot(f"q{r // 2}")
                    c0 = P * (r % 2)
                    return lambda k: (w[:, k, c0:c0 + P], h_cols(k))

                plan = [(f"q{r // 2}", q_of(r), P) for r in range(R)]
                plan += [("cmp", keys_of("cmp", 0), P), ("cmp", keys_of("cmp", P), P),
                         ("slc", keys_of("slc", 0), P), ("win", keys_of("win", 0), P)]
                for f, (name, lhs, m) in enumerate(plan):
                    have(pe, name)
                    if f >= 2:
                        pe.wait_ge(sem("f_copied"), f - 1)
                    feature_major(f % 2, lhs, KT, m).then_inc(sem("f_done"), 1)
                    released[number[name]] = (sem("f_done"), f + 1)
                for t in range(TILES):
                    n = rows_of(t)
                    if t >= 2:
                        pe.wait_ge(sem("v_copied"), t - 1)
                    for j, name in enumerate(("slc", "win")):
                        for k in range(KT):
                            mm = nc.tensor.matmul(ps[0:n, 6 + t % 2, P * j:P * j + P],
                                                  hT[:, k, P * t:P * t + n], slot(name)[:, k, P:2 * P],
                                                  start=(k == 0), stop=(k == KT - 1))
                    mm.then_inc(sem("v_done"), 1)
                for name in ("slc", "win"):
                    released[number[name]] = (sem("v_done"), TILES)
                have(pe, "ga")
                pe.wait_ge(sem("f_copied"), NFT - 2)
                feature_major(0, keys_of("ga", 0, 48, 48), KT, 48).then_inc(sem("f_done"), 1)
                released[number["ga"]] = (sem("f_done"), NFT)
                pe.wait_ge(sem("f_copied"), NFT - 1)
                pe.wait_ge(sem("v_copied"), TILES)
                for t in range(TILES):
                    n = rows_of(t)
                    if t >= 2:
                        pe.wait_ge(sem("ktok_copied"), t - 1)
                    for j in range(4):
                        mm = nc.tensor.transpose(ps[0:n, 6 + t % 2, P * j:P * j + P],
                                                 kT[:, j, P * t:P * t + n], ident[:, :])
                    mm.then_inc(sem("ktok_done"), 1)
                pe.wait_ge(sem("f_copied"), NFT)
                for t in range(TILES):
                    n = rows_of(t)
                    mm = nc.tensor.transpose(ps[0:n, 3, 24 * t:24 * t + 24],
                                             gaT[0:24, P * t:P * t + n], ident[0:24, 0:24])
                mm.then_inc(sem("gate_done"), 1)

            @block.gpsimd
            def _(pool):
                pool.dma_start(ng_col, a["norm_g"].rearrange("o (k p) -> p (o k)", p=P),
                               allow_slow_non_contiguous=True).then_inc(sem("vectors"), 16)
                pool.dma_start(ab_col, a["gla_alpha_b"].rearrange("o (k p) -> p (o k)", p=P),
                               allow_slow_non_contiguous=True).then_inc(sem("vectors"), 16)
                pool.dma_start(gn_col, a["gla_norm_g"].rearrange("o (k p) -> p (o k)", p=P),
                               allow_slow_non_contiguous=True).then_inc(sem("vectors"), 16)
                for v, name in enumerate(("phi_k_pe", "phi_v_pe")):
                    for par in range(2):
                        pool.dma_start(pe2[HD * par:HD * par + HD, v, :],
                                       a[name][0].rearrange("(s q) d -> q d s", q=2)[par],
                                       allow_slow_non_contiguous=True).then_inc(sem("vectors"), 16)
                pool.dma_start(pt_all, a["page_table"].rearrange("b g -> (b g)").unsqueeze(0)
                               .to_broadcast([P, DB * NPAGES])).then_inc(sem("table"), 16)
                for m in (ident, tri):
                    pool.memset(m[:, :], 0.0 if m is ident else 1.0).then_inc(sem("consts0"), 1)
                pool.wait_ge(sem("consts0"), 2)
                pool.affine_select(out=ident[:, :], in_=ident[:, :], compare_op=ALU.not_equal, fill=1.0,
                                   base=0, pattern=[[-1, P]], channel_multiplier=1).then_inc(sem("consts"), 1)
                pool.affine_select(out=tri[:, :], in_=tri[:, :], compare_op=ALU.is_ge, fill=0.0,
                                   base=0, pattern=[[1, P]], channel_multiplier=-1).then_inc(sem("consts"), 1)
                for h in range(H):
                    pool.memset(slope[:, h:h + 1], 2.0 ** -(h + 1)).then_inc(sem("slopes"), 1)
                pool.wait_ge(sem("slopes"), H)
                for q in range(4):
                    pool.iota(pbase[32 * q:32 * q + 32, :], pattern=[[0, 1]], base=0,
                              channel_multiplier=1).then_inc(sem("pbase"), 1)
                    pool.wait_ge(sem("pbase"), q + 1)
                pool.memset(ssq, 1.0).then_inc(sem("consts"), 1)
                pool.memset(kc[:, :], 0.0).then_inc(sem("consts"), 1)
                link = linker(pool, "pool_link")
                link(nc.gpsimd.iota(pi, pattern=[[0, 1]], base=0, channel_multiplier=1))
                pool.wait_ge(sem("squares"), TILES)
                link(nc.gpsimd.iota(zx[:, 0:PAST].rearrange("p (j c) -> p j c", j=4), pattern=[[-1, 4], [-4, P]],
                                    base=PAST, channel_multiplier=0, allow_small_or_imprecise_dtypes=True))
                link(nc.gpsimd.iota(zx[:, PAST:NK].rearrange("p (b t) -> p b t", t=DS), pattern=[[0, DB], [-1, DS]],
                                    base=0, channel_multiplier=0, allow_small_or_imprecise_dtypes=True))
                link(nc.gpsimd.iota(bcols.rearrange("p (b t) -> p b t", t=DS), pattern=[[1, DB], [0, DS]],
                                    base=0, channel_multiplier=0, allow_small_or_imprecise_dtypes=True))
                link(nc.gpsimd.iota(zcb[:, :], pattern=[[-CS, NCS]], base=PAST - (CB - 1), channel_multiplier=0,
                                    allow_small_or_imprecise_dtypes=True))
                pool.sem_inc(sem("z_iota"), 1)
                pool.wait_ge(sem("idx_ready"), 1)
                for n in range(NPG):
                    gather_cmp(pool, n)

            @block.vector
            def _(dve):
                link = linker(dve, "dve_link")
                dve.wait_ge(sem("squares"), TILES)
                link(nc.vector.tensor_scalar(rstd, ssq, 1.0 / D, EPS, ALU.mult, ALU.add))
                dve.sem_inc(sem("var_ready"), 1)
                dve.wait_ge(sem("sd_ready"), 1)
                nc.vector.reciprocal(rstd, ssq).then_inc(sem("rstd_ready"), 1)
                dve.wait_ge(sem("vectors"), 16 * 7)
                for t in range(TILES):
                    n = rows_of(t)
                    for half in range(2):
                        dve.wait_ge(sem("xT_done"), 2 * t + half + 1)
                        nc.vector.tensor_tensor(
                            hT[:, 4 * half:4 * half + 4, P * t:P * t + n],
                            ps[:, 6 + half, :].rearrange("p (k c) -> p k c", k=4)[:, :, 0:n],
                            ng_col[:, 4 * half:4 * half + 4].unsqueeze(2).to_broadcast([P, 4, n]),
                            ALU.mult).then_inc(sem("hT_ready"), 1)
                dve.wait_ge(sem("table"), 16)
                dve.wait_ge(sem("pbase"), 4)
                for q in range(NPAGES):
                    rr = slice(32 * q, 32 * q + 32)
                    link(nc.vector.tensor_scalar(
                        idx[rr, :], pt_all[rr, :].rearrange("p (b g) -> p b g", g=NPAGES)[:, :, q],
                        32, None, ALU.mult))
                    ins = nc.vector.tensor_tensor(idx[rr, :], idx[rr, :], pbase[rr, :].to_broadcast([32, DB]),
                                                  ALU.add)
                    link(ins)
                dve.sem_inc(sem("idx_ready"), 1)
                dve.wait_ge(sem("z_iota"), 1)
                link(nc.vector.tensor_scalar(hi, pi, 3, None, ALU.bitwise_and))
                link(nc.vector.tensor_copy(t_row, hi))
                link(nc.vector.tensor_scalar(hi, pi, 5, None, ALU.logical_shift_right))
                link(nc.vector.tensor_copy(b_row, hi))
                link(nc.vector.tensor_scalar(hi, pi, 2, 7, ALU.logical_shift_right, ALU.bitwise_and))
                link(nc.vector.tensor_copy(hf, hi))
                link(nc.vector.tensor_scalar(m0, hf, float(R), None, ALU.is_lt))
                link(nc.vector.tensor_scalar(m1, hf, float(R), None, ALU.is_ge))
                link(nc.vector.tensor_scalar(hi, hi, -1, 126, ALU.mult, ALU.add))
                link(nc.vector.tensor_scalar(si, hi, 23, None, ALU.logical_shift_left))
                link(nc.vector.tensor_copy(sl_row, zcol[:, 2:3]))
                link(nc.vector.tensor_scalar(zcb[:, :], zcb[:, :], t_row, sl_row, ALU.add, ALU.mult))
                link(nc.vector.tensor_scalar(zx[:, :], zx[:, :], t_row, None, ALU.add))
                new = slice(PAST, NK)
                for gp in range(2):
                    for br in range(2):
                        zb = zbias[:, gp, br, :]
                        link(nc.vector.tensor_scalar(zb, zx[:, :], sl_row, None, ALU.mult))
                        link(nc.vector.tensor_scalar(zm[:, new], zx[:, new], 0.0, BIG, ALU.is_lt, ALU.mult))
                        link(nc.vector.tensor_tensor(zb[:, new], zb[:, new], zm[:, new], ALU.add))
                        link(nc.vector.tensor_scalar(zm[:, new], bcols, float(-NB * gp), b_row, ALU.add, ALU.not_equal))
                        link(nc.vector.tensor_scalar(zm[:, new], zm[:, new], BIG, None, ALU.mult))
                        link(nc.vector.tensor_tensor(zb[:, new], zb[:, new], zm[:, new], ALU.add))
                        if br == 1:
                            link(nc.vector.tensor_scalar(zm[:, :], zx[:, :], float(WIN), BIG, ALU.is_ge, ALU.mult))
                            link(nc.vector.tensor_tensor(zb, zb, zm[:, :], ALU.add))
                for t in range(TILES):
                    n = rows_of(t)
                    dve.wait_ge(sem("ktok_done"), t + 1)
                    nc.vector.tensor_copy(ktok[0:n, t, :], ps[0:n, 6 + t % 2, :]).then_inc(sem("ktok_copied"), 1)

            @block.scalar
            def _(act):
                act.wait_ge(sem("consts"), 3)
                for t in range(TILES):
                    n = rows_of(t)
                    act.wait_ge(sem(f"x_loaded{t}"), 16)
                    if t >= 1:
                        act.wait_ge(sem("squares"), t)
                    nc.scalar.activation(junk1[0:n, 0:D], x_all[0:n, t, :], ACT.Square,
                                         accum_out=ssq[0:n, t:t + 1]).then_inc(sem("squares"), 1)
                act.wait_ge(sem("var_ready"), 1)
                act.wait_ge(sem("squares"), TILES)
                nc.scalar.activation(ssq, rstd, ACT.Sqrt).then_inc(sem("sd_ready"), 1)
                act.wait_ge(sem("rstd_ready"), 1)
                for t in range(TILES):
                    n = rows_of(t)
                    nc.scalar.activation(x_all[0:n, t, :], x_all[0:n, t, :], ACT.Copy,
                                         scale=rstd[0:n, t:t + 1]).then_inc(sem("xn_ready"), 1)
                for f in range(NFT - 1):
                    act.wait_ge(sem("f_done"), f + 1)
                    dst = qT[:, f, :] if f < R else kT[:, f - R, :]
                    nc.scalar.activation(split3(dst), banks(f % 2), ACT.Copy,
                                         scale=-HD ** -0.5 if f < R else 1.0).then_inc(sem("f_copied"), 1)
                for t in range(TILES):
                    n = rows_of(t)
                    act.wait_ge(sem("v_done"), t + 1)
                    nc.scalar.activation(vtok[0:n, t, :], ps[0:n, 6 + t % 2, 0:256], ACT.Copy)\
                        .then_inc(sem("v_copied"), 1)
                act.wait_ge(sem("f_done"), NFT)
                nc.scalar.activation(split3(gaT[:, :]), banks(0, 48), ACT.Copy).then_inc(sem("f_copied"), 1)
                act.wait_ge(sem("gate_done"), 1)
                nc.scalar.activation(gate[:, 0:PT, :], ps[:, 3, 0:24 * PT].rearrange("p (t c) -> p t c", c=24),
                                     ACT.Sigmoid).then_inc(sem("gate_ready"), 1)
                nc.scalar.activation(gate[0:ST, PT, :], ps[0:ST, 3, 24 * PT:24 * PT + 24],
                                     ACT.Sigmoid).then_inc(sem("gate_ready"), 1)

            @block.sync
            def _(sp):
                for t in range(TILES):
                    src = a["x_prompt"][0, P * t:P * t + P, :] if t < PT else \
                        a["x_sample"].rearrange("b s d -> (b s) d")
                    sp.dma_start(x_all[0:rows_of(t), t, :], src).then_inc(sem(f"x_loaded{t}"), 16)
                load_chunks(sp, "q0", "w1v")
                for src, dst in ((a["cache_k_win"], s_kw), (a["cache_v_win"], s_vw)):
                    store(sp, dst[0, :, 0:WIN - DS].rearrange("b s g d -> b (s g d)"),
                          src[0, :, DS:WIN].rearrange("b s g d -> b (s g d)"))
                sp.wait_ge(sem("v_copied"), TILES)
                for j, (pd, sd) in enumerate(((p_vs, s_vs), (p_vw, s_vw))):
                    t0 = 0 if j == 0 else PT - WIN // P
                    store(sp, pd[0, 0].rearrange("(t p) g d -> p t (g d)", p=P), vtok[:, t0:PT, P * j:P * j + P])
                    if j == 0:
                        store(sp, sd[0].rearrange("b s g d -> (b s) (g d)"), vtok[0:ST, PT, 0:P])
                    else:
                        for b in range(DB):
                            store(sp, sd[0, b, WIN - DS:WIN].rearrange("s g d -> s (g d)"),
                                  vtok[DS * b:DS * b + DS, PT, P:2 * P])
                sp.wait_ge(sem("ktok_copied"), TILES)
                for j, (pd, sd) in enumerate(((p_kc, s_kc), (p_vc, s_vc), (p_ks, s_ks), (p_kw, s_kw))):
                    t0 = 0 if j < 3 else PT - WIN // P
                    store(sp, pd[0, 0].rearrange("(t p) g d -> p t (g d)", p=P), ktok[:, t0:PT, P * j:P * j + P])
                    if j < 3:
                        store(sp, sd[0].rearrange("b s g d -> (b s) (g d)"), ktok[0:ST, PT, P * j:P * j + P])
                    else:
                        for b in range(DB):
                            store(sp, sd[0, b, WIN - DS:WIN].rearrange("s g d -> s (g d)"),
                                  ktok[DS * b:DS * b + DS, PT, P * j:P * j + P])
                sp.wait_ge(sem("gate_ready"), 2)
                for b in range(DB):
                    sp.dma_start(gate_spill[b].rearrange("x t c -> t c x"),
                                 gate[DS * b:DS * b + DS, PT, :].rearrange("t (c x) -> t c x", c=3),
                                 allow_slow_non_contiguous=True).then_inc(sem("gate_spilled"), 16)
                sp.wait_ge(sem("stored"), 16 * out_count[0])
        s1.close()

        s2 = ExitStack()
        cX = sb(s2, "cX", [P, 2, G, NB, 2, P])
        kX = sb(s2, "kX", [P, 2, G, SEQ // 2])
        w2 = sb(s2, "w2", [P, 2, HD])
        hid = sb(s2, "hid", [P, 2, 2 * (64 + DB * NCS)])
        cbias = sb(s2, "cbias", [P, 2])
        NS2, NSH = DB * NCS, NB * NCS
        STEPS = 4
        hid_reads = (8, 12, 20, 24)

        def turn_bank(n, par):
            return (6, 3)[n % 2] + par

        with nc.Block() as block:
            @block.tensor
            def _(pe):
                def turn(st):
                    for n in range(NB * st, NB * st + NB):
                        pe.wait_ge(sem(f"page_loaded{n % NPG}"), 16 * (n // NPG + 1))
                        if n >= 2:
                            for who in ("cX_dve", "cX_act"):
                                pe.wait_ge(sem(who), n - 1)
                        for j in range(4):
                            mm = nc.tensor.transpose(ps[:, turn_bank(n, j % 2), P * (j // 2):P * (j // 2) + P],
                                                     pages[:, n % NPG, P * j:P * j + P], ident[:, :])
                        mm.then_inc(sem("pT_done"), 1)

                def hidden(st):
                    kv, half = divmod(st, 2)
                    for who in ("cX_dve", "cX_act"):
                        pe.wait_ge(sem(who), NB * (st + 1))
                    name = "w1" + "kv"[kv]
                    if half == 0:
                        have(pe, name)
                        for who in ("kX_dve", "kX_act"):
                            pe.wait_ge(sem(who), 4)
                    if st >= 1:
                        pe.wait_ge(sem("hid_read"), hid_reads[st - 1])
                    if st == 2:
                        pe.wait_ge(sem("c2_copied"), 2)
                    w = wr[:, number[name] % NSLOT, :].rearrange("p (s c) -> p s c", c=P)
                    for s in range(16):
                        flags = dict(start=(s == 0), stop=(s == 15))
                        if half == 0:
                            nc.tensor.matmul(ps[:, 5, 511:512], w[:, s, :], pe2[:, kv, s:s + 1], **flags)
                            nc.tensor.matmul(ps[:, 2, 0:G * NCP].rearrange("p (g c) -> p g c", g=G), w[:, s, :],
                                             kX[:, kv, :, s:s + 8 * (NCP - 1) + 1:8], **flags)
                        c0 = s // 2
                        mm = nc.tensor.matmul(ps[:, 0, 0:G * NSH].rearrange("p (b c) -> p b c", b=G * NB), w[:, s, :],
                                              cX[:, half, :, :, s % 2, c0:c0 + 4 * (NCS - 1) + 1:4]
                                              .rearrange("p g b c -> p (g b) c"), **flags)
                    mm.then_inc(sem("hid_done"), 1)
                    released[number[name]] = (sem("hid_done"), st + 1)

                def second(kv):
                    if kv == 0:
                        pe.wait_ge(sem("w2_loaded"), 32)
                    pe.wait_ge(sem("hid_ready"), 6 * (kv + 1))
                    if kv == 0:
                        for g in range(G):
                            nc.tensor.matmul(ps[HD * g:HD * g + HD, 5, 0:NCP], w2[:, 0, :],
                                             hid[:, 0, 64 * g:64 * g + NCP], start=True, stop=True)
                        for g in range(G):
                            mm = nc.tensor.matmul(ps[HD * g:HD * g + HD, 5, 64:64 + NS2], w2[:, 0, :],
                                                  hid[:, 0, 128 + NS2 * g:128 + NS2 * g + NS2],
                                                  start=True, stop=True)
                    else:
                        pe.wait_ge(sem("c2_copied"), 2)
                        for g in range(G):
                            nc.tensor.matmul(ps[0:NCP, 5, HD * g:HD * g + HD],
                                             hid[:, 0, 64 * g:64 * g + NCP], w2[:, 1, :], start=True, stop=True)
                        for b in range(DB):
                            for g in range(G):
                                c0 = 128 + NS2 * g + NCS * b
                                mm = nc.tensor.matmul(
                                    ps[0:NCS, 6 + b // 4, P * (b % 4) + HD * g:P * (b % 4) + HD * g + HD],
                                    hid[:, 0, c0:c0 + NCS], w2[:, 1, :], start=True, stop=True)
                    mm.then_inc(sem("c2_done"), 1)

                turn(0)
                turn(1)
                hidden(0)
                turn(2)
                hidden(1)
                second(0)
                turn(3)
                hidden(2)
                hidden(3)
                second(1)

            @block.gpsimd
            def _(pool):
                for n in range(NPG, 2 * DB):
                    gather_cmp(pool, n)

            def regroup(copy, par, name):
                def prompt():
                    for kv in range(2):
                        for g in range(G):
                            copy(kX[HD * par:HD * par + HD, kv, g, :], kT[HD * g:HD * g + HD, kv, par:SEQ:2])\
                                .then_inc(sem("kX_" + name), 1)

                def batches(eng, st):
                    if st >= 2:
                        eng.wait_ge(sem("hid_done"), st - 1)
                    for n in range(NB * st, NB * st + NB):
                        eng.wait_ge(sem("pT_done"), n + 1)
                        for g in range(G):
                            ins = copy(cX[HD * par:HD * par + HD, st % 2, g, n % NB, :, :],
                                       ps[HD * g:HD * g + HD, turn_bank(n, par), 0:2 * P].rearrange(
                                           "p (j c) -> p j c", c=P))
                        ins.then_inc(sem("cX_" + name), 1)
                return prompt, batches

            @block.vector
            def _(dve):
                link = linker(dve, "dve_link")
                prompt, batches = regroup(nc.vector.tensor_copy, 0, "dve")

                def silu(st):
                    kv, half = divmod(st, 2)
                    dve.wait_ge(sem("hid_read"), hid_reads[st])
                    spans = [(64 * g, NCP) for g in range(G)] if half == 0 else []
                    spans += [(128 + NS2 * g + NSH * half, NSH) for g in range(G)]
                    for c0, n in spans:
                        nc.vector.tensor_tensor(hid[:, 0, c0:c0 + n], hid[:, 0, c0:c0 + n], hid[:, 1, c0:c0 + n],
                                                ALU.mult).then_inc(sem("hid_ready"), 1)

                def bias_of(kv):
                    dve.wait_ge(sem("hid_done"), 2 * kv + 1)
                    nc.vector.tensor_copy(cbias[:, kv:kv + 1], ps[:, 5, 511:512]).then_inc(sem("cbias_ready"), 1)

                batches(dve, 0)
                prompt()
                batches(dve, 1)
                bias_of(0)
                batches(dve, 2)
                silu(0)
                silu(1)
                dve.wait_ge(sem("c2_done"), 1)
                nc.vector.tensor_copy(kc[:, 0:NCP], ps[:, 5, 0:NCP]).then_inc(sem("c2_copied"), 1)
                nc.vector.tensor_copy(kcs[:, :, :].rearrange("p b c -> p (b c)"), ps[:, 5, 64:64 + NS2])\
                    .then_inc(sem("c2_copied"), 1)
                batches(dve, 3)
                bias_of(1)
                silu(2)
                silu(3)
                link(nc.vector.memset(vc[:, :], 0.0))
                dve.wait_ge(sem("c2_done"), 2)
                nc.vector.tensor_copy(vc[0:NCP, :], ps[0:NCP, 5, 0:P]).then_inc(sem("c2_copied"), 1)
                nc.vector.tensor_copy(vcs[:, :, :].rearrange("p (x b) c -> p x (b c)", x=2),
                                      ps[0:NCS, 6:8, :]).then_inc(sem("c2_copied"), 1)

            @block.scalar
            def _(act):
                copy = lambda dst, src: nc.scalar.activation(dst, src, ACT.Copy)
                prompt, batches = regroup(copy, 1, "act")

                def activations(st):
                    kv, half = divmod(st, 2)
                    act.wait_ge(sem("cbias_ready"), kv + 1)
                    act.wait_ge(sem("hid_done"), st + 1)
                    if st == 2:
                        act.wait_ge(sem("c2_done"), 1)
                    spans = [(2, NCP * g, 64 * g, NCP) for g in range(G)] if half == 0 else []
                    spans += [(0, NSH * g, 128 + NS2 * g + NSH * half, NSH) for g in range(G)]
                    for bank, b0, c0, n in spans:
                        for i, func in enumerate((ACT.Identity, ACT.Sigmoid)):
                            nc.scalar.activation(hid[:, i, c0:c0 + n], ps[:, bank, b0:b0 + n], func,
                                                 bias=cbias[:, kv:kv + 1]).then_inc(sem("hid_read"), 1)

                batches(act, 0)
                prompt()
                batches(act, 1)
                activations(0)
                batches(act, 2)
                activations(1)
                batches(act, 3)
                activations(2)
                activations(3)

            @block.sync
            def _(sp):
                for kv in range(2):
                    sp.dma_start(w2[:, kv, :], a[("phi_k_w2", "phi_v_w2")[kv]][0]).then_inc(sem("w2_loaded"), 16)
                load_chunks(sp, "gqk0", "gv1")
        s2.close()
        pgs.close()

        s3 = ExitStack()
        sS = sb(s3, "sS", [P, 2, 1024])
        pP = sb(s3, "pP", [P, 2, 1024])
        pPT = sb(s3, "pPT", [P, 2, 1024])
        bias = sb(s3, "bias", [P, 2, 1024 + 640])
        ndist = sb(s3, "ndist", [P, 1024])
        cdist = sb(s3, "cdist", [P, 2, 512])
        stat = sb(s3, "stat", [P, 256])
        tmp = sb(s3, "tmp", [P, 2, 512])
        cP = pP[:, :, 512:1024]
        mcol = stat[:, 0:16]
        wcol = stat[:, 32:48]

        def lcol(h):
            return stat[:, 64 + 16 * (h % 2):80 + 16 * (h % 2)]

        mcmp = (stat[:, 96:104], stat[:, 48:56])
        lcmp = (stat[:, 104:112], stat[:, 56:64])

        def units():
            return [(h, i, br) for h in range(H) for i in range(PT) for br in range(2)]

        U = units()

        def keys_range(i, br):
            k0 = 0 if br == 0 else max(0, i - WIN // P)
            return k0, i + 1 - k0

        parts, nparts = [], 0
        for h, i, br in U:
            nk = keys_range(i, br)[1]
            cuts = [(0, nk)] if nk <= 4 else [(0, (nk + 1) // 2), ((nk + 1) // 2, nk // 2)]
            parts.append([(nparts + j, c, w) for j, (c, w) in enumerate(cuts)])
            nparts += len(cuts)

        def copied(m):
            return sem(("pT_act", "pT_dve")[m % 2]), m // 2 + 1

        def copy_part(eng, copy, n, which):
            for m, c, w in parts[n]:
                if m % 2 != which:
                    continue
                eng.wait_ge(sem("pT_ready"), m + 1)
                if n >= 2:
                    eng.wait_ge(sem("av_done"), n - 1)
                copy(pPT[:, n % 2, P * c:P * (c + w)], ps[:, 4 + m % 2, 0:P * w])\
                    .then_inc(sem(("pT_act", "pT_dve")[which]), 1)

        with nc.Block() as block:
            @block.tensor
            def _(pe):
                def cmp_scores(i):
                    if i >= 2:
                        pe.wait_ge(sem("cmp_scored"), i - 1)
                    for h in range(H):
                        g, r = h // R, h % R
                        mm = nc.tensor.matmul(ps[:, 2 * (i % 2) + g, 64 * r:64 * r + 64],
                                              qT[HD * g:HD * g + HD, r, P * i:P * i + P],
                                              kc[HD * g:HD * g + HD, :], start=True, stop=True)
                    mm.then_inc(sem("cmp_qk"), 1)

                def cmp_turn(i):
                    pe.wait_ge(sem("cmp_probs"), i + 1)
                    if i >= 1:
                        pe.wait_ge(sem("cmp_pT"), 2 * i)
                    for h in range(H):
                        mm = nc.tensor.transpose(ps[0:64, 4 + h // 4, P * (h % 4):P * (h % 4) + P],
                                                 cP[:, i % 2, 64 * h:64 * h + 64], ident[:, :])
                        if h % 4 == 3:
                            mm.then_inc(sem("cmp_T"), 1)

                def cmp_values(i):
                    pe.wait_ge(sem("cmp_pT"), 2 * i + 2)
                    if i >= 2:
                        pe.wait_ge(sem("cmp_out"), i - 1)
                    for h in range(H):
                        mm = nc.tensor.matmul(ps[:, 6 + i % 2, HD * h:HD * h + HD], pPT[0:64, i % 2, P * h:P * h + P],
                                              vc[:, HD * (h // R):HD * (h // R) + HD], start=True, stop=True)
                    mm.then_inc(sem("cmp_av"), 1)

                cmp_scores(0)
                cmp_scores(1)
                for i in range(PT + 1):
                    if i < PT:
                        cmp_turn(i)
                    if i + 2 < PT:
                        cmp_scores(i + 2)
                    if i >= 1:
                        cmp_values(i - 1)
                pe.wait_ge(sem("cmp_out"), PT)

                def scores(n):
                    h, i, br = U[n]
                    g, r = h // R, h % R
                    k0, nk = keys_range(i, br)
                    if n >= 2:
                        pe.wait_ge(sem("scored"), n - 1)
                    for c in range(0, nk, 4):
                        w = min(4, nk - c) * P
                        mm = nc.tensor.matmul(ps[:, 2 * (n % 2) + c // 4, 0:w],
                                              qT[HD * g:HD * g + HD, r, P * i:P * i + P],
                                              kT[HD * g:HD * g + HD, 2 + br, P * (k0 + c):P * (k0 + c) + w],
                                              start=True, stop=True)
                    mm.then_inc(sem("qk_done"), 1)

                def transposes(n):
                    pe.wait_ge(sem("probs"), n + 1)
                    for m, c, w in parts[n]:
                        if m >= 2:
                            pe.wait_ge(*copied(m - 2))
                        for k in range(w):
                            mm = nc.tensor.transpose(ps[:, 4 + m % 2, P * k:P * k + P],
                                                     pP[:, n % 2, P * (c + k):P * (c + k) + P], ident[:, :])
                        mm.then_inc(sem("pT_ready"), 1)

                def values(n):
                    h, i, br = U[n]
                    g = h // R
                    k0, nk = keys_range(i, br)
                    for m, c, w in parts[n]:
                        pe.wait_ge(*copied(m))
                    if i == 0 and h >= 1:
                        pe.wait_ge(sem("head_out"), 2 * (h - 1) + br + 1)
                    copies = min(2, PT - i)
                    for k in range(nk):
                        v = vtok[:, k0 + k, P * br + HD * g:P * br + HD * g + HD].unsqueeze(1)
                        mm = nc.tensor.matmul(
                            ps[:, 6 + br, HD * i:HD * (i + copies)].rearrange("p (x d) -> p x d", x=copies),
                            pPT[:, n % 2, P * k:P * k + P], v.to_broadcast([P, copies, HD]),
                            start=(k == 0), stop=(k == nk - 1))
                    mm.then_inc(sem("av_done"), 1)

                scores(0)
                scores(1)
                for n in range(len(U) + 1):
                    if n < len(U):
                        transposes(n)
                    if n >= 1:
                        values(n - 1)
                    if n + 2 < len(U):
                        scores(n + 2)

            @block.gpsimd
            def _(pool):
                link = linker(pool, "pool_link")
                pool.wait_ge(sem("slopes"), H)
                for i in range(PT):
                    if i >= 2:
                        pool.wait_ge(sem("cmp_scored"), i - 1)
                    v = cdist[:, i % 2, :].rearrange("p (h c) -> p h c", h=H)
                    link(nc.gpsimd.iota(v, pattern=[[0, H], [-CS, 64]], base=P * i - (CB - 1), channel_multiplier=1,
                                        allow_small_or_imprecise_dtypes=True))
                    link(nc.gpsimd.tensor_tensor(v, v, slope[:, :].unsqueeze(2).to_broadcast([P, H, 64]), ALU.mult))
                    nc.gpsimd.affine_select(out=v, in_=v, compare_op=ALU.is_ge, fill=BIG, base=P * i - (CB - 1),
                                            pattern=[[0, H], [-CS, 64]], channel_multiplier=1)\
                        .then_inc(sem("cbias"), 1)
                link(nc.gpsimd.iota(ndist[:, :], pattern=[[-1, 1024]], base=896, channel_multiplier=1,
                                    allow_small_or_imprecise_dtypes=True))
                for h in range(H):
                    if h >= 2:
                        pool.wait_ge(sem("scored"), 16 * (h - 1))
                    bs, bw = bias[:, h % 2, 0:1024], bias[:, h % 2, 1024:1664]
                    link(nc.gpsimd.tensor_scalar(bs, ndist[:, :], 2.0 ** -(h + 1), None, ALU.mult))
                    link(nc.gpsimd.affine_select(out=bs, in_=bs, compare_op=ALU.is_ge, fill=BIG, base=896,
                                                 pattern=[[-1, 1024]], channel_multiplier=1))
                    link(nc.gpsimd.tensor_copy(bw, bs[:, 384:1024]))
                    nc.gpsimd.affine_select(out=bw[:, 0:P], in_=bw[:, 0:P], compare_op=ALU.is_gt, fill=BIG, base=0,
                                            pattern=[[1, P]], channel_multiplier=-1).then_inc(sem("bias_ready"), 1)

            @block.vector
            def _(dve):
                link = linker(dve, "dve_link")
                v8 = lambda ap: ap.rearrange("p (h c) -> p h c", h=H)
                wide = lambda ap: ap.unsqueeze(2).to_broadcast([P, H, 64])
                def cmp_score(i):
                    dve.wait_ge(sem("cmp_qk"), i + 1)
                    dve.wait_ge(sem("cbias"), i + 1)
                    if i >= 2:
                        dve.wait_ge(sem("cmp_exp"), i - 1)
                    t = sS[:, i % 2, 0:512]
                    nc.vector.tensor_tensor(t.rearrange("p (g c) -> p g c", g=G),
                                            ps[:, 2 * (i % 2):2 * (i % 2) + 2, 0:256],
                                            cdist[:, i % 2, :].rearrange("p (g c) -> p g c", g=G), ALU.add)\
                        .then_inc(sem("cmp_scored"), 1)
                    dve.wait_ge(sem("cmp_scored"), i + 1)
                    m = mcmp[i % 2]
                    if i >= 2:
                        dve.wait_ge(sem("cmp_sub"), i - 1)
                    link(nc.vector.tensor_reduce(m, v8(t), AX, ALU.min))
                    nc.vector.tensor_tensor(v8(sS[:, i % 2, 512:1024]), v8(t), wide(m), ALU.subtract)\
                        .then_inc(sem("cmp_sub"), 1)

                def cmp_weights(i):
                    e = pP[:, i % 2, 0:512]
                    dve.wait_ge(sem("cmp_exp"), i + 1)
                    if P * i < CB - 1:
                        link(nc.vector.scalar_tensor_tensor(out=e, in0=sS[:, i % 2, 0:512], scalar=0.5 * BIG, in1=e,
                                                            op0=ALU.is_lt, op1=ALU.mult))
                    l = lcmp[i % 2]
                    if i >= 2:
                        dve.wait_ge(sem("cmp_probs"), i - 1)
                    link(nc.vector.tensor_reduce(l, v8(e), AX, ALU.add))
                    link(nc.vector.tensor_scalar(l, l, TINY, None, ALU.max))
                    link(nc.vector.reciprocal(l, l))
                    link(nc.vector.tensor_tensor(l, l, gate[:, i, 0:8], ALU.mult))
                    if i >= 2:
                        dve.wait_ge(sem("cmp_T"), 2 * (i - 1))
                    nc.vector.tensor_tensor(v8(cP[:, i % 2, :]), v8(e), wide(l), ALU.mult)\
                        .then_inc(sem("cmp_probs"), 1)

                cmp_score(0)
                for i in range(PT):
                    if i + 1 < PT:
                        cmp_score(i + 1)
                    cmp_weights(i)
                dve.wait_ge(sem("cmp_out"), PT)

                def score(n):
                    h, i, br = U[n]
                    k0, nk = keys_range(i, br)
                    dve.wait_ge(sem("qk_done"), n + 1)
                    dve.wait_ge(sem("bias_ready"), h + 1)
                    if n >= 2:
                        dve.wait_ge(sem("probs"), n - 1)
                    w = nk * P
                    b0 = (1024 if br == 0 else 1664) - w
                    nc.vector.tensor_tensor_reduce(
                        sS[:, n % 2, 0:w], ps[:, 2 * (n % 2):2 * (n % 2) + 2, :].rearrange("p a c -> p (a c)")[:, 0:w],
                        bias[:, h % 2, b0:b0 + w], 1.0, 3e38, ALU.add, ALU.min,
                        mcol[:, 2 * i + br:2 * i + br + 1]).then_inc(sem("scored"), 1)

                def finish(h):
                    dve.wait_ge(sem("probs"), 16 * h + 16)
                    w = wcol.rearrange("p (i b) -> p b i", b=2)
                    link(nc.vector.tensor_scalar(wcol, lcol(h), TINY, None, ALU.max))
                    link(nc.vector.reciprocal(wcol, wcol))
                    link(nc.vector.tensor_tensor(w, w, gate[:, 0:PT, 8 + h:24:8].rearrange("p i b -> p b i"), ALU.mult))
                    for br in range(2):
                        dve.wait_ge(sem("av_done"), 16 * h + 15 + br)
                        nc.vector.tensor_tensor(v8(tmp[:, br, :]), v8(ps[:, 6 + br, :]), wide(w[:, br, :]), ALU.mult)\
                            .then_inc(sem("head_out"), 1)
                    o = o_acc[:, 0:PT, HD * h:HD * h + HD]
                    for br in range(2):
                        dve.wait_ge(sem("head_out"), 2 * h + br + 1)
                        link(nc.vector.tensor_tensor(o, o, v8(tmp[:, br, :]), ALU.add))

                score(0)
                score(1)
                for n in range(len(U) + 1):
                    if n < len(U):
                        copy_part(dve, nc.vector.tensor_copy, n, 1)
                    if n >= 1 and n % 16 == 0:
                        finish(n // 16 - 1)
                    if n + 2 < len(U):
                        score(n + 2)

            @block.scalar
            def _(act):
                def cmp_copies(i):
                    for j in range(2):
                        act.wait_ge(sem("cmp_T"), 2 * i + j + 1)
                        if i >= 2:
                            act.wait_ge(sem("cmp_av"), i - 1)
                        nc.scalar.activation(pPT[0:64, i % 2, 512 * j:512 * j + 512], ps[0:64, 4 + j, :], ACT.Copy)\
                            .then_inc(sem("cmp_pT"), 1)

                for i in range(PT + 1):
                    if i < PT:
                        act.wait_ge(sem("cmp_sub"), i + 1)
                        if i >= 2:
                            act.wait_ge(sem("cmp_probs"), i - 1)
                        nc.scalar.activation(pP[:, i % 2, 0:512], sS[:, i % 2, 512:1024], ACT.Exp, scale=-1.0)\
                            .then_inc(sem("cmp_exp"), 1)
                    if i >= 1:
                        cmp_copies(i - 1)
                    if i >= 2:
                        act.wait_ge(sem("cmp_av"), i - 1)
                        nc.scalar.activation(o_acc[:, i - 2, :], ps[:, 6 + i % 2, :], ACT.Copy)\
                            .then_inc(sem("cmp_out"), 1)
                act.wait_ge(sem("cmp_av"), PT)
                nc.scalar.activation(o_acc[:, PT - 1, :], ps[:, 6 + (PT - 1) % 2, :], ACT.Copy).then_inc(sem("cmp_out"), 1)

                def probs(n):
                    h, i, br = U[n]
                    w = keys_range(i, br)[1] * P
                    act.wait_ge(sem("scored"), n + 1)
                    if n >= 2:
                        act.wait_ge(sem("pT_ready"), parts[n - 2][-1][0] + 1)
                    if h >= 2 and i == 0:
                        act.wait_ge(sem("head_out"), 2 * (h - 1))
                    c = 2 * i + br
                    nc.scalar.activation(pP[:, n % 2, 0:w], sS[:, n % 2, 0:w], ACT.Exp, bias=mcol[:, c:c + 1],
                                         scale=-1.0, accum_out=lcol(h)[:, c:c + 1]).then_inc(sem("probs"), 1)

                copy = lambda dst, src: nc.scalar.activation(dst, src, ACT.Copy)
                probs(0)
                for n in range(len(U)):
                    if n + 1 < len(U):
                        probs(n + 1)
                    copy_part(act, copy, n, 0)

        s3.close()


        s4 = ExitStack()
        Qb = sb(s4, "Qb", [P, DB, 32])
        kp = sb(s4, "kp", [P, 2, 4, 512])
        vp = sb(s4, "vp", [P, 2, 4, 512])
        kpT = sb(s4, "kpT", [P, 4, 512])
        zS = sb(s4, "zS", [P, NK])
        zP = sb(s4, "zP", [P, NK])
        zPT = sb(s4, "zPT", [P, 5, P])
        orow = sb(s4, "orow", [P, 2, HD])
        grow = sb(s4, "grow", [P, 2, 3])
        zmin, zsum, w0, w1 = (zcol[:, c:c + 1] for c in range(9, 13))
        ZU = [(gp, br) for gp in range(2) for br in range(3)]
        PU = [(gp, br) for gp, br in ZU if br < 2]
        with nc.Block() as block:
            @block.tensor
            def _(pe):
                u2 = 0
                pe.wait_ge(sem("Qb_ready"), G * R)
                for u, (gp, br) in enumerate(ZU):
                    nk = NCS if br == 2 else NK
                    if br < 2:
                        pe.wait_ge(sem(f"kp_loaded{u2 % 2}"), 16 * NB * (u2 // 2 + 1))
                        for b in range(NB):
                            c = NB * u2 + b
                            if c >= 2:
                                pe.wait_ge(sem("kpT_copied"), c - 1)
                            for j in range(4):
                                mm = nc.tensor.transpose(ps[:, 4 + c % 2, P * j:P * j + P],
                                                         kp[:, u2 % 2, b, P * j:P * j + P], ident[:, :])
                            mm.then_inc(sem("kpT_done"), 1)
                        pe.wait_ge(sem("kpT_copied"), NB * (u2 + 1))
                    if u >= 1:
                        pe.wait_ge(sem("z_scored"), u)
                    for b in range(NB):
                        rows = slice(32 * b, 32 * b + 32)
                        q = Qb[:, NB * gp + b, :]
                        if br == 2:
                            mm = nc.tensor.matmul(ps[rows, 0, 0:NCS], q, kcs[:, NB * gp + b, :], start=True, stop=True)
                        else:
                            nc.tensor.matmul(ps[rows, 0, 0:PAST], q, kpT[:, b, :], start=True, stop=True)
                            mm = nc.tensor.matmul(ps[rows, 1, 0:ST], q, kT[:, 2 + br, SEQ:TOK], start=True, stop=True)
                    mm.then_inc(sem("z_qk"), 1)
                    pe.wait_ge(sem("z_probs"), u + 1)
                    if u >= 1:
                        pe.wait_ge(sem("zPT_copied"), u)
                    if br == 2:
                        mm = nc.tensor.transpose(ps[0:NCS, 2, 0:P], zP[:, 0:NCS], ident[:, :])
                    else:
                        for j in range(4):
                            nc.tensor.transpose(ps[:, 2, P * j:P * j + P], zP[:, P * j:P * j + P], ident[:, :])
                        mm = nc.tensor.transpose(ps[0:ST, 3, 0:P], zP[:, PAST:NK], ident[:, :])
                    mm.then_inc(sem("zPT_done"), 1)
                    pe.wait_ge(sem("zPT_copied"), u + 1)
                    if u >= 1:
                        pe.wait_ge(sem("z_out"), u)
                    if br < 2:
                        pe.wait_ge(sem(f"vp_loaded{u2 % 2}"), 16 * NB * (u2 // 2 + 1))
                    for b in range(NB):
                        rows = slice(32 * b, 32 * b + 32)
                        if br == 2:
                            mm = nc.tensor.matmul(ps[rows, 6, 0:P], zPT[0:NCS, 0, rows], vcs[:, NB * gp + b, :],
                                                  start=True, stop=True)
                        else:
                            for j in range(4):
                                nc.tensor.matmul(ps[rows, 6, 0:P], zPT[:, j, rows], vp[:, u2 % 2, b, P * j:P * j + P],
                                                 start=(j == 0), stop=False)
                            mm = nc.tensor.matmul(ps[rows, 6, 0:P], zPT[0:ST, 4, rows],
                                                  vtok[0:ST, PT, P * br:P * br + P], start=False, stop=True)
                    mm.then_inc(sem("z_av"), 1)
                    if br < 2:
                        u2 += 1

            @block.gpsimd
            def _(pool):
                link = linker(pool, "pool_link")
                def fetch(n):
                    gp, br = PU[n]
                    for dst, name, slc, win in ((kp, "kp", a["cache_k_slc"], a["cache_k_win"]),
                                                (vp, "vp", a["cache_v_slc"], a["cache_v_win"])):
                        for b in range(NB):
                            B = NB * gp + b
                            if br == 0:
                                ins = pool.indirect_dma_start(
                                    dst[:, n % 2, b, :], None, slc.rearrange("o n (s j) g d -> (o n s) (j g d)", j=4),
                                    bass.IndirectOffsetOnAxis(ap=idx[:, B:B + 1], axis=0))
                            else:
                                ins = pool.dma_start(dst[:, n % 2, b, :],
                                                     win[0, B].rearrange("(p j) g d -> p (j g d)", j=4))
                            ins.then_inc(sem(f"{name}_loaded{n % 2}"), 16)

                fetch(0)
                fetch(1)
                link(nc.gpsimd.memset(Qb[:, :, :], 0.0))
                pool.sem_inc(sem("Qb_zero"), 1)
                for n in range(2, len(PU)):
                    pool.wait_ge(sem("z_av"), ZU.index(PU[n - 2]) + 1)
                    fetch(n)

            @block.vector
            def _(dve):
                link = linker(dve, "dve_link")
                dve.wait_ge(sem("Qb_zero"), 1)
                for r in range(R):
                    for g in range(G):
                        rows = slice(HD * g, HD * g + HD)
                        c0 = DS * R * g + DS * r
                        nc.vector.tensor_copy(Qb[rows, :, c0:c0 + DS],
                                              qT[rows, r, SEQ:TOK].rearrange("p (b t) -> p b t", t=DS))\
                            .then_inc(sem("Qb_ready"), 1)
                link(nc.vector.memset(orow[:, :, :], 0.0))
                dve.wait_ge(sem("grow_loaded"), 16)
                u2 = 0
                for u, (gp, br) in enumerate(ZU):
                    if br < 2:
                        for b in range(NB):
                            c = NB * u2 + b
                            dve.wait_ge(sem("kpT_done"), c + 1)
                            if b == 0 and u >= 1:
                                dve.wait_ge(sem("z_qk"), u)
                            nc.vector.tensor_copy(kpT[:, b, :], ps[:, 4 + c % 2, :]).then_inc(sem("kpT_copied"), 1)
                        u2 += 1
                    nk = NCS if br == 2 else NK
                    dve.wait_ge(sem("z_qk"), u + 1)
                    if u >= 1:
                        dve.wait_ge(sem("z_probs"), u)
                    nc.vector.tensor_tensor_reduce(
                        zS[:, 0:nk], ps[:, 0:2, :].rearrange("p a c -> p (a c)")[:, 0:nk],
                        zcb[:, :] if br == 2 else zbias[:, gp, br, :], 1.0, 3e38, ALU.add, ALU.min, zmin)\
                        .then_inc(sem("z_scored"), 1)
                    dve.wait_ge(sem("zPT_done"), u + 1)
                    if u >= 1:
                        dve.wait_ge(sem("z_av"), u)
                    if br == 2:
                        nc.vector.tensor_copy(zPT[0:NCS, 0, :], ps[0:NCS, 2, 0:P]).then_inc(sem("zPT_copied"), 1)
                    else:
                        link(nc.vector.tensor_copy(zPT[:, 0:4, :].rearrange("p j c -> p (j c)"), ps[:, 2, :]))
                        nc.vector.tensor_copy(zPT[0:ST, 4, :], ps[0:ST, 3, 0:P]).then_inc(sem("zPT_copied"), 1)
                    link(nc.vector.tensor_scalar(w0, zsum, TINY, None, ALU.max))
                    link(nc.vector.reciprocal(w0, w0))
                    gcol = (1, 2, 0)[br]
                    link(nc.vector.tensor_tensor(w0, w0, grow[:, gp, gcol:gcol + 1], ALU.mult))
                    link(nc.vector.tensor_tensor(w1, w0, m1, ALU.mult))
                    link(nc.vector.tensor_tensor(w0, w0, m0, ALU.mult))
                    dve.wait_ge(sem("z_av"), u + 1)
                    link(nc.vector.scalar_tensor_tensor(out=orow[:, gp, :], in0=ps[:, 6, 0:HD], scalar=w0,
                                                        in1=orow[:, gp, :], op0=ALU.mult, op1=ALU.add))
                    nc.vector.scalar_tensor_tensor(out=orow[:, gp, :], in0=ps[:, 6, HD:P], scalar=w1,
                                                   in1=orow[:, gp, :], op0=ALU.mult, op1=ALU.add)\
                        .then_inc(sem("z_out"), 1)
                    dve.wait_ge(sem("z_out"), u + 1)

            @block.scalar
            def _(act):
                for u, (gp, br) in enumerate(ZU):
                    nk = NCS if br == 2 else NK
                    act.wait_ge(sem("z_scored"), u + 1)
                    if u >= 1:
                        act.wait_ge(sem("zPT_done"), u)
                        act.wait_ge(sem("z_out"), u)
                    nc.scalar.activation(zP[:, 0:nk], zS[:, 0:nk], ACT.Exp, bias=zmin, scale=-1.0,
                                         accum_out=zsum).then_inc(sem("z_probs"), 1)

            @block.sync
            def _(sp):
                sp.wait_ge(sem("gate_spilled"), 16 * DB)
                sp.dma_start(grow[:, :, :], gate_spill.rearrange("(q b) x t c -> (b x t) q c", q=2))\
                    .then_inc(sem("grow_loaded"), 16)
                sp.wait_ge(sem("z_out"), len(ZU))
                sp.dma_start(orow_spill.rearrange("(q b) x t d -> (b x t) q d", q=2), orow[:, :, :])\
                    .then_inc(sem("orow_spilled"), 16)
                sp.wait_ge(sem("orow_spilled"), 16)
                for b in range(DB):
                    sp.dma_start(o_acc[DS * b:DS * b + DS, PT, :].rearrange("t (x d) -> t x d", d=HD),
                                 orow_spill[b].rearrange("x t d -> t x d")).then_inc(sem("o_sample"), 16)
                sp.wait_ge(sem("o_sample"), 16 * DB)
                sp.dma_start(o_spill[:, 0:PT, :], o_acc[:, 0:PT, :]).then_inc(sem("o_spilled"), 16)
                sp.dma_start(o_spill[0:ST, PT, :], o_acc[0:ST, PT, :]).then_inc(sem("o_spilled"), 16)
                sp.wait_ge(sem("o_spilled"), 32)
        s4.close()
        nsa.close()

        og = sb(ctx, "og", [P, TILES, GH * DV])
        s5 = ExitStack()
        NCH = SEQ // CH
        raw = sb(s5, "raw", [P, 3, TOK])
        e1 = sb(s5, "e1", [P, TOK])
        bsum = sb(s5, "bsum", [P, TOK])
        eb = sb(s5, "eb", [P, TOK])
        qd = sb(s5, "qd", [P, TOK])
        qi = sb(s5, "qi", [P, SEQ])
        kt = sb(s5, "kt", [P, TOK])
        Wk = sb(s5, "Wk", [P, PT, 4, P])
        W4 = sb(s5, "W4", [P, PT, P])
        vh = sb(s5, "vh", [P, 2, TILES, DV])
        S = sb(s5, "S", [P, 2, DV])
        S0 = sb(s5, "S0", [P, DB, DV])
        reset = sb(s5, "reset", [P, TOK])
        dec = sb(s5, "dec", [P, PT, 5])
        kis = sb(s5, "kis", [P, ST])
        Qm = sb(s5, "Qm", [P, DB, ST])
        bmr = sb(s5, "bmr", [P, DB, ST])
        bmt = sb(s5, "bmt", [ST, DB])
        tris = sb(s5, "tris", [ST, ST])
        ATs = sb(s5, "ATs", [ST, ST])
        aup = sb(s5, "aup", [48, GH * DK])
        AT = e1[:, 0:SEQ]
        k4 = kt[:, 0:SEQ]
        Km = bsum[0:ST, 0:DB * DK]
        ebt = eb[:, 0:SEQ].rearrange("p (t c i) -> p t c i", t=PT, c=4)
        NP_ = 3
        ncore = PT + 1
        with nc.Block() as block:
            @block.tensor
            def _(pe):
                def project(h):
                    if h >= 1:
                        pe.wait_ge(sem("raw_copied"), 3 * h)
                    name = f"gqk{h}"
                    have(pe, name)
                    w = slot(name)
                    for f, lhs in enumerate((lambda k: (w[:, k, 0:P], h_cols(k)), lambda k: (w[:, k, P:2 * P], h_cols(k)))):
                        feature_major(f % 2, lhs, KT).then_inc(sem("g_done"), 1)
                    released[number[name]] = (sem("g_done"), 3 * h + 2)
                    if h == 0:
                        pe.wait_ge(sem("aup_loaded"), 16)
                    pe.wait_ge(sem("raw_copied"), 3 * h + 1)
                    for n in range(3):
                        mm = nc.tensor.matmul(ps[:, n, 0:NF], aup[32:48, DK * h:DK * h + DK],
                                              gaT[32:48, NF * n:NF * n + NF], start=True, stop=True)
                    mm.then_inc(sem("g_done"), 1)
                    have(pe, f"gv{h}")
                    for t in range(TILES):
                        n, c = rows_of(t), TILES * h + t
                        if c >= 2:
                            pe.wait_ge(sem("gv_copied"), c - 1)
                        for k in range(KT):
                            mm = nc.tensor.matmul(ps[0:n, 6 + c % 2, 0:DV], hT[:, k, P * t:P * t + n],
                                                  slot(f"gv{h}")[:, k, :], start=(k == 0), stop=(k == KT - 1))
                        mm.then_inc(sem("gv_done"), 1)
                    released[number[f"gv{h}"]] = (sem("gv_done"), TILES * (h + 1))

                def core(h, last):
                    pe.wait_ge(sem("elem_done"), h + 1)
                    pe.wait_ge(sem("raw_copied"), 3 * min(h + 2, GH))
                    pe.wait_ge(sem("gv_copied"), TILES * min(h + 2, GH))
                    for t in range(PT):
                        for c in range(4):
                            c0 = P * (t % 4) + CH * c
                            mm = nc.tensor.matmul(ps[:, t // 4, c0:c0 + CH], Wk[:, t, c, :],
                                                  qd[:, P * t + CH * c:P * t + CH * c + CH], start=True, stop=True)
                        if t % 4 == 3:
                            mm.then_inc(sem("at_done"), 1)
                    for t in range(PT):
                        mm = nc.tensor.transpose(ps[:, 2 + t // 4, P * (t % 4):P * (t % 4) + P], W4[:, t, :], ident[:, :])
                        if t % 4 == 3:
                            mm.then_inc(sem("w4_done"), 1)
                    for t in range(PT):
                        if t % 4 == 0:
                            pe.wait_ge(sem("k4_copied"), 2 * h + t // 4 + 1)
                            pe.wait_ge(sem("at_copied"), 2 * h + t // 4 + 1)
                        c = PT * h + t
                        if t >= 2:
                            pe.wait_ge(sem("S_ready"), c - 1)
                        nc.tensor.matmul(ps[:, 4 + t % 2, 0:DV], k4[:, P * t:P * t + P], vh[:, h % 2, t, :],
                                         start=True, stop=True).then_inc(sem("u_done"), 1)
                        if t >= 2:
                            pe.wait_ge(sem("go_copied"), ncore * h + t - 1)
                        mm = nc.tensor.matmul(ps[:, 6 + t % 2, 0:DV], AT[:, P * t:P * t + P], vh[:, h % 2, t, :],
                                              start=True, stop=(t == 0))
                        if t >= 1:
                            pe.wait_ge(sem("S_ready"), c)
                            mm = nc.tensor.matmul(ps[:, 6 + t % 2, 0:DV], qi[:, P * t:P * t + P], S[:, t % 2, :],
                                                  start=False, stop=True)
                        mm.then_inc(sem("go_done"), 1)
                    nc.tensor.transpose(ps[0:ST, 2, 0:P], kt[:, SEQ:TOK], ident[:, :])
                    nc.tensor.matmul(ps[0:ST, 0, 0:ST], kis[:, :], qd[:, SEQ:TOK], start=True, stop=True)\
                        .then_inc(sem("sA_done"), 1)
                    pe.wait_ge(sem("sA_ready"), h + 1)
                    pe.wait_ge(sem("S0_loaded"), 16 * (h + 1))
                    pe.wait_ge(sem("go_copied"), ncore * h + PT - 1)
                    vs = vh[0:ST, h % 2, PT, :]
                    nc.tensor.matmul(ps[0:ST, 6, 0:DV], ATs[:, :], vs, start=True, stop=False)
                    for b in range(DB):
                        mm = nc.tensor.matmul(ps[0:ST, 6, 0:DV], Qm[:, b, :], S0[:, b, :], start=False, stop=(b == DB - 1))
                    mm.then_inc(sem("go_done"), 1)
                    pe.wait_ge(sem("S_ready"), PT * (h + 1))
                    for b in range(DB):
                        c = DB * h + b
                        if b >= 2:
                            pe.wait_ge(sem("sS_ready"), c - 1)
                        nc.tensor.matmul(ps[:, 4 + b % 2, 0:DV], Km[:, DK * b:DK * b + DK], vs, start=True, stop=True)\
                            .then_inc(sem("su_done"), 1)
                    pe.wait_ge(sem("sS_ready"), DB * (h + 1))
                    pe.wait_ge(sem("go_copied"), ncore * (h + 1))

                for h in range(GH):
                    project(h)
                    if h >= 1:
                        core(h - 1, False)
                core(GH - 1, True)

            @block.gpsimd
            def _(pool):
                link = linker(pool, "pool_link")
                pool.dma_start(aup[32:48, :], a["gla_alpha_up"][0]).then_inc(sem("aup_loaded"), 16)
                for m in (reset, bmr, bmt, Wk):
                    f = m[tuple([slice(None)] * len(m.shape))]
                    nc.gpsimd.memset(f, 0.0 if m is Wk else 1.0).then_inc(sem("g_ones"), 1)
                nc.gpsimd.tensor_copy(tris[:, :], tri[0:ST, 0:ST]).then_inc(sem("g_ones"), 1)
                nc.gpsimd.memset(dec[:, :, 0:1], 1.0).then_inc(sem("g_ones"), 1)
                pool.wait_ge(sem("g_ones"), 6)
                link(nc.gpsimd.memset(reset[:, 0:SEQ:CH], 0.0))
                link(nc.gpsimd.memset(reset[:, SEQ:TOK:DS], 0.0))
                keep = lambda out, base, pattern, cm: link(nc.gpsimd.affine_select(
                    out=out, in_=out, compare_op=ALU.is_ge, fill=0.0, base=base, pattern=pattern, channel_multiplier=cm))
                keep(bmr[:, :, :], 0, [[-DS, DB], [1, ST]], 0)
                keep(bmr[:, :, :], DS - 1, [[DS, DB], [-1, ST]], 0)
                keep(bmt[:, :], 0, [[-DS, DB]], 1)
                keep(bmt[:, :], DS - 1, [[DS, DB]], -1)
                keep(tris[:, :].rearrange("p (b t) -> p b t", t=DS), 0, [[-DS, DB], [0, DS]], 1)
                pool.sem_inc(sem("g_masks"), 1)

            @block.vector
            def _(dve):
                link = linker(dve, "dve_link")
                chunks_of = lambda ap: ap[:, 0:SEQ].rearrange("p (n i) -> p n i", i=CH)
                seqs_of = lambda ap: ap[:, SEQ:TOK].rearrange("p (b t) -> p b t", t=DS)
                tt = nc.vector.tensor_tensor

                def elementwise(h):
                    if h >= 1:
                        dve.wait_ge(sem("su_done"), DB * h)
                    dve.wait_ge(sem("raw_copied"), 3 * (h + 1))
                    q, k, z = raw[:, 0, :], raw[:, 1, :], raw[:, 2, :]
                    nc.vector.scalar_tensor_tensor(out=e1[:, :], in0=z, scalar=-1.0, in1=z, op0=ALU.mult, op1=ALU.min)\
                        .then_inc(sem("to_act"), 1)
                    dve.wait_ge(sem("from_act"), 4 * h + 1)
                    link(nc.vector.scalar_tensor_tensor(out=eb[:, :], in0=z, scalar=0.0, in1=e1[:, :],
                                                        op0=ALU.min, op1=ALU.subtract))
                    nc.vector.tensor_tensor_scan(bsum[:, :], reset[:, :], eb[:, :], 0.0, ALU.mult, ALU.add)\
                        .then_inc(sem("to_act"), 1)
                    dve.wait_ge(sem("to_act"), 3 * h + 2)
                    dve.wait_ge(sem("from_act"), 4 * h + 3)
                    link(tt(qd[:, :], q, eb[:, :], ALU.mult))
                    link(tt(diag(),
                            k[:, 0:SEQ].rearrange("p (t c i) -> p t c i", t=PT, c=4),
                            e1[:, 0:SEQ].rearrange("p (t c i) -> p t c i", t=PT, c=4), ALU.mult))
                    link(tt(kis[:, :], k[:, SEQ:TOK], e1[:, SEQ:TOK], ALU.mult))
                    link(tt(chunks_of(e1), chunks_of(bsum)[:, :, CH - 1:CH].to_broadcast([P, NCH, CH]), chunks_of(bsum),
                            ALU.subtract))
                    tt(seqs_of(e1), seqs_of(bsum)[:, :, DS - 1:DS].to_broadcast([P, DB, DS]), seqs_of(bsum),
                       ALU.subtract).then_inc(sem("to_act"), 1)
                    dve.wait_ge(sem("from_act"), 4 * h + 4)
                    link(tt(kt[:, :], k, e1[:, :], ALU.mult))
                    kc4 = kt[:, 0:SEQ].rearrange("p (t c i) -> p t c i", t=PT, c=4)
                    for c in range(1, 5):
                        dst = Wk[:, :, c, :] if c < 4 else W4[:, :, :]
                        if c > 1:
                            w = CH * (c - 1)
                            link(tt(dst[:, :, 0:w], Wk[:, :, c - 1, 0:w],
                                    ebt[:, :, c - 1, CH - 1:CH].to_broadcast([P, PT, w]), ALU.mult))
                        link(nc.vector.tensor_copy(dst[:, :, CH * (c - 1):CH * c], kc4[:, :, c - 1, :]))
                        link(tt(dec[:, :, c:c + 1], dec[:, :, c - 1:c], ebt[:, :, c - 1, CH - 1:CH], ALU.mult))
                    link(tt(qi[:, :].rearrange("p (t c i) -> p t c i", t=PT, c=4),
                            qd[:, 0:SEQ].rearrange("p (t c i) -> p t c i", t=PT, c=4),
                            dec[:, :, 0:4].unsqueeze(3).to_broadcast([P, PT, 4, CH]), ALU.mult))
                    tt(Qm[:, :, :], qd[:, SEQ:TOK].unsqueeze(1).to_broadcast([P, DB, ST]), bmr[:, :, :], ALU.mult)\
                        .then_inc(sem("elem_done"), 1)
                    dve.wait_ge(sem("elem_done"), h + 1)

                def diag():
                    v = Wk[:, :, :, :].rearrange("p t c i -> p t (c i)")
                    return bass.AP(v.tensor, v.offset, [v.ap[0], [4 * P, PT], [P + CH, 4], [1, CH]])

                def core(h):
                    for j in range(2):
                        dve.wait_ge(sem("at_done"), 2 * h + j + 1)
                        tt(AT[:, 512 * j:512 * j + 512].rearrange("p (t i) -> p t i", t=4),
                           ps[:, j, :].rearrange("p (t i) -> p t i", t=4),
                           tri[:, :].unsqueeze(1).to_broadcast([P, 4, P]), ALU.mult).then_inc(sem("at_copied"), 1)
                    for t in range(PT):
                        c = PT * h + t
                        dve.wait_ge(sem("u_done"), c + 1)
                        dst, u = S[:, (t + 1) % 2, :], ps[:, 4 + t % 2, 0:DV]
                        if t >= 1:
                            dve.wait_ge(sem("go_done"), ncore * h + t)
                            dve.wait_ge(sem("S_ready"), c)
                            ins = nc.vector.scalar_tensor_tensor(out=dst, in0=S[:, t % 2, :], scalar=dec[:, t, 4:5],
                                                                 in1=u, op0=ALU.mult, op1=ALU.add)
                        else:
                            ins = nc.vector.tensor_copy(dst, u)
                        ins.then_inc(sem("S_ready"), 1)
                        if t == 0 and h >= 1:
                            dve.wait_ge(sem("pgla_stored"), 16 * h)
                    dve.wait_ge(sem("sA_done"), h + 1)
                    if h == 0:
                        dve.wait_ge(sem("g_masks"), 1)
                    link(tt(Km.rearrange("p (b c) -> p b c", b=DB), ps[0:ST, 2, 0:P].unsqueeze(1).to_broadcast([ST, DB, P]),
                            bmt[:, :].unsqueeze(2).to_broadcast([ST, DB, P]), ALU.mult))
                    tt(ATs[:, :], ps[0:ST, 0, 0:ST], tris[:, :], ALU.mult).then_inc(sem("sA_ready"), 1)
                    dve.wait_ge(sem("go_done"), ncore * (h + 1))
                    for b in range(DB):
                        dve.wait_ge(sem("su_done"), DB * h + b + 1)
                        nc.vector.scalar_tensor_tensor(out=S0[:, b, :], in0=S0[:, b, :],
                                                       scalar=eb[:, SEQ + DS * b + DS - 1:SEQ + DS * b + DS],
                                                       in1=ps[:, 4 + b % 2, 0:DV], op0=ALU.mult, op1=ALU.add)\
                            .then_inc(sem("sS_ready"), 1)

                dve.wait_ge(sem("g_masks"), 1)
                for h in range(GH):
                    if h >= 1:
                        core(h - 1)
                    elementwise(h)
                core(GH - 1)

            @block.scalar
            def _(act):
                act.wait_ge(sem("vectors"), 16 * 7)

                def project(h):
                    if h >= 1:
                        act.wait_ge(sem("elem_done"), h)
                    for f in range(3):
                        act.wait_ge(sem("g_done"), 3 * h + f + 1)
                        if f < 2:
                            ins = nc.scalar.activation(split3(raw[:, f, :]), banks(f % 2), ACT.Copy,
                                                       scale=DK ** -0.5 if f == 0 else 1.0)
                        else:
                            ins = nc.scalar.activation(split3(raw[:, f, :]), banks(0), ACT.Identity,
                                                       bias=ab_col[:, h:h + 1])
                        ins.then_inc(sem("raw_copied"), 1)
                    for t in range(TILES):
                        n, c = rows_of(t), TILES * h + t
                        act.wait_ge(sem("gv_done"), c + 1)
                        nc.scalar.activation(vh[0:n, h % 2, t, :], ps[0:n, 6 + c % 2, 0:DV], ACT.Copy)\
                            .then_inc(sem("gv_copied"), 1)

                def elementwise(h):
                    act.wait_ge(sem("to_act"), 3 * h + 1)
                    nc.scalar.activation(e1[:, :], e1[:, :], ACT.Exp).then_inc(sem("act_link"), 1)
                    act.wait_ge(sem("act_link"), h + 1)
                    nc.scalar.activation(e1[:, :], e1[:, :], ACT.Ln, bias=1.0).then_inc(sem("from_act"), 1)
                    act.wait_ge(sem("to_act"), 3 * h + 2)
                    nc.scalar.activation(eb[:, :], bsum[:, :], ACT.Exp, scale=1.0 / TAU).then_inc(sem("from_act"), 1)
                    nc.scalar.activation(e1[:, :], bsum[:, :], ACT.Exp, scale=-1.0 / TAU).then_inc(sem("from_act"), 1)
                    act.wait_ge(sem("to_act"), 3 * h + 3)
                    nc.scalar.activation(e1[:, :], e1[:, :], ACT.Exp, scale=1.0 / TAU).then_inc(sem("from_act"), 1)

                def core(h):
                    for j in range(2):
                        act.wait_ge(sem("w4_done"), 2 * h + j + 1)
                        nc.scalar.activation(k4[:, 512 * j:512 * j + 512], ps[:, 2 + j, :], ACT.Copy)\
                            .then_inc(sem("k4_copied"), 1)
                    for t in range(TILES):
                        n = rows_of(t)
                        act.wait_ge(sem("go_done"), ncore * h + t + 1)
                        nc.scalar.activation(og[0:n, t, DV * h:DV * h + DV], ps[0:n, 6 + t % 2, 0:DV], ACT.Copy)\
                            .then_inc(sem("go_copied"), 1)

                for h in range(GH):
                    project(h)
                    if h >= 1:
                        core(h - 1)
                    elementwise(h)
                core(GH - 1)

            @block.sync
            def _(sp):
                sp.dma_start(S0[:, :, :], a["state_gla"][0, :, 0].rearrange("b k v -> k b v")).then_inc(sem("S0_loaded"), 16)
                for h in range(GH):
                    if h == 0:
                        load_chunks(sp, "gqk2", "gqk2")
                        load_chunks(sp, "gv2", "gv2")
                    if h == 1:
                        load_chunks(sp, "gqk3", "gv3")
                    sp.wait_ge(sem("S_ready"), PT * (h + 1))
                    sp.dma_start(p_gla[0, 0, h], S[:, 0, :]).then_inc(sem("pgla_stored"), 16)
                    sp.wait_ge(sem("sS_ready"), DB * (h + 1))
                    sp.dma_start(s_gla[0, :, h].rearrange("b k v -> k b v"), S0[:, :, :]).then_inc(sem("sgla_stored"), 16)
                    sp.wait_ge(sem("sgla_stored"), 16 * (h + 1))
                    if h + 1 < GH:
                        sp.dma_start(S0[:, :, :], a["state_gla"][0, :, h + 1].rearrange("b k v -> k b v"))\
                            .then_inc(sem("S0_loaded"), 16)
                    if h == 1:
                        load_chunks(sp, "za0", "za1")
                load_chunks(sp, "zb0", "zb1")
                sp.wait_ge(sem("pgla_stored"), 16 * GH)
        s5.close()

        oT = sb(ctx, "oT", [P, 4, TOK])
        ogT = sb(ctx, "ogT", [P, KT, TOK])
        s6 = ExitStack()
        oN = sb(s6, "oN", [P, TILES, 512])
        zz = sb(s6, "zz", [P, 2, TOK])
        zg = sb(s6, "zg", [P, 2, TOK])
        junk = zg[:, 0, 0:DV]
        gss = sb(s6, "gss", [P, TILES * GH])
        grs = sb(s6, "grs", [P, TILES * GH])
        ogv = og[:, :, :].rearrange("p t (h v) -> p (t h) v", h=GH)
        NZ = 12
        with nc.Block() as block:
            @block.tensor
            def _(pe):
                def gates(f):
                    name = f"za{f // 2}" if f < 4 else f"zb{(f - 4) // 2}"
                    have(pe, name)
                    if f >= 2:
                        pe.wait_ge(sem("z_copied"), 2 * (f - 1))
                    w = slot(name)
                    feature_major(f % 2, lambda k: (w[:, k, P * (f % 2):P * (f % 2) + P], h_cols(k)), KT)\
                        .then_inc(sem("z_done"), 1)
                    released[number[name]] = (sem("z_done"), f + 1)

                def turn(f):
                    src = oN[:, :, P * f:P * f + P] if f < 4 else og[:, :, P * (f - 4):P * (f - 4) + P]
                    if f == 0:
                        pe.wait_ge(sem("oN_loaded"), 32)
                    if f == 4:
                        pe.wait_ge(sem("og_normed"), 2)
                    for j in range(3):
                        last = 3 * f + (0, -1, 1)[j]
                        if last > 0:
                            pe.wait_ge(sem("oT_copied"), last)
                        for t in range(4 * j, min(4 * j + 4, TILES)):
                            n = rows_of(t)
                            mm = nc.tensor.transpose(ps[:, 6 + j % 2, P * (t % 4):P * (t % 4) + n], src[0:n, t, :],
                                                     ident[0:n, 0:n])
                        mm.then_inc(sem("oT_done"), 1)

                for f in range(NZ):
                    gates(f)
                    if f >= 1:
                        turn(f - 1)
                turn(NZ - 1)

            @block.vector
            def _(dve):
                link = linker(dve, "dve_link")
                dve.wait_ge(sem("g_squares"), GH * TILES)
                link(nc.vector.tensor_scalar(grs[:, :], gss[:, :], 1.0 / DV, EPS, ALU.mult, ALU.add))
                dve.sem_inc(sem("g_var"), 1)
                dve.wait_ge(sem("g_sd"), 1)
                link(nc.vector.reciprocal(grs[:, :], gss[:, :]))
                NG = GH * PT
                nc.vector.tensor_tensor(ogv[:, 0:NG, :], ogv[:, 0:NG, :],
                                        grs[:, 0:NG].unsqueeze(2).to_broadcast([P, NG, DV]), ALU.mult)\
                    .then_inc(sem("og_normed"), 1)
                nc.vector.tensor_tensor(ogv[0:ST, NG:, :], ogv[0:ST, NG:, :],
                                        grs[0:ST, NG:].unsqueeze(2).to_broadcast([ST, GH, DV]), ALU.mult)\
                    .then_inc(sem("og_normed"), 1)
                for f in range(NZ):
                    dve.wait_ge(sem("z_copied"), 2 * (f + 1))
                    z = zz[:, f % 2, :]
                    link(nc.vector.tensor_tensor(z, z, zg[:, f % 2, :], ALU.mult))
                    for j in range(3):
                        dve.wait_ge(sem("oT_done"), 3 * f + j + 1)
                        w = min(512, TOK - 512 * j)
                        c = slice(512 * j, 512 * j + w)
                        src = ps[:, 6 + j % 2, 0:w]
                        if f < 4:
                            ins = nc.vector.tensor_tensor(oT[:, f, c], src, z[:, c], ALU.mult)
                        else:
                            ins = nc.vector.scalar_tensor_tensor(out=ogT[:, f - 4, c], in0=src,
                                                                 scalar=gn_col[:, f % 2:f % 2 + 1], in1=z[:, c],
                                                                 op0=ALU.mult, op1=ALU.mult)
                        ins.then_inc(sem("oT_copied"), 1)

            @block.gpsimd
            def _(pool):
                pool.memset(gss[:, :], 1.0).then_inc(sem("gss_ones"), 1)

            @block.scalar
            def _(act):
                act.wait_ge(sem("gss_ones"), 1)
                for t in range(TILES):
                    n = rows_of(t)
                    for h in range(GH):
                        c = GH * t + h
                        if c >= 1:
                            act.wait_ge(sem("g_squares"), c)
                        nc.scalar.activation(junk[0:n, :], og[0:n, t, DV * h:DV * h + DV], ACT.Square,
                                             accum_out=gss[0:n, c:c + 1]).then_inc(sem("g_squares"), 1)
                act.wait_ge(sem("g_var"), 1)
                act.wait_ge(sem("g_squares"), GH * TILES)
                nc.scalar.activation(gss[:, :], grs[:, :], ACT.Sqrt).then_inc(sem("g_sd"), 1)
                for f in range(NZ):
                    act.wait_ge(sem("z_done"), f + 1)
                    if f >= 2:
                        act.wait_ge(sem("oT_copied"), 3 * (f - 1))
                    nc.scalar.activation(split3(zz[:, f % 2, :]), banks(f % 2), ACT.Copy).then_inc(sem("z_copied"), 1)
                    nc.scalar.activation(split3(zg[:, f % 2, :]), banks(f % 2), ACT.Sigmoid).then_inc(sem("z_copied"), 1)

            @block.sync
            def _(sp):
                sp.dma_start(oN[:, 0:PT, :], o_spill[:, 0:PT, :]).then_inc(sem("oN_loaded"), 16)
                sp.dma_start(oN[0:ST, PT, :], o_spill[0:ST, PT, :]).then_inc(sem("oN_loaded"), 16)
                load_chunks(sp, "zb2", "wa0")
        s6.close()

        mixT = og[:, :, :].rearrange("p t c -> p (t c)")[:, 0:KT * TOK].rearrange("p (k c) -> p k c", k=KT)
        s7 = ExitStack()
        sg = sb(s7, "sg", [P, 4, TOK])
        ta = sb(s7, "ta", [P, 2, TOK])
        tb = sb(s7, "tb", [P, TOK])
        kinds = ("ma", "wa", "mb", "wb")
        steps = [(j, kind, s) for j in range(4) for kind in kinds for s in range(2)]
        with nc.Block() as block:
            def drained(n):
                j, kind, s = steps[n]
                who = "m_gated" if kind[0] == "m" else "m_merged"
                return sem(who), sum(1 for q in steps[:n + 1] if q[1][0] == kind[0])

            @block.tensor
            def _(pe):
                for n, (j, kind, s) in enumerate(steps):
                    name = f"{kind}{j}"
                    have(pe, name)
                    if n >= 2:
                        pe.wait_ge(*drained(n - 2))
                    w = slot(name)
                    if kind == "wa":
                        rhs = lambda k: (lambda i: oT[:, k, NF * i:NF * i + NF])
                    elif kind == "wb":
                        rhs = lambda k: (lambda i: ogT[:, k, NF * i:NF * i + NF])
                    else:
                        rhs = h_cols
                    feature_major(n % 2, lambda k: (w[:, k, P * s:P * s + P], rhs(k)), 4 if kind == "wa" else KT)\
                        .then_inc(sem("m_done"), 1)
                    released[number[name]] = (sem("m_done"), n + 1)

            @block.scalar
            def _(act):
                for n, (j, kind, s) in enumerate(steps):
                    if kind[0] != "m":
                        continue
                    act.wait_ge(sem("m_done"), n + 1)
                    i = s if kind == "ma" else 2 + s
                    if j >= 1:
                        act.wait_ge(*drained(steps.index((j - 1, "w" + kind[1], s))))
                    nc.scalar.activation(split3(sg[:, i, :]), banks(n % 2), ACT.Sigmoid).then_inc(sem("m_gated"), 1)

            @block.vector
            def _(dve):
                link = linker(dve, "dve_link")
                for n, (j, kind, s) in enumerate(steps):
                    if kind[0] != "w":
                        continue
                    dve.wait_ge(sem("m_done"), n + 1)
                    i = s if kind == "wa" else 2 + s
                    dve.wait_ge(*drained(steps.index((j, "m" + kind[1], s))))
                    dst = ta[:, s, :] if kind == "wa" else tb[:, :]
                    nc.vector.tensor_tensor(split3(dst), banks(n % 2), split3(sg[:, i, :]), ALU.mult)\
                        .then_inc(sem("m_merged"), 1)
                    if kind == "wb":
                        dve.wait_ge(*drained(n))
                        link(nc.vector.tensor_tensor(mixT[:, 2 * j + s, :], ta[:, s, :], tb[:, :], ALU.add))

            @block.sync
            def _(sp):
                load_chunks(sp, "mb0", "wo3")
        s7.close()

        s8 = ExitStack()
        xr = sb(s8, "xr", [P, 3, D])
        yy = sb(s8, "yy", [P, 3, D])
        jk = sb(s8, "jk", [P, D])
        fg = sb(s8, "fg", [P, D])
        fst = sb(s8, "fst", [P, 2 * TILES])
        with nc.Block() as block:
            @block.tensor
            def _(pe):
                for t in range(TILES):
                    n = rows_of(t)
                    if t >= 4:
                        pe.wait_ge(sem("y_added"), t - 3)
                    for j in range(4):
                        have(pe, f"wo{j}")
                        for k in range(KT):
                            mm = nc.tensor.matmul(ps[0:n, 2 * (t % 4) + j // 2, 256 * (j % 2):256 * (j % 2) + 256],
                                                  mixT[:, k, P * t:P * t + n], slot(f"wo{j}")[:, k, :],
                                                  start=(k == 0), stop=(k == KT - 1))
                    mm.then_inc(sem("y_done"), 1)

            @block.vector
            def _(dve):
                link = linker(dve, "dve_link")
                dve.wait_ge(sem("fg_loaded"), 16)
                for t in range(TILES):
                    n = rows_of(t)
                    dve.wait_ge(sem("y_done"), t + 1)
                    dve.wait_ge(sem(f"xr_loaded{t % 3}"), 16 * (t // 3 + 1))
                    if t >= 3:
                        dve.wait_ge(sem(f"y_stored{t % 3}"), 16 * (t // 3))
                    y = yy[0:n, t % 3, :]
                    nc.vector.tensor_tensor(y, ps[0:n, 2 * (t % 4):2 * (t % 4) + 2, :].rearrange("p a c -> p (a c)"),
                                            xr[0:n, t % 3, :], ALU.add).then_inc(sem("y_added"), 1)
                    ss, r = fst[0:n, 2 * t:2 * t + 1], fst[0:n, 2 * t + 1:2 * t + 2]
                    dve.wait_ge(sem("y_squared"), t + 1)
                    nc.vector.tensor_scalar(r, ss, 1.0 / D, EPS, ALU.mult, ALU.add).then_inc(sem("y_var"), 1)
                    dve.wait_ge(sem("y_sd"), t + 1)
                    link(nc.vector.reciprocal(r, ss))
                    nc.vector.scalar_tensor_tensor(out=y, in0=y, scalar=r, in1=fg[0:n, :], op0=ALU.mult, op1=ALU.mult)\
                        .then_inc(sem("y_ready"), 1)

            @block.scalar
            def _(act):
                for t in range(TILES):
                    n = rows_of(t)
                    ss, r = fst[0:n, 2 * t:2 * t + 1], fst[0:n, 2 * t + 1:2 * t + 2]
                    act.wait_ge(sem("y_added"), t + 1)
                    if t >= 1:
                        act.wait_ge(sem("y_squared"), t)
                    nc.scalar.activation(jk[0:n, :], yy[0:n, t % 3, :], ACT.Square, accum_out=ss)\
                        .then_inc(sem("y_squared"), 1)
                    act.wait_ge(sem("y_var"), t + 1)
                    nc.scalar.activation(ss, r, ACT.Sqrt).then_inc(sem("y_sd"), 1)

            @block.sync
            def _(sp):
                sp.dma_start(fg[:, :], a["final_norm_g"].unsqueeze(0).to_broadcast([P, D])).then_inc(sem("fg_loaded"), 16)

                def load_x(t):
                    src = a["x_prompt"][0, P * t:P * t + P, :] if t < PT else \
                        a["x_sample"].rearrange("b s d -> (b s) d")
                    sp.dma_start(xr[0:rows_of(t), t % 3, :], src).then_inc(sem(f"xr_loaded{t % 3}"), 16)

                for t in range(3):
                    load_x(t)
                for t in range(TILES):
                    if t + 3 < TILES:
                        sp.wait_ge(sem("y_added"), t + 1)
                        load_x(t + 3)
                    sp.wait_ge(sem("y_ready"), t + 1)
                    dst = y_p[0, P * t:P * t + P, :] if t < PT else y_s.rearrange("b s d -> (b s) d")
                    sp.dma_start(dst, yy[0:rows_of(t), t % 3, :]).then_inc(sem(f"y_stored{t % 3}"), 16)
                for s in range(3):
                    sp.wait_ge(sem(f"y_stored{s}"), 16 * 3)
                sp.wait_ge(sem("stored"), 16 * out_count[0])
                sp.wait_ge(sem("sgla_stored"), 16 * GH)
        s8.close()


_INS = ["x_prompt", "x_sample", "cache_k_cmp", "cache_v_cmp", "cache_k_slc", "cache_v_slc", "cache_k_win",
        "cache_v_win", "state_gla", "page_table", "norm_g", "w_in", "phi_k_pe", "phi_k_w1", "phi_k_w2",
        "phi_v_pe", "phi_v_w1", "phi_v_w2", "gla_alpha_up", "gla_alpha_b", "gla_norm_g", "w_branch_a",
        "w_branch_b", "w_out", "final_norm_g"]
_OUTS = ([(1, SEQ, D), (DB, DS, D)] + [(1, 1, SEQ, G, HD)] * 4 + [(1, 1, WIN, G, HD)] * 2 + [(1, 1, GH, DK, DV)]
         + [(1, DB, DS, G, HD)] * 4 + [(1, DB, WIN, G, HD)] * 2 + [(1, DB, GH, DK, DV)])


def kernel(**inputs):
    import numpy as _np
    import concourse.bacc as _bacc
    from concourse import mybir as _mybir
    from concourse.bass_utils import run_bass_kernel_spmd as _run

    nc = _bacc.Bacc("TRN2", target_bir_lowering=False, num_devices=1)
    arrays, args = {}, {}
    for name in _INS:
        x = _np.ascontiguousarray(inputs[name])
        arrays[f"in_{name}"] = x
        args[name] = nc.dram_tensor(f"in_{name}", x.shape, _mybir.dt.from_np(x.dtype), kind="ExternalInput").ap()
    outs = [nc.dram_tensor(f"out_{i}", shape, F32, kind="ExternalOutput").ap() for i, shape in enumerate(_OUTS)]
    hybrid_step(nc, args, outs)
    r = _run(nc, [arrays], core_ids=[0])
    return tuple(r.results[0][f"out_{i}"] for i in range(len(_OUTS)))
```

```python
from contextlib import ExitStack

import concourse.bass as bass
from concourse import mybir

F32 = mybir.dt.float32
I32 = mybir.dt.int32
ALU = mybir.AluOpType
ACT = mybir.ActivationFunctionType
AX = mybir.AxisListType.X

P = 128
D = 1024
KT = D // P
SEQ = 1024
PT = SEQ // P
DB, DS = 8, 4
ST = DB * DS
TILES = PT + 1
TOK = SEQ + ST
NF = TOK // 3
PAST, PAGE, NPAGES, NPOOL = 512, 128, 4, 40
H, G, R, HD = 8, 2, 4, 64
CB, CS = 32, 16
NCP = (SEQ - CB) // CS + 1
NCS = (PAST + DS - CB) // CS + 1
WIN = 512
GH, DK, DV = 4, 128, 256
RANK, TAU = 16, 16.0
CH = 32
EPS, BIG, TINY = 1e-6, 1e30, 1e-30
NSLOT = 4
C_Q, C_KV, C_GATE, C_ZA = 0, 512, 1280, 1304
C_QG, C_KG, C_VG, C_AL, C_ZB, C_MRG = 1816, 2328, 2840, 3864, 3880, 4904


def rows_of(t):
    return P if t < PT else ST


def hybrid_step(nc, a, outs):
    (y_p, y_s, p_kc, p_vc, p_ks, p_vs, p_kw, p_vw, p_gla,
     s_kc, s_vc, s_ks, s_vs, s_kw, s_vw, s_gla) = outs
    w_in = a["w_in"][0]
    ctx = ExitStack()
    sem_names = {}

    def sem(name):
        if name not in sem_names:
            sem_names[name] = ctx.enter_context(nc.semaphore(name))
        return sem_names[name]

    def sb(stack, name, shape, dt=F32):
        return stack.enter_context(nc.sbuf_tensor(name, shape, dt))

    with ctx:
        hT = sb(ctx, "hT", [P, KT, TOK])
        wr = sb(ctx, "wr", [P, NSLOT, 2048])
        gaT = sb(ctx, "gaT", [48, TOK])
        gate = sb(ctx, "gate", [P, TILES, 24])
        ident = sb(ctx, "ident", [P, P])
        tri = sb(ctx, "tri", [P, P])
        small = sb(ctx, "small", [P, 256])
        idx = sb(ctx, "idx", [P, DB], I32)
        ps = ctx.enter_context(nc.psum_tensor("ps", [P, 8, 512], F32))

        o_spill = nc.dram_tensor("o_spill", [P, PT, 512], F32, kind="Internal").ap()
        gate_spill = nc.dram_tensor("gate_spill", [DB, H, DS, 3], F32, kind="Internal").ap()
        orow_spill = nc.dram_tensor("orow_spill", [DB, H, DS, HD], F32, kind="Internal").ap()

        ng_col = small[:, 0:8]
        ab_col = small[:, 8:12]
        gn_col = small[:, 12:14]
        ssq = small[:, 16:25]
        rstd = small[:, 32:41]
        pe2 = small[:, 64:96].rearrange("p (v s) -> p v s", v=2)
        pt_all = small[:, 128:160].bitcast(I32)
        pbase = small[:, 160:161].bitcast(I32)

        link_count = {}

        def linker(eng, name):
            s = sem(name)

            def link(ins):
                link_count[name] = link_count.get(name, 0) + 1
                ins.then_inc(s, 1)
                eng.wait_ge(s, link_count[name])
            return link

        chunks, number = [], {}

        def chunk(name, *parts):
            number[name] = len(chunks)
            chunks.append(parts)

        def cols(src, c0, n, ks=KT, at=0, width=256):
            v = src.rearrange("(k p) c -> p k c", p=P)
            h = ks // 2
            return [(k0, h, at, n, width, v[:, k0:k0 + h, c0:c0 + n]) for k0 in (0, h)]

        def pair(src, c0, c1, n=P):
            v = src.rearrange("(k p) c -> p k c", p=P)
            return [(0, KT, at, n, 256, v[:, :, c:c + n]) for at, c in ((0, c0), (P, c1))]

        for j in range(2):
            v = w_in.rearrange("(k p) c -> p k c", p=P)
            chunk(f"q{j}", *[(0, KT, P * r + HD * g, HD, 256,
                              v[:, :, C_Q + 256 * g + P * j + HD * r:C_Q + 256 * g + P * j + HD * r + HD])
                             for r in range(2) for g in range(G)])
        chunk("cmp", *cols(w_in, C_KV, 256))
        chunk("slc", *cols(w_in, C_KV + 256, 256))
        chunk("win", *cols(w_in, C_KV + 512, 256))
        vin = w_in.rearrange("(k p) c -> p k c", p=P)
        chunk("ga", (0, KT, 0, 32, 48, vin[:, :, C_GATE:C_GATE + 32]),
              (0, KT, 32, RANK, 48, vin[:, :, C_AL:C_AL + RANK]))
        for kv in "kv":
            w1 = a[f"phi_{kv}_w1"][0].rearrange("(s p) c -> p s c", p=P)
            chunk(f"w1{kv}", *[(8 * i, 8, 0, P, P, w1[:, 8 * i:8 * i + 8, :]) for i in range(2)])
        for h in range(GH):
            chunk(f"gqk{h}", *pair(w_in, C_QG + P * h, C_KG + P * h))
            chunk(f"gv{h}", *cols(w_in, C_VG + DV * h, DV))
        for j in range(2):
            chunk(f"za{j}", *cols(w_in, C_ZA + 256 * j, 256))
        for j in range(4):
            chunk(f"zb{j}", *cols(w_in, C_ZB + 256 * j, 256))
        for j in range(4):
            chunk(f"ma{j}", *cols(w_in, C_MRG + 256 * j, 256))
            chunk(f"wa{j}", *cols(a["w_branch_a"][0], 256 * j, 256, ks=4))
            chunk(f"mb{j}", *cols(w_in, C_MRG + D + 256 * j, 256))
            chunk(f"wb{j}", *cols(a["w_branch_b"][0], 256 * j, 256))
        for j in range(4):
            chunk(f"wo{j}", *cols(a["w_out"][0], 256 * j, 256))

        released = {}

        def slot(name, width=256):
            return wr[:, number[name] % NSLOT, 0:KT * width].rearrange("p (k c) -> p k c", c=width)

        def have(eng, name):
            n = number[name]
            eng.wait_ge(sem(f"w_loaded{n % NSLOT}"), 16 * sum(len(c) for c in chunks[n % NSLOT:n + 1:NSLOT]))

        def load_chunks(eng, first, last):
            for n in range(number[first], number[last] + 1):
                if n >= NSLOT:
                    eng.wait_ge(*released[n - NSLOT])
                s = n % NSLOT
                for part in chunks[n]:
                    k0, nk, at, w, width, src = part
                    dst = wr[:, s, 0:2048 // width * width].rearrange("p (k c) -> p k c", c=width)[
                        :, k0:k0 + nk, at:at + w]
                    eng.dma_start(dst, src).then_inc(sem(f"w_loaded{s}"), 16)

        out_count = {}

        def store(eng, dst, src, name="stored"):
            out_count[name] = out_count.get(name, 0) + 1
            return eng.dma_start(dst, src).then_inc(sem(name), 16)

        def feature_major(set_, lhs, ntile, m=P):
            for n in range(3):
                for k in range(ntile):
                    mm = nc.tensor.matmul(ps[0:m, 3 * set_ + n, 0:NF], lhs(k)[0], lhs(k)[1](n),
                                          start=(k == 0), stop=(k == ntile - 1))
            return mm

        def h_cols(k):
            return lambda n: hT[:, k, NF * n:NF * n + NF]

        def banks(set_, m=P):
            return ps[0:m, 3 * set_:3 * set_ + 3, 0:NF]

        def split3(ap):
            return ap.rearrange("p (n c) -> p n c", n=3)

        nsa = ExitStack()
        qT = sb(nsa, "qT", [P, R, TOK])
        kT = sb(nsa, "kT", [P, 4, TOK])
        vtok = sb(nsa, "vtok", [P, TILES, 256])
        o_acc = sb(nsa, "o_acc", [P, PT, 512])
        slope = sb(nsa, "slope", [P, H])
        kc = sb(nsa, "kc", [P, 64])
        vc = sb(nsa, "vc", [64, P])
        kcs = sb(nsa, "kcs", [P, DB, NCS])
        vcs = sb(nsa, "vcs", [NCS, DB, P])
        NK = PAST + ST
        zbias = sb(nsa, "zbias", [P, 2, 2, NK])
        zcb = sb(nsa, "zcb", [P, NCS])
        zcol = sb(nsa, "zcol", [P, 64])
        pi, hi, si = (zcol[:, c:c + 1].bitcast(I32) for c in (0, 1, 2))
        t_row, b_row, sl_row, m0, m1, hf = (zcol[:, c:c + 1] for c in range(3, 9))
        bcols = zcol[:, 16:48]
        NB = 4
        pgs = ExitStack()
        NPG = 6
        pages = sb(pgs, "pages", [P, NPG, 512])

        def gather_cmp(pool, n):
            if n >= NPG:
                pool.wait_ge(sem("pT_done"), n - NPG + 1)
            src = a[("cache_k_cmp", "cache_v_cmp")[n // DB]].rearrange("o n (s j) g d -> (o n s) (j g d)", j=4)
            pool.indirect_dma_start(pages[:, n % NPG, :], None, src,
                                    bass.IndirectOffsetOnAxis(ap=idx[:, n % DB:n % DB + 1], axis=0))\
                .then_inc(sem(f"page_loaded{n % NPG}"), 16)


        s1 = ExitStack()
        x_all = sb(s1, "x_all", [P, TILES, D])
        junk1 = sb(s1, "junk1", [P, 2 * (PAST + ST)])
        ktok = x_all[:, :, 0:512]
        zx, zm = junk1[:, 0:PAST + ST], junk1[:, PAST + ST:2 * (PAST + ST)]
        norm_groups = ((0, 3), (3, 6), (6, TILES))
        NFT = 9
        with nc.Block() as block:
            @block.tensor
            def _(pe):
                pe.wait_ge(sem("consts"), 4)
                for t in range(TILES):
                    n = rows_of(t)
                    pe.wait_ge(sem("xn_ready"), t + 1)
                    for half in range(2):
                        if t >= 1:
                            pe.wait_ge(sem("hT_ready"), 2 * t + half - 1)
                        for k in range(4):
                            mm = nc.tensor.transpose(ps[:, 6 + half, P * k:P * k + n],
                                                     x_all[0:n, t, P * (4 * half + k):P * (4 * half + k) + P],
                                                     ident[0:n, 0:n])
                        mm.then_inc(sem("xT_done"), 1)
                pe.wait_ge(sem("hT_ready"), 2 * TILES)

                def keys_of(name, c0, width=256, m=P):
                    w = slot(name, width)
                    return lambda k: (w[:, k, c0:c0 + m], h_cols(k))

                def q_of(r):
                    w = slot(f"q{r // 2}")
                    c0 = P * (r % 2)
                    return lambda k: (w[:, k, c0:c0 + P], h_cols(k))

                plan = [(f"q{r // 2}", q_of(r), P) for r in range(R)]
                plan += [("cmp", keys_of("cmp", 0), P), ("cmp", keys_of("cmp", P), P),
                         ("slc", keys_of("slc", 0), P), ("win", keys_of("win", 0), P)]
                for f, (name, lhs, m) in enumerate(plan):
                    have(pe, name)
                    if f >= 2:
                        pe.wait_ge(sem("f_copied"), f - 1)
                    feature_major(f % 2, lhs, KT, m).then_inc(sem("f_done"), 1)
                    released[number[name]] = (sem("f_done"), f + 1)
                have(pe, "ga")
                pe.wait_ge(sem("f_copied"), NFT - 2)
                feature_major(0, keys_of("ga", 0, 48, 48), KT, 48).then_inc(sem("f_done"), 1)
                released[number["ga"]] = (sem("f_done"), NFT)
                pe.wait_ge(sem("f_copied"), NFT - 1)
                for t in range(TILES):
                    n = rows_of(t)
                    if t >= 2:
                        pe.wait_ge(sem("ktok_copied"), t - 1)
                    for j in range(4):
                        mm = nc.tensor.transpose(ps[0:n, 6 + t % 2, P * j:P * j + P],
                                                 kT[:, j, P * t:P * t + n], ident[:, :])
                    mm.then_inc(sem("ktok_done"), 1)
                pe.wait_ge(sem("f_copied"), NFT)
                for t in range(TILES):
                    n = rows_of(t)
                    mm = nc.tensor.transpose(ps[0:n, 3, 24 * t:24 * t + 24],
                                             gaT[0:24, P * t:P * t + n], ident[0:24, 0:24])
                mm.then_inc(sem("gate_done"), 1)
                pe.wait_ge(sem("ktok_copied"), TILES)
                for t in range(TILES):
                    n = rows_of(t)
                    if t >= 2:
                        pe.wait_ge(sem("v_copied"), t - 1)
                    for j, name in enumerate(("slc", "win")):
                        for k in range(KT):
                            mm = nc.tensor.matmul(ps[0:n, 6 + t % 2, P * j:P * j + P],
                                                  hT[:, k, P * t:P * t + n], slot(name)[:, k, P:2 * P],
                                                  start=(k == 0), stop=(k == KT - 1))
                    mm.then_inc(sem("v_done"), 1)
                for name in ("slc", "win"):
                    released[number[name]] = (sem("v_done"), TILES)

            @block.gpsimd
            def _(pool):
                pool.dma_start(ab_col, a["gla_alpha_b"].rearrange("o (k p) -> p (o k)", p=P),
                               allow_slow_non_contiguous=True).then_inc(sem("vectors"), 16)
                pool.dma_start(gn_col, a["gla_norm_g"].rearrange("o (k p) -> p (o k)", p=P),
                               allow_slow_non_contiguous=True).then_inc(sem("vectors"), 16)
                for v, name in enumerate(("phi_k_pe", "phi_v_pe")):
                    for par in range(2):
                        pool.dma_start(pe2[HD * par:HD * par + HD, v, :],
                                       a[name][0].rearrange("(s q) d -> q d s", q=2)[par],
                                       allow_slow_non_contiguous=True).then_inc(sem("vectors"), 16)
                pool.dma_start(pt_all, a["page_table"].rearrange("b g -> (b g)").unsqueeze(0)
                               .to_broadcast([P, DB * NPAGES])).then_inc(sem("table"), 16)
                for m in (ident, tri):
                    pool.memset(m[:, :], 0.0 if m is ident else 1.0).then_inc(sem("consts0"), 1)
                pool.wait_ge(sem("consts0"), 2)
                pool.affine_select(out=ident[:, :], in_=ident[:, :], compare_op=ALU.not_equal, fill=1.0,
                                   base=0, pattern=[[-1, P]], channel_multiplier=1).then_inc(sem("consts"), 1)
                pool.affine_select(out=tri[:, :], in_=tri[:, :], compare_op=ALU.is_ge, fill=0.0,
                                   base=0, pattern=[[1, P]], channel_multiplier=-1).then_inc(sem("consts"), 1)
                for h in range(H):
                    pool.memset(slope[:, h:h + 1], 2.0 ** -(h + 1)).then_inc(sem("slopes"), 1)
                pool.wait_ge(sem("slopes"), H)
                for q in range(4):
                    pool.iota(pbase[32 * q:32 * q + 32, :], pattern=[[0, 1]], base=0,
                              channel_multiplier=1).then_inc(sem("pbase"), 1)
                    pool.wait_ge(sem("pbase"), q + 1)
                pool.memset(ssq, 1.0).then_inc(sem("consts"), 1)
                pool.memset(kc[:, :], 0.0).then_inc(sem("consts"), 1)
                link = linker(pool, "pool_link")
                link(nc.gpsimd.iota(pi, pattern=[[0, 1]], base=0, channel_multiplier=1))
                pool.wait_ge(sem("squares"), TILES)
                link(nc.gpsimd.iota(zx[:, 0:PAST].rearrange("p (j c) -> p j c", j=4), pattern=[[-1, 4], [-4, P]],
                                    base=PAST, channel_multiplier=0, allow_small_or_imprecise_dtypes=True))
                link(nc.gpsimd.iota(zx[:, PAST:NK].rearrange("p (b t) -> p b t", t=DS), pattern=[[0, DB], [-1, DS]],
                                    base=0, channel_multiplier=0, allow_small_or_imprecise_dtypes=True))
                link(nc.gpsimd.iota(bcols.rearrange("p (b t) -> p b t", t=DS), pattern=[[1, DB], [0, DS]],
                                    base=0, channel_multiplier=0, allow_small_or_imprecise_dtypes=True))
                link(nc.gpsimd.iota(zcb[:, :], pattern=[[-CS, NCS]], base=PAST - (CB - 1), channel_multiplier=0,
                                    allow_small_or_imprecise_dtypes=True))
                pool.sem_inc(sem("z_iota"), 1)
                pool.wait_ge(sem("idx_ready"), 1)
                for n in range(NPG):
                    gather_cmp(pool, n)

            @block.vector
            def _(dve):
                link = linker(dve, "dve_link")
                for i, (t0, t1) in enumerate(norm_groups):
                    dve.wait_ge(sem("squares"), t1)
                    link(nc.vector.tensor_scalar(rstd[:, t0:t1], ssq[:, t0:t1], 1.0 / D, EPS, ALU.mult, ALU.add))
                    dve.sem_inc(sem("var_ready"), 1)
                    dve.wait_ge(sem("sd_ready"), i + 1)
                    nc.vector.reciprocal(rstd[:, t0:t1], ssq[:, t0:t1]).then_inc(sem("rstd_ready"), 1)
                    if i == 0:
                        dve.wait_ge(sem("ng_loaded"), 16)
                    for t, half in ((t, half) for t in range(t0, t1) for half in range(2)):
                        n = rows_of(t)
                        dve.wait_ge(sem("xT_done"), 2 * t + half + 1)
                        nc.vector.tensor_tensor(
                            hT[:, 4 * half:4 * half + 4, P * t:P * t + n],
                            ps[:, 6 + half, :].rearrange("p (k c) -> p k c", k=4)[:, :, 0:n],
                            ng_col[:, 4 * half:4 * half + 4].unsqueeze(2).to_broadcast([P, 4, n]),
                            ALU.mult).then_inc(sem("hT_ready"), 1)
                dve.wait_ge(sem("vectors"), 16 * 6)
                dve.wait_ge(sem("table"), 16)
                dve.wait_ge(sem("pbase"), 4)
                for q in range(NPAGES):
                    rr = slice(32 * q, 32 * q + 32)
                    link(nc.vector.tensor_scalar(
                        idx[rr, :], pt_all[rr, :].rearrange("p (b g) -> p b g", g=NPAGES)[:, :, q],
                        32, None, ALU.mult))
                    ins = nc.vector.tensor_tensor(idx[rr, :], idx[rr, :], pbase[rr, :].to_broadcast([32, DB]),
                                                  ALU.add)
                    link(ins)
                dve.sem_inc(sem("idx_ready"), 1)
                dve.wait_ge(sem("z_iota"), 1)
                link(nc.vector.tensor_scalar(hi, pi, 3, None, ALU.bitwise_and))
                link(nc.vector.tensor_copy(t_row, hi))
                link(nc.vector.tensor_scalar(hi, pi, 5, None, ALU.logical_shift_right))
                link(nc.vector.tensor_copy(b_row, hi))
                link(nc.vector.tensor_scalar(hi, pi, 2, 7, ALU.logical_shift_right, ALU.bitwise_and))
                link(nc.vector.tensor_copy(hf, hi))
                link(nc.vector.tensor_scalar(m0, hf, float(R), None, ALU.is_lt))
                link(nc.vector.tensor_scalar(m1, hf, float(R), None, ALU.is_ge))
                link(nc.vector.tensor_scalar(hi, hi, -1, 126, ALU.mult, ALU.add))
                link(nc.vector.tensor_scalar(si, hi, 23, None, ALU.logical_shift_left))
                link(nc.vector.tensor_copy(sl_row, zcol[:, 2:3]))
                link(nc.vector.tensor_scalar(zcb[:, :], zcb[:, :], t_row, sl_row, ALU.add, ALU.mult))
                link(nc.vector.tensor_scalar(zx[:, :], zx[:, :], t_row, None, ALU.add))
                new = slice(PAST, NK)
                for gp in range(2):
                    for br in range(2):
                        zb = zbias[:, gp, br, :]
                        link(nc.vector.tensor_scalar(zb, zx[:, :], sl_row, None, ALU.mult))
                        link(nc.vector.tensor_scalar(zm[:, new], zx[:, new], 0.0, BIG, ALU.is_lt, ALU.mult))
                        link(nc.vector.tensor_tensor(zb[:, new], zb[:, new], zm[:, new], ALU.add))
                        link(nc.vector.tensor_scalar(zm[:, new], bcols, float(-NB * gp), b_row, ALU.add, ALU.not_equal))
                        link(nc.vector.tensor_scalar(zm[:, new], zm[:, new], BIG, None, ALU.mult))
                        link(nc.vector.tensor_tensor(zb[:, new], zb[:, new], zm[:, new], ALU.add))
                        if br == 1:
                            link(nc.vector.tensor_scalar(zm[:, :], zx[:, :], float(WIN), BIG, ALU.is_ge, ALU.mult))
                            link(nc.vector.tensor_tensor(zb, zb, zm[:, :], ALU.add))
                for t in range(TILES):
                    n = rows_of(t)
                    dve.wait_ge(sem("ktok_done"), t + 1)
                    nc.vector.tensor_copy(ktok[0:n, t, :], ps[0:n, 6 + t % 2, :]).then_inc(sem("ktok_copied"), 1)

            @block.scalar
            def _(act):
                act.wait_ge(sem("consts"), 3)
                for i, (t0, t1) in enumerate(norm_groups):
                    for t in range(t0, t1):
                        n = rows_of(t)
                        act.wait_ge(sem(f"x_loaded{t}"), 16)
                        if t >= 1:
                            act.wait_ge(sem("squares"), t)
                        nc.scalar.activation(junk1[0:n, 0:D], x_all[0:n, t, :], ACT.Square,
                                             accum_out=ssq[0:n, t:t + 1]).then_inc(sem("squares"), 1)
                    act.wait_ge(sem("var_ready"), i + 1)
                    act.wait_ge(sem("squares"), t1)
                    nc.scalar.activation(ssq[:, t0:t1], rstd[:, t0:t1], ACT.Sqrt).then_inc(sem("sd_ready"), 1)
                    act.wait_ge(sem("rstd_ready"), i + 1)
                    for t in range(t0, t1):
                        n = rows_of(t)
                        nc.scalar.activation(x_all[0:n, t, :], x_all[0:n, t, :], ACT.Copy,
                                             scale=rstd[0:n, t:t + 1]).then_inc(sem("xn_ready"), 1)
                for f in range(NFT - 1):
                    act.wait_ge(sem("f_done"), f + 1)
                    dst = qT[:, f, :] if f < R else kT[:, f - R, :]
                    nc.scalar.activation(split3(dst), banks(f % 2), ACT.Copy,
                                         scale=-HD ** -0.5 if f < R else 1.0).then_inc(sem("f_copied"), 1)
                act.wait_ge(sem("f_done"), NFT)
                nc.scalar.activation(split3(gaT[:, :]), banks(0, 48), ACT.Copy).then_inc(sem("f_copied"), 1)
                act.wait_ge(sem("gate_done"), 1)
                nc.scalar.activation(gate[:, 0:PT, :], ps[:, 3, 0:24 * PT].rearrange("p (t c) -> p t c", c=24),
                                     ACT.Sigmoid).then_inc(sem("gate_ready"), 1)
                nc.scalar.activation(gate[0:ST, PT, :], ps[0:ST, 3, 24 * PT:24 * PT + 24],
                                     ACT.Sigmoid).then_inc(sem("gate_ready"), 1)
                for t in range(TILES):
                    n = rows_of(t)
                    act.wait_ge(sem("v_done"), t + 1)
                    nc.scalar.activation(vtok[0:n, t, :], ps[0:n, 6 + t % 2, 0:256], ACT.Copy)\
                        .then_inc(sem("v_copied"), 1)

            @block.sync
            def _(sp):
                sp.dma_start(ng_col, a["norm_g"].rearrange("o (k p) -> p (o k)", p=P),
                             allow_slow_non_contiguous=True).then_inc(sem("ng_loaded"), 16)
                for t in range(TILES):
                    src = a["x_prompt"][0, P * t:P * t + P, :] if t < PT else \
                        a["x_sample"].rearrange("b s d -> (b s) d")
                    sp.dma_start(x_all[0:rows_of(t), t, :], src).then_inc(sem(f"x_loaded{t}"), 16)
                load_chunks(sp, "q0", "w1k")
                for src, dst in ((a["cache_k_win"], s_kw), (a["cache_v_win"], s_vw)):
                    store(sp, dst[0, :, 0:WIN - DS].rearrange("b s g d -> b (s g d)"),
                          src[0, :, DS:WIN].rearrange("b s g d -> b (s g d)"))
                sp.wait_ge(sem("ktok_copied"), TILES)
                for j, (pd, sd) in enumerate(((p_kc, s_kc), (p_vc, s_vc), (p_ks, s_ks), (p_kw, s_kw))):
                    t0 = 0 if j < 3 else PT - WIN // P
                    store(sp, pd[0, 0].rearrange("(t p) g d -> p t (g d)", p=P), ktok[:, t0:PT, P * j:P * j + P], "ktok_stored")
                    if j < 3:
                        store(sp, sd[0].rearrange("b s g d -> (b s) (g d)"), ktok[0:ST, PT, P * j:P * j + P], "ktok_stored")
                    else:
                        for b in range(DB):
                            store(sp, sd[0, b, WIN - DS:WIN].rearrange("s g d -> s (g d)"),
                                  ktok[DS * b:DS * b + DS, PT, P * j:P * j + P], "ktok_stored")
                sp.wait_ge(sem("gate_ready"), 2)
                for b in range(DB):
                    sp.dma_start(gate_spill[b].rearrange("x t c -> t c x"),
                                 gate[DS * b:DS * b + DS, PT, :].rearrange("t (c x) -> t c x", c=3),
                                 allow_slow_non_contiguous=True).then_inc(sem("gate_spilled"), 16)
                load_chunks(sp, "w1v", "w1v")
                sp.wait_ge(sem("v_copied"), TILES)
                for j, (pd, sd) in enumerate(((p_vs, s_vs), (p_vw, s_vw))):
                    t0 = 0 if j == 0 else PT - WIN // P
                    store(sp, pd[0, 0].rearrange("(t p) g d -> p t (g d)", p=P), vtok[:, t0:PT, P * j:P * j + P])
                    if j == 0:
                        store(sp, sd[0].rearrange("b s g d -> (b s) (g d)"), vtok[0:ST, PT, 0:P])
                    else:
                        for b in range(DB):
                            store(sp, sd[0, b, WIN - DS:WIN].rearrange("s g d -> s (g d)"),
                                  vtok[DS * b:DS * b + DS, PT, P:2 * P])
                sp.wait_ge(sem("ktok_stored"), 16 * out_count["ktok_stored"])
        s1.close()

        s2 = ExitStack()
        cX = sb(s2, "cX", [P, 2, G, NB, 2, P])
        kX = sb(s2, "kX", [P, 2, G, SEQ // 2])
        w2 = sb(s2, "w2", [P, 2, HD])
        hid = sb(s2, "hid", [P, 2, 2 * (64 + DB * NCS)])
        cbias = sb(s2, "cbias", [P, 2])
        NS2, NSH = DB * NCS, NB * NCS
        hid_reads = (8, 12, 20, 24)

        def turn_bank(n, par):
            return (6, 3)[n % 2] + par

        with nc.Block() as block:
            @block.tensor
            def _(pe):
                def turn(st):
                    for n in range(NB * st, NB * st + NB):
                        pe.wait_ge(sem(f"page_loaded{n % NPG}"), 16 * (n // NPG + 1))
                        if n >= 2:
                            for who in ("cX_dve", "cX_act"):
                                pe.wait_ge(sem(who), n - 1)
                        for j in range(4):
                            mm = nc.tensor.transpose(ps[:, turn_bank(n, j % 2), P * (j // 2):P * (j // 2) + P],
                                                     pages[:, n % NPG, P * j:P * j + P], ident[:, :])
                        mm.then_inc(sem("pT_done"), 1)

                def hidden(st):
                    kv, half = divmod(st, 2)
                    for who in ("cX_dve", "cX_act"):
                        pe.wait_ge(sem(who), NB * (st + 1))
                    name = "w1" + "kv"[kv]
                    if half == 0:
                        have(pe, name)
                        for who in ("kX_dve", "kX_act"):
                            pe.wait_ge(sem(who), 4)
                    if st >= 1:
                        pe.wait_ge(sem("hid_read"), hid_reads[st - 1])
                    if st == 2:
                        pe.wait_ge(sem("c2_copied"), 2)
                    w = wr[:, number[name] % NSLOT, :].rearrange("p (s c) -> p s c", c=P)
                    for s in range(16):
                        flags = dict(start=(s == 0), stop=(s == 15))
                        if half == 0:
                            nc.tensor.matmul(ps[:, 5, 511:512], w[:, s, :], pe2[:, kv, s:s + 1], **flags)
                            nc.tensor.matmul(ps[:, 2, 0:G * NCP].rearrange("p (g c) -> p g c", g=G), w[:, s, :],
                                             kX[:, kv, :, s:s + 8 * (NCP - 1) + 1:8], **flags)
                        c0 = s // 2
                        mm = nc.tensor.matmul(ps[:, 0, 0:G * NSH].rearrange("p (b c) -> p b c", b=G * NB), w[:, s, :],
                                              cX[:, half, :, :, s % 2, c0:c0 + 4 * (NCS - 1) + 1:4]
                                              .rearrange("p g b c -> p (g b) c"), **flags)
                    mm.then_inc(sem("hid_done"), 1)
                    released[number[name]] = (sem("hid_done"), st + 1)

                def second(kv):
                    if kv == 0:
                        pe.wait_ge(sem("w2_loaded"), 32)
                    pe.wait_ge(sem("hid_ready"), 6 * (kv + 1))
                    if kv == 0:
                        for g in range(G):
                            nc.tensor.matmul(ps[HD * g:HD * g + HD, 5, 0:NCP], w2[:, 0, :],
                                             hid[:, 0, 64 * g:64 * g + NCP], start=True, stop=True)
                        for g in range(G):
                            mm = nc.tensor.matmul(ps[HD * g:HD * g + HD, 5, 64:64 + NS2], w2[:, 0, :],
                                                  hid[:, 0, 128 + NS2 * g:128 + NS2 * g + NS2],
                                                  start=True, stop=True)
                    else:
                        pe.wait_ge(sem("c2_copied"), 2)
                        for g in range(G):
                            nc.tensor.matmul(ps[0:NCP, 5, HD * g:HD * g + HD],
                                             hid[:, 0, 64 * g:64 * g + NCP], w2[:, 1, :], start=True, stop=True)
                        for b in range(DB):
                            for g in range(G):
                                c0 = 128 + NS2 * g + NCS * b
                                mm = nc.tensor.matmul(
                                    ps[0:NCS, 6 + b // 4, P * (b % 4) + HD * g:P * (b % 4) + HD * g + HD],
                                    hid[:, 0, c0:c0 + NCS], w2[:, 1, :], start=True, stop=True)
                    mm.then_inc(sem("c2_done"), 1)

                turn(0)
                turn(1)
                hidden(0)
                turn(2)
                hidden(1)
                second(0)
                turn(3)
                hidden(2)
                hidden(3)
                second(1)

            @block.gpsimd
            def _(pool):
                for n in range(NPG, 2 * DB):
                    gather_cmp(pool, n)

            def regroup(copy, par, name):
                def prompt():
                    for kv in range(2):
                        for g in range(G):
                            copy(kX[HD * par:HD * par + HD, kv, g, :], kT[HD * g:HD * g + HD, kv, par:SEQ:2])\
                                .then_inc(sem("kX_" + name), 1)

                def batches(eng, st):
                    if st >= 2:
                        eng.wait_ge(sem("hid_done"), st - 1)
                    for n in range(NB * st, NB * st + NB):
                        eng.wait_ge(sem("pT_done"), n + 1)
                        for g in range(G):
                            ins = copy(cX[HD * par:HD * par + HD, st % 2, g, n % NB, :, :],
                                       ps[HD * g:HD * g + HD, turn_bank(n, par), 0:2 * P].rearrange(
                                           "p (j c) -> p j c", c=P))
                        ins.then_inc(sem("cX_" + name), 1)
                return prompt, batches

            @block.vector
            def _(dve):
                link = linker(dve, "dve_link")
                prompt, batches = regroup(nc.vector.tensor_copy, 0, "dve")

                def silu(st):
                    kv, half = divmod(st, 2)
                    dve.wait_ge(sem("hid_read"), hid_reads[st])
                    spans = [(64 * g, NCP) for g in range(G)] if half == 0 else []
                    spans += [(128 + NS2 * g + NSH * half, NSH) for g in range(G)]
                    for c0, n in spans:
                        nc.vector.tensor_tensor(hid[:, 0, c0:c0 + n], hid[:, 0, c0:c0 + n], hid[:, 1, c0:c0 + n],
                                                ALU.mult).then_inc(sem("hid_ready"), 1)

                def bias_of(kv):
                    dve.wait_ge(sem("hid_done"), 2 * kv + 1)
                    nc.vector.tensor_copy(cbias[:, kv:kv + 1], ps[:, 5, 511:512]).then_inc(sem("cbias_ready"), 1)

                batches(dve, 0)
                prompt()
                batches(dve, 1)
                bias_of(0)
                batches(dve, 2)
                silu(0)
                silu(1)
                dve.wait_ge(sem("c2_done"), 1)
                nc.vector.tensor_copy(kc[:, 0:NCP], ps[:, 5, 0:NCP]).then_inc(sem("c2_copied"), 1)
                nc.vector.tensor_copy(kcs[:, :, :].rearrange("p b c -> p (b c)"), ps[:, 5, 64:64 + NS2])\
                    .then_inc(sem("c2_copied"), 1)
                batches(dve, 3)
                bias_of(1)
                silu(2)
                silu(3)
                link(nc.vector.memset(vc[:, :], 0.0))
                dve.wait_ge(sem("c2_done"), 2)
                nc.vector.tensor_copy(vc[0:NCP, :], ps[0:NCP, 5, 0:P]).then_inc(sem("c2_copied"), 1)
                nc.vector.tensor_copy(vcs[:, :, :].rearrange("p (x b) c -> p x (b c)", x=2),
                                      ps[0:NCS, 6:8, :]).then_inc(sem("c2_copied"), 1)

            @block.scalar
            def _(act):
                copy = lambda dst, src: nc.scalar.activation(dst, src, ACT.Copy)
                prompt, batches = regroup(copy, 1, "act")

                def activations(st):
                    kv, half = divmod(st, 2)
                    act.wait_ge(sem("cbias_ready"), kv + 1)
                    act.wait_ge(sem("hid_done"), st + 1)
                    if st == 2:
                        act.wait_ge(sem("c2_done"), 1)
                    spans = [(2, NCP * g, 64 * g, NCP) for g in range(G)] if half == 0 else []
                    spans += [(0, NSH * g, 128 + NS2 * g + NSH * half, NSH) for g in range(G)]
                    for bank, b0, c0, n in spans:
                        for i, func in enumerate((ACT.Identity, ACT.Sigmoid)):
                            nc.scalar.activation(hid[:, i, c0:c0 + n], ps[:, bank, b0:b0 + n], func,
                                                 bias=cbias[:, kv:kv + 1]).then_inc(sem("hid_read"), 1)

                batches(act, 0)
                prompt()
                batches(act, 1)
                activations(0)
                batches(act, 2)
                activations(1)
                batches(act, 3)
                activations(2)
                activations(3)

            @block.sync
            def _(sp):
                for kv in range(2):
                    sp.dma_start(w2[:, kv, :], a[("phi_k_w2", "phi_v_w2")[kv]][0]).then_inc(sem("w2_loaded"), 16)
                load_chunks(sp, "gqk0", "gv1")
        s2.close()
        pgs.close()

        s3 = ExitStack()
        sS = sb(s3, "sS", [P, 2, 1024])
        pP = sb(s3, "pP", [P, 2, 1024])
        pPT = sb(s3, "pPT", [P, 2, 1024])
        bias = sb(s3, "bias", [P, 2, 1024 + 640])
        ndist = sb(s3, "ndist", [P, 1024])
        cdist = sb(s3, "cdist", [P, 2, 512])
        stat = sb(s3, "stat", [P, 256])
        tmp = sb(s3, "tmp", [P, 2, 512])
        cP = pP[:, :, 512:1024]
        mcol = stat[:, 0:16]
        wcol = stat[:, 32:48]

        def lcol(h):
            return stat[:, 64 + 16 * (h % 2):80 + 16 * (h % 2)]

        mcmp = (stat[:, 96:104], stat[:, 48:56])
        lcmp = (stat[:, 104:112], stat[:, 56:64])

        def units():
            return [(h, i, br) for h in range(H) for i in range(PT) for br in range(2)]

        U = units()

        def keys_range(i, br):
            k0 = 0 if br == 0 else max(0, i - WIN // P)
            return k0, i + 1 - k0

        parts, nparts = [], 0
        for h, i, br in U:
            nk = keys_range(i, br)[1]
            cuts = [(0, nk)] if nk <= 4 else [(0, (nk + 1) // 2), ((nk + 1) // 2, nk // 2)]
            parts.append([(nparts + j, c, w) for j, (c, w) in enumerate(cuts)])
            nparts += len(cuts)

        def copied(m):
            return sem(("pT_act", "pT_dve")[m % 2]), m // 2 + 1

        def copy_part(eng, copy, n, which):
            for m, c, w in parts[n]:
                if m % 2 != which:
                    continue
                eng.wait_ge(sem("pT_ready"), m + 1)
                if n >= 2:
                    eng.wait_ge(sem("av_done"), n - 1)
                copy(pPT[:, n % 2, P * c:P * (c + w)], ps[:, 4 + m % 2, 0:P * w])\
                    .then_inc(sem(("pT_act", "pT_dve")[which]), 1)

        with nc.Block() as block:
            @block.tensor
            def _(pe):
                def cmp_scores(i):
                    if i >= 2:
                        pe.wait_ge(sem("cmp_scored"), i - 1)
                    for h in range(H):
                        g, r = h // R, h % R
                        mm = nc.tensor.matmul(ps[:, 2 * (i % 2) + g, 64 * r:64 * r + P].rearrange(
                                                  "p (x c) -> p x c", x=2),
                                              qT[HD * g:HD * g + HD, r, P * i:P * i + P],
                                              kc[HD * g:HD * g + HD, :].unsqueeze(1).to_broadcast([HD, 2, 64]),
                                              start=True, stop=True)
                    mm.then_inc(sem("cmp_qk"), 1)

                def cmp_turn(i):
                    pe.wait_ge(sem("cmp_probs"), i + 1)
                    if i >= 1:
                        pe.wait_ge(sem("cmp_pT"), 2 * i)
                    for h in range(H):
                        mm = nc.tensor.transpose(ps[0:64, 4 + h // 4, P * (h % 4):P * (h % 4) + P],
                                                 cP[:, i % 2, 64 * h:64 * h + 64], ident[:, :])
                        if h % 4 == 3:
                            mm.then_inc(sem("cmp_T"), 1)

                def cmp_values(i):
                    pe.wait_ge(sem("cmp_pT"), 2 * i + 2)
                    if i >= 2:
                        pe.wait_ge(sem("cmp_out"), i - 1)
                    for h in range(H):
                        x = min(2, H - h)
                        v = vc[:, HD * (h // R):HD * (h // R) + HD].unsqueeze(1).to_broadcast([64, x, HD])
                        mm = nc.tensor.matmul(ps[:, 6 + i % 2, HD * h:HD * (h + x)].rearrange("p (x d) -> p x d", x=x),
                                              pPT[0:64, i % 2, P * h:P * h + P], v, start=True, stop=True)
                    mm.then_inc(sem("cmp_av"), 1)

                cmp_scores(0)
                cmp_scores(1)
                for i in range(PT + 1):
                    if i < PT:
                        cmp_turn(i)
                    if i + 2 < PT:
                        cmp_scores(i + 2)
                    if i >= 1:
                        cmp_values(i - 1)
                pe.wait_ge(sem("cmp_out"), PT)

                def scores(n):
                    h, i, br = U[n]
                    g, r = h // R, h % R
                    k0, nk = keys_range(i, br)
                    if n >= 2:
                        pe.wait_ge(sem("scored"), n - 1)
                    for c in range(0, nk, 4):
                        w = min(4, nk - c) * P
                        mm = nc.tensor.matmul(ps[:, 2 * (n % 2) + c // 4, 0:w],
                                              qT[HD * g:HD * g + HD, r, P * i:P * i + P],
                                              kT[HD * g:HD * g + HD, 2 + br, P * (k0 + c):P * (k0 + c) + w],
                                              start=True, stop=True)
                    mm.then_inc(sem("qk_done"), 1)

                def transposes(n):
                    pe.wait_ge(sem("probs"), n + 1)
                    for m, c, w in parts[n]:
                        if m >= 2:
                            pe.wait_ge(*copied(m - 2))
                        for k in range(w):
                            mm = nc.tensor.transpose(ps[:, 4 + m % 2, P * k:P * k + P],
                                                     pP[:, n % 2, P * (c + k):P * (c + k) + P], ident[:, :])
                        mm.then_inc(sem("pT_ready"), 1)

                def values(n):
                    h, i, br = U[n]
                    g = h // R
                    k0, nk = keys_range(i, br)
                    for m, c, w in parts[n]:
                        pe.wait_ge(*copied(m))
                    if i == 0 and h >= 1:
                        pe.wait_ge(sem("head_out"), 2 * (h - 1) + br + 1)
                    copies = min(2, PT - i)
                    for k in range(nk):
                        v = vtok[:, k0 + k, P * br + HD * g:P * br + HD * g + HD].unsqueeze(1)
                        mm = nc.tensor.matmul(
                            ps[:, 6 + br, HD * i:HD * (i + copies)].rearrange("p (x d) -> p x d", x=copies),
                            pPT[:, n % 2, P * k:P * k + P], v.to_broadcast([P, copies, HD]),
                            start=(k == 0), stop=(k == nk - 1))
                    mm.then_inc(sem("av_done"), 1)

                scores(0)
                scores(1)
                for n in range(len(U) + 1):
                    if n < len(U):
                        transposes(n)
                    if n >= 1:
                        values(n - 1)
                    if n + 2 < len(U):
                        scores(n + 2)

            @block.gpsimd
            def _(pool):
                link = linker(pool, "pool_link")
                pool.wait_ge(sem("slopes"), H)
                for i in range(PT):
                    if i >= 2:
                        pool.wait_ge(sem("cmp_scored"), i - 1)
                    v = cdist[:, i % 2, :].rearrange("p (h c) -> p h c", h=H)
                    link(nc.gpsimd.iota(v, pattern=[[0, H], [-CS, 64]], base=P * i - (CB - 1), channel_multiplier=1,
                                        allow_small_or_imprecise_dtypes=True))
                    link(nc.gpsimd.tensor_tensor(v, v, slope[:, :].unsqueeze(2).to_broadcast([P, H, 64]), ALU.mult))
                    nc.gpsimd.affine_select(out=v, in_=v, compare_op=ALU.is_ge, fill=BIG, base=P * i - (CB - 1),
                                            pattern=[[0, H], [-CS, 64]], channel_multiplier=1)\
                        .then_inc(sem("cbias"), 1)
                link(nc.gpsimd.iota(ndist[:, :], pattern=[[-1, 1024]], base=896, channel_multiplier=1,
                                    allow_small_or_imprecise_dtypes=True))
                for h in range(H):
                    if h >= 2:
                        pool.wait_ge(sem("scored"), 16 * (h - 1))
                    bs, bw = bias[:, h % 2, 0:1024], bias[:, h % 2, 1024:1664]
                    link(nc.gpsimd.tensor_scalar(bs, ndist[:, :], 2.0 ** -(h + 1), None, ALU.mult))
                    link(nc.gpsimd.affine_select(out=bs, in_=bs, compare_op=ALU.is_ge, fill=BIG, base=896,
                                                 pattern=[[-1, 1024]], channel_multiplier=1))
                    link(nc.gpsimd.tensor_copy(bw, bs[:, 384:1024]))
                    nc.gpsimd.affine_select(out=bw[:, 0:P], in_=bw[:, 0:P], compare_op=ALU.is_gt, fill=BIG, base=0,
                                            pattern=[[1, P]], channel_multiplier=-1).then_inc(sem("bias_ready"), 1)

            @block.vector
            def _(dve):
                link = linker(dve, "dve_link")
                v8 = lambda ap: ap.rearrange("p (h c) -> p h c", h=H)
                wide = lambda ap: ap.unsqueeze(2).to_broadcast([P, H, 64])
                def cmp_score(i):
                    dve.wait_ge(sem("cmp_qk"), i + 1)
                    dve.wait_ge(sem("cbias"), i + 1)
                    if i >= 2:
                        dve.wait_ge(sem("cmp_exp"), i - 1)
                    t = sS[:, i % 2, 0:512]
                    nc.vector.tensor_tensor(t.rearrange("p (g c) -> p g c", g=G),
                                            ps[:, 2 * (i % 2):2 * (i % 2) + 2, 0:256],
                                            cdist[:, i % 2, :].rearrange("p (g c) -> p g c", g=G), ALU.add)\
                        .then_inc(sem("cmp_scored"), 1)
                    dve.wait_ge(sem("cmp_scored"), i + 1)
                    m = mcmp[i % 2]
                    if i >= 2:
                        dve.wait_ge(sem("cmp_sub"), i - 1)
                    link(nc.vector.tensor_reduce(m, v8(t), AX, ALU.min))
                    nc.vector.tensor_tensor(v8(sS[:, i % 2, 512:1024]), v8(t), wide(m), ALU.subtract)\
                        .then_inc(sem("cmp_sub"), 1)

                def cmp_weights(i):
                    e = pP[:, i % 2, 0:512]
                    dve.wait_ge(sem("cmp_exp"), i + 1)
                    if P * i < CB - 1:
                        link(nc.vector.scalar_tensor_tensor(out=e, in0=sS[:, i % 2, 0:512], scalar=0.5 * BIG, in1=e,
                                                            op0=ALU.is_lt, op1=ALU.mult))
                    l = lcmp[i % 2]
                    if i >= 2:
                        dve.wait_ge(sem("cmp_probs"), i - 1)
                    link(nc.vector.tensor_reduce(l, v8(e), AX, ALU.add))
                    link(nc.vector.tensor_scalar(l, l, TINY, None, ALU.max))
                    link(nc.vector.reciprocal(l, l))
                    link(nc.vector.tensor_tensor(l, l, gate[:, i, 0:8], ALU.mult))
                    if i >= 2:
                        dve.wait_ge(sem("cmp_T"), 2 * (i - 1))
                    nc.vector.tensor_tensor(v8(cP[:, i % 2, :]), v8(e), wide(l), ALU.mult)\
                        .then_inc(sem("cmp_probs"), 1)

                cmp_score(0)
                cmp_score(1)
                cmp_weights(0)
                for i in range(1, PT):
                    cmp_weights(i)
                    if i + 1 < PT:
                        cmp_score(i + 1)
                dve.wait_ge(sem("cmp_out"), PT)

                def score(n):
                    h, i, br = U[n]
                    k0, nk = keys_range(i, br)
                    dve.wait_ge(sem("qk_done"), n + 1)
                    dve.wait_ge(sem("bias_ready"), h + 1)
                    if n >= 2:
                        dve.wait_ge(sem("probs"), n - 1)
                    w = nk * P
                    b0 = (1024 if br == 0 else 1664) - w
                    nc.vector.tensor_tensor_reduce(
                        sS[:, n % 2, 0:w], ps[:, 2 * (n % 2):2 * (n % 2) + 2, :].rearrange("p a c -> p (a c)")[:, 0:w],
                        bias[:, h % 2, b0:b0 + w], 1.0, 3e38, ALU.add, ALU.min,
                        mcol[:, 2 * i + br:2 * i + br + 1]).then_inc(sem("scored"), 1)

                w = wcol.rearrange("p (i b) -> p b i", b=2)

                def weigh(h):
                    dve.wait_ge(sem("probs"), 16 * h + 16)
                    link(nc.vector.tensor_scalar(wcol, lcol(h), TINY, None, ALU.max))
                    link(nc.vector.reciprocal(wcol, wcol))
                    link(nc.vector.tensor_tensor(w, w, gate[:, 0:PT, 8 + h:24:8].rearrange("p i b -> p b i"), ALU.mult))

                def scale(h):
                    for br in range(2):
                        dve.wait_ge(sem("av_done"), 16 * h + 15 + br)
                        nc.vector.tensor_tensor(v8(tmp[:, br, :]), v8(ps[:, 6 + br, :]), wide(w[:, br, :]), ALU.mult)\
                            .then_inc(sem("head_out"), 1)

                def add(h):
                    o = o_acc[:, 0:PT, HD * h:HD * h + HD]
                    for br in range(2):
                        dve.wait_ge(sem("head_out"), 2 * h + br + 1)
                        link(nc.vector.tensor_tensor(o, o, v8(tmp[:, br, :]), ALU.add))

                score(0)
                score(1)
                for n in range(len(U) + 1):
                    head_end = n >= 1 and n % 16 == 0
                    if head_end:
                        weigh(n // 16 - 1)
                    if n < len(U):
                        copy_part(dve, nc.vector.tensor_copy, n, 1)
                    if head_end:
                        scale(n // 16 - 1)
                    if n + 2 < len(U):
                        score(n + 2)
                    if head_end:
                        add(n // 16 - 1)

            @block.scalar
            def _(act):
                def cmp_copies(i):
                    for j in range(2):
                        act.wait_ge(sem("cmp_T"), 2 * i + j + 1)
                        if i >= 2:
                            act.wait_ge(sem("cmp_av"), i - 1)
                        nc.scalar.activation(pPT[0:64, i % 2, 512 * j:512 * j + 512], ps[0:64, 4 + j, :], ACT.Copy)\
                            .then_inc(sem("cmp_pT"), 1)

                for i in range(PT + 1):
                    if i < PT:
                        act.wait_ge(sem("cmp_sub"), i + 1)
                        if i >= 2:
                            act.wait_ge(sem("cmp_probs"), i - 1)
                        nc.scalar.activation(pP[:, i % 2, 0:512], sS[:, i % 2, 512:1024], ACT.Exp, scale=-1.0)\
                            .then_inc(sem("cmp_exp"), 1)
                    if i >= 1:
                        cmp_copies(i - 1)
                    if i >= 2:
                        act.wait_ge(sem("cmp_av"), i - 1)
                        nc.scalar.activation(o_acc[:, i - 2, :], ps[:, 6 + i % 2, :], ACT.Copy)\
                            .then_inc(sem("cmp_out"), 1)
                act.wait_ge(sem("cmp_av"), PT)
                nc.scalar.activation(o_acc[:, PT - 1, :], ps[:, 6 + (PT - 1) % 2, :], ACT.Copy).then_inc(sem("cmp_out"), 1)

                def probs(n):
                    h, i, br = U[n]
                    w = keys_range(i, br)[1] * P
                    act.wait_ge(sem("scored"), n + 1)
                    if n >= 2:
                        act.wait_ge(sem("pT_ready"), parts[n - 2][-1][0] + 1)
                    if h >= 2 and i == 0:
                        act.wait_ge(sem("head_out"), 2 * (h - 1))
                    c = 2 * i + br
                    nc.scalar.activation(pP[:, n % 2, 0:w], sS[:, n % 2, 0:w], ACT.Exp, bias=mcol[:, c:c + 1],
                                         scale=-1.0, accum_out=lcol(h)[:, c:c + 1]).then_inc(sem("probs"), 1)

                copy = lambda dst, src: nc.scalar.activation(dst, src, ACT.Copy)
                probs(0)
                for n in range(len(U)):
                    if n + 1 < len(U):
                        probs(n + 1)
                    copy_part(act, copy, n, 0)

        s3.close()

        s4 = ExitStack()
        Qb = sb(s4, "Qb", [P, DB, 32])
        kp = sb(s4, "kp", [P, 2, 4, 512])
        vp = sb(s4, "vp", [P, 2, 4, 512])
        kpT = sb(s4, "kpT", [P, 2, NB, 512])
        zS = sb(s4, "zS", [P, 2, NK])
        zP = sb(s4, "zP", [P, 2, NK])
        zPT = sb(s4, "zPT", [P, 5, P])
        orow = sb(s4, "orow", [P, 2, HD])
        grow = sb(s4, "grow", [P, 2, 3])
        w0, w1 = (zcol[:, c:c + 1] for c in (9, 10))
        zmin = [zcol[:, c:c + 1] for c in (11, 12)]
        zsum = [zcol[:, c:c + 1] for c in (13, 14)]
        ZU = [(0, 2), (1, 2)] + [(gp, br) for gp in range(2) for br in range(2)]
        PU = [(gp, br) for gp, br in ZU if br < 2]

        def fetch(eng, n):
            gp, br = PU[n]
            for dst, name, slc, win in ((kp, "kp", a["cache_k_slc"], a["cache_k_win"]),
                                        (vp, "vp", a["cache_v_slc"], a["cache_v_win"])):
                if n >= 2 and name == "kp":
                    eng.wait_ge(sem("kpT_done"), NB * (n - 1))
                elif n >= 2:
                    eng.wait_ge(sem("z_av"), ZU.index(PU[n - 2]) + 1)
                for b in range(NB):
                    B = NB * gp + b
                    if br == 0:
                        ins = eng.indirect_dma_start(
                            dst[:, n % 2, b, :], None, slc.rearrange("o n (s j) g d -> (o n s) (j g d)", j=4),
                            bass.IndirectOffsetOnAxis(ap=idx[:, B:B + 1], axis=0))
                    else:
                        ins = eng.dma_start(dst[:, n % 2, b, :],
                                            win[0, B].rearrange("(p j) g d -> p (j g d)", j=4))
                    ins.then_inc(sem(f"{name}_loaded{n % 2}"), 16)

        def copy_keys(eng, copy, u, which):
            u2 = PU.index(ZU[u])
            for b in range(which, NB, 2):
                eng.wait_ge(sem("kpT_done"), NB * u2 + b + 1)
                if b == which and u2 >= 2:
                    eng.wait_ge(sem("z_qk"), u - 1)
                copy(kpT[:, u2 % 2, b, :], ps[:, 4 + b % 2, :]).then_inc(sem(("kpT_dve", "kpT_act")[which]), 1)

        with nc.Block() as block:
            @block.tensor
            def _(pe):
                pe.wait_ge(sem("Qb_ready"), G * R)

                def front(u):
                    gp, br = ZU[u]
                    s0 = 2 * (u % 2)
                    if br < 2:
                        u2 = PU.index(ZU[u])
                        pe.wait_ge(sem(f"kp_loaded{u2 % 2}"), 16 * NB * (u2 // 2 + 1))
                        for b in range(NB):
                            c = NB * u2 + b
                            if c >= 2:
                                pe.wait_ge(sem(("kpT_dve", "kpT_act")[c % 2]), c // 2)
                            for j in range(4):
                                mm = nc.tensor.transpose(ps[:, 4 + c % 2, P * j:P * j + P],
                                                         kp[:, u2 % 2, b, P * j:P * j + P], ident[:, :])
                            mm.then_inc(sem("kpT_done"), 1)
                        for who in ("kpT_dve", "kpT_act"):
                            pe.wait_ge(sem(who), 2 * (u2 + 1))
                    if u >= 2:
                        pe.wait_ge(sem("z_scored"), u - 1)
                    for b in range(NB):
                        rows = slice(32 * b, 32 * b + 32)
                        q = Qb[:, NB * gp + b, :]
                        if br == 2:
                            mm = nc.tensor.matmul(ps[rows, s0, 0:NCS], q, kcs[:, NB * gp + b, :], start=True, stop=True)
                        else:
                            nc.tensor.matmul(ps[rows, s0, 0:PAST], q, kpT[:, u2 % 2, b, :], start=True, stop=True)
                            mm = nc.tensor.matmul(ps[rows, s0 + 1, 0:ST], q, kT[:, 2 + br, SEQ:TOK],
                                                  start=True, stop=True)
                    mm.then_inc(sem("z_qk"), 1)

                def back(u):
                    gp, br = ZU[u]
                    pe.wait_ge(sem("z_probs"), u + 1)
                    if u >= 1:
                        pe.wait_ge(sem("zPT_copied"), u)
                        pe.wait_ge(sem("z_out"), u)
                    if br == 2:
                        mm = nc.tensor.transpose(ps[0:NCS, 7, 0:P], zP[:, u % 2, 0:NCS], ident[:, :])
                    else:
                        u2 = PU.index(ZU[u])
                        for j in range(4):
                            nc.tensor.transpose(ps[:, 7, P * j:P * j + P], zP[:, u % 2, P * j:P * j + P], ident[:, :])
                        mm = nc.tensor.transpose(ps[0:ST, 6, 2 * P:3 * P], zP[:, u % 2, PAST:NK], ident[:, :])
                    mm.then_inc(sem("zPT_done"), 1)
                    pe.wait_ge(sem("zPT_copied"), u + 1)
                    if br < 2:
                        pe.wait_ge(sem(f"vp_loaded{u2 % 2}"), 16 * NB * (u2 // 2 + 1))
                    for b in range(NB):
                        rows = slice(32 * b, 32 * b + 32)
                        if br == 2:
                            mm = nc.tensor.matmul(ps[rows, 6, 0:P], zPT[0:NCS, 0, rows], vcs[:, NB * gp + b, :],
                                                  start=True, stop=True)
                        else:
                            for j in range(4):
                                nc.tensor.matmul(ps[rows, 6, 0:P], zPT[:, j, rows], vp[:, u2 % 2, b, P * j:P * j + P],
                                                 start=(j == 0), stop=False)
                            mm = nc.tensor.matmul(ps[rows, 6, 0:P], zPT[0:ST, 4, rows],
                                                  vtok[0:ST, PT, P * br:P * br + P], start=False, stop=True)
                    mm.then_inc(sem("z_av"), 1)

                front(0)
                for u in range(len(ZU)):
                    if u + 1 < len(ZU):
                        front(u + 1)
                    back(u)

            @block.gpsimd
            def _(pool):
                link = linker(pool, "pool_link")
                link(nc.gpsimd.memset(Qb[:, :, :], 0.0))
                pool.sem_inc(sem("Qb_zero"), 1)
                fetch(pool, 0)
                fetch(pool, 2)

            @block.vector
            def _(dve):
                link = linker(dve, "dve_link")
                dve.wait_ge(sem("Qb_zero"), 1)
                for r in range(R):
                    for g in range(G):
                        rows = slice(HD * g, HD * g + HD)
                        c0 = DS * R * g + DS * r
                        nc.vector.tensor_copy(Qb[rows, :, c0:c0 + DS],
                                              qT[rows, r, SEQ:TOK].rearrange("p (b t) -> p b t", t=DS))\
                            .then_inc(sem("Qb_ready"), 1)
                link(nc.vector.memset(orow[:, :, :], 0.0))
                dve.wait_ge(sem("grow_loaded"), 16)

                def front(u):
                    gp, br = ZU[u]
                    if br < 2:
                        copy_keys(dve, nc.vector.tensor_copy, u, 0)
                    nk = NCS if br == 2 else NK
                    dve.wait_ge(sem("z_qk"), u + 1)
                    if u >= 2:
                        dve.wait_ge(sem("z_probs"), u - 1)
                    nc.vector.tensor_tensor_reduce(
                        zS[:, u % 2, 0:nk], ps[:, 2 * (u % 2):2 * (u % 2) + 2, :].rearrange("p a c -> p (a c)")[:, 0:nk],
                        zcb[:, :] if br == 2 else zbias[:, gp, br, :], 1.0, 3e38, ALU.add, ALU.min, zmin[u % 2])\
                        .then_inc(sem("z_scored"), 1)

                def back(u):
                    gp, br = ZU[u]
                    dve.wait_ge(sem("z_probs"), u + 1)
                    link(nc.vector.tensor_scalar(w0, zsum[u % 2], TINY, None, ALU.max))
                    link(nc.vector.reciprocal(w0, w0))
                    gcol = (1, 2, 0)[br]
                    link(nc.vector.tensor_tensor(w0, w0, grow[:, gp, gcol:gcol + 1], ALU.mult))
                    link(nc.vector.tensor_tensor(w1, w0, m1, ALU.mult))
                    link(nc.vector.tensor_tensor(w0, w0, m0, ALU.mult))
                    dve.wait_ge(sem("zPT_done"), u + 1)
                    if u >= 1:
                        dve.wait_ge(sem("z_av"), u)
                    if br == 2:
                        nc.vector.tensor_copy(zPT[0:NCS, 0, :], ps[0:NCS, 7, 0:P]).then_inc(sem("zPT_copied"), 1)
                    else:
                        link(nc.vector.tensor_copy(zPT[:, 0:4, :].rearrange("p j c -> p (j c)"), ps[:, 7, :]))
                        nc.vector.tensor_copy(zPT[0:ST, 4, :], ps[0:ST, 6, 2 * P:3 * P]).then_inc(sem("zPT_copied"), 1)
                    dve.wait_ge(sem("z_av"), u + 1)
                    link(nc.vector.scalar_tensor_tensor(out=orow[:, gp, :], in0=ps[:, 6, 0:HD], scalar=w0,
                                                        in1=orow[:, gp, :], op0=ALU.mult, op1=ALU.add))
                    nc.vector.scalar_tensor_tensor(out=orow[:, gp, :], in0=ps[:, 6, HD:P], scalar=w1,
                                                   in1=orow[:, gp, :], op0=ALU.mult, op1=ALU.add)\
                        .then_inc(sem("z_out"), 1)
                    dve.wait_ge(sem("z_out"), u + 1)

                front(0)
                for u in range(len(ZU)):
                    if u + 1 < len(ZU):
                        front(u + 1)
                    back(u)

            @block.scalar
            def _(act):
                copy = lambda dst, src: nc.scalar.activation(dst, src, ACT.Copy)

                def probs(u):
                    br = ZU[u][1]
                    nk = NCS if br == 2 else NK
                    act.wait_ge(sem("z_scored"), u + 1)
                    if u >= 2:
                        act.wait_ge(sem("zPT_done"), u - 1)
                        act.wait_ge(sem("z_out"), u - 1)
                    nc.scalar.activation(zP[:, u % 2, 0:nk], zS[:, u % 2, 0:nk], ACT.Exp, bias=zmin[u % 2], scale=-1.0,
                                         accum_out=zsum[u % 2]).then_inc(sem("z_probs"), 1)

                probs(0)
                for u in range(1, len(ZU)):
                    if ZU[u][1] < 2:
                        copy_keys(act, copy, u, 1)
                    probs(u)

            @block.sync
            def _(sp):
                sp.wait_ge(sem("gate_spilled"), 16 * DB)
                sp.dma_start(grow[:, :, :], gate_spill.rearrange("(q b) x t c -> (b x t) q c", q=2))\
                    .then_inc(sem("grow_loaded"), 16)
                fetch(sp, 1)
                sp.dma_start(o_spill, o_acc[:, 0:PT, :]).then_inc(sem("o_spilled"), 16)
                fetch(sp, 3)
                for gp in range(2):
                    sp.wait_ge(sem("z_out"), max(u for u, unit in enumerate(ZU) if unit[0] == gp) + 1)
                    sp.dma_start(orow_spill[NB * gp:NB * gp + NB].rearrange("b x t d -> (b x t) d"), orow[:, gp, :])\
                        .then_inc(sem("orow_spilled"), 16)
                sp.wait_ge(sem("orow_spilled"), 32)
                sp.wait_ge(sem("o_spilled"), 16)
        s4.close()
        nsa.close()

        og = sb(ctx, "og", [P, TILES, GH * DV])
        s5 = ExitStack()
        NCH = SEQ // CH
        raw = sb(s5, "raw", [P, 3, TOK])
        e1 = sb(s5, "e1", [P, TOK])
        ls = sb(s5, "ls", [P, TOK])
        bsum = sb(s5, "bsum", [P, TOK])
        eb = sb(s5, "eb", [P, TOK])
        qd = sb(s5, "qd", [P, TOK])
        qi = sb(s5, "qi", [P, SEQ])
        kt = sb(s5, "kt", [P, TOK])
        Wk = sb(s5, "Wk", [P, PT, 4, P])
        W4 = sb(s5, "W4", [P, PT, P])
        vh = sb(s5, "vh", [P, 2, TILES, DV])
        S = sb(s5, "S", [P, 2, DV])
        S0 = sb(s5, "S0", [P, DB, DV])
        reset = sb(s5, "reset", [P, TOK])
        dec = sb(s5, "dec", [P, PT, 5])
        kis = sb(s5, "kis", [P, ST])
        Qm = sb(s5, "Qm", [P, DB, ST])
        bmr = sb(s5, "bmr", [P, DB, ST])
        bmt = sb(s5, "bmt", [ST, DB])
        tris = sb(s5, "tris", [ST, ST])
        ATs = sb(s5, "ATs", [ST, ST])
        aup = sb(s5, "aup", [48, GH * DK])
        AT = e1[:, 0:SEQ]
        k4 = kt[:, 0:SEQ]
        Km = bsum[0:ST, 0:DB * DK]
        ebt = eb[:, 0:SEQ].rearrange("p (t c i) -> p t c i", t=PT, c=4)
        ncore = PT + 1
        with nc.Block() as block:
            @block.tensor
            def _(pe):
                def project(h):
                    if h >= 1:
                        pe.wait_ge(sem("raw_copied"), 3 * h)
                    name = f"gqk{h}"
                    have(pe, name)
                    w = slot(name)
                    for f, lhs in enumerate((lambda k: (w[:, k, 0:P], h_cols(k)), lambda k: (w[:, k, P:2 * P], h_cols(k)))):
                        feature_major(f % 2, lhs, KT).then_inc(sem("g_done"), 1)
                    released[number[name]] = (sem("g_done"), 3 * h + 2)
                    if h == 0:
                        pe.wait_ge(sem("aup_loaded"), 16)
                    pe.wait_ge(sem("raw_copied"), 3 * h + 1)
                    for n in range(3):
                        mm = nc.tensor.matmul(ps[:, n, 0:NF], aup[32:48, DK * h:DK * h + DK],
                                              gaT[32:48, NF * n:NF * n + NF], start=True, stop=True)
                    mm.then_inc(sem("g_done"), 1)
                    have(pe, f"gv{h}")
                    for t in range(TILES):
                        n, c = rows_of(t), TILES * h + t
                        if c >= 2:
                            pe.wait_ge(sem("gv_copied"), c - 1)
                        for k in range(KT):
                            mm = nc.tensor.matmul(ps[0:n, 6 + c % 2, 0:DV], hT[:, k, P * t:P * t + n],
                                                  slot(f"gv{h}")[:, k, :], start=(k == 0), stop=(k == KT - 1))
                        mm.then_inc(sem("gv_done"), 1)
                    released[number[f"gv{h}"]] = (sem("gv_done"), TILES * (h + 1))

                def core(h):
                    pe.wait_ge(sem("elem_done"), h + 1)
                    pe.wait_ge(sem("raw_copied"), 3 * min(h + 2, GH))
                    pe.wait_ge(sem("gv_copied"), TILES * min(h + 2, GH))
                    for t in range(PT):
                        for c in range(4):
                            c0 = P * (t % 4) + CH * c
                            w = min(P, 512 - c0)
                            mm = nc.tensor.matmul(ps[:, t // 4, c0:c0 + w], Wk[:, t, c, :],
                                                  qd[:, P * t + CH * c:P * t + CH * c + w], start=True, stop=True)
                        if t % 4 == 3:
                            mm.then_inc(sem("at_done"), 1)
                    for t in range(PT):
                        mm = nc.tensor.transpose(ps[:, 2 + t // 4, P * (t % 4):P * (t % 4) + P], W4[:, t, :], ident[:, :])
                        if t % 4 == 3:
                            mm.then_inc(sem("w4_done"), 1)
                    pe.wait_ge(sem("qi_ready"), h + 1)
                    for t in range(PT):
                        if t % 4 == 0:
                            pe.wait_ge(sem("k4_copied"), 2 * h + t // 4 + 1)
                            pe.wait_ge(sem("at_copied"), 2 * h + t // 4 + 1)
                        c = PT * h + t
                        if t >= 2:
                            pe.wait_ge(sem("S_ready"), c - 1)
                        nc.tensor.matmul(ps[:, 4 + t % 2, 0:DV], k4[:, P * t:P * t + P], vh[:, h % 2, t, :],
                                         start=True, stop=True).then_inc(sem("u_done"), 1)
                        if t >= 2:
                            pe.wait_ge(sem("go_copied"), ncore * h + t - 1)
                        mm = nc.tensor.matmul(ps[:, 6 + t % 2, 0:DV], AT[:, P * t:P * t + P], vh[:, h % 2, t, :],
                                              start=True, stop=(t == 0))
                        if t >= 1:
                            pe.wait_ge(sem("S_ready"), c)
                            mm = nc.tensor.matmul(ps[:, 6 + t % 2, 0:DV], qi[:, P * t:P * t + P], S[:, t % 2, :],
                                                  start=False, stop=True)
                        mm.then_inc(sem("go_done"), 1)
                    nc.tensor.transpose(ps[0:ST, 2, 0:P], kt[:, SEQ:TOK], ident[:, :])
                    nc.tensor.matmul(ps[0:ST, 0, 0:ST], kis[:, :], qd[:, SEQ:TOK], start=True, stop=True)\
                        .then_inc(sem("sA_done"), 1)
                    pe.wait_ge(sem("sA_ready"), h + 1)
                    pe.wait_ge(sem("S0_loaded"), 16 * (h + 1))
                    pe.wait_ge(sem("go_copied"), ncore * h + PT - 1)
                    vs = vh[0:ST, h % 2, PT, :]
                    nc.tensor.matmul(ps[0:ST, 6, 0:DV], ATs[:, :], vs, start=True, stop=False)
                    for b in range(DB):
                        mm = nc.tensor.matmul(ps[0:ST, 6, 0:DV], Qm[:, b, :], S0[:, b, :], start=False, stop=(b == DB - 1))
                    mm.then_inc(sem("go_done"), 1)
                    pe.wait_ge(sem("S_ready"), PT * (h + 1))
                    for b in range(DB):
                        c = DB * h + b
                        if b >= 2:
                            pe.wait_ge(sem("sS_ready"), c - 1)
                        nc.tensor.matmul(ps[:, 4 + b % 2, 0:DV], Km[:, DK * b:DK * b + DK], vs, start=True, stop=True)\
                            .then_inc(sem("su_done"), 1)
                    pe.wait_ge(sem("sS_ready"), DB * (h + 1))
                    pe.wait_ge(sem("go_copied"), ncore * (h + 1))

                for h in range(GH):
                    project(h)
                    if h >= 1:
                        core(h - 1)
                core(GH - 1)

            @block.gpsimd
            def _(pool):
                link = linker(pool, "pool_link")
                pool.dma_start(aup[32:48, :], a["gla_alpha_up"][0]).then_inc(sem("aup_loaded"), 16)
                for m in (reset, bmr, bmt, Wk):
                    f = m[tuple([slice(None)] * len(m.shape))]
                    nc.gpsimd.memset(f, 0.0 if m is Wk else 1.0).then_inc(sem("g_ones"), 1)
                nc.gpsimd.tensor_copy(tris[:, :], tri[0:ST, 0:ST]).then_inc(sem("g_ones"), 1)
                nc.gpsimd.memset(dec[:, :, 0:1], 1.0).then_inc(sem("g_ones"), 1)
                pool.wait_ge(sem("g_ones"), 6)
                link(nc.gpsimd.memset(reset[:, 0:SEQ:CH], 0.0))
                link(nc.gpsimd.memset(reset[:, SEQ:TOK:DS], 0.0))
                keep = lambda out, base, pattern, cm: link(nc.gpsimd.affine_select(
                    out=out, in_=out, compare_op=ALU.is_ge, fill=0.0, base=base, pattern=pattern, channel_multiplier=cm))
                keep(bmr[:, :, :], 0, [[-DS, DB], [1, ST]], 0)
                keep(bmr[:, :, :], DS - 1, [[DS, DB], [-1, ST]], 0)
                keep(bmt[:, :], 0, [[-DS, DB]], 1)
                keep(bmt[:, :], DS - 1, [[DS, DB]], -1)
                keep(tris[:, :].rearrange("p (b t) -> p b t", t=DS), 0, [[-DS, DB], [0, DS]], 1)
                pool.sem_inc(sem("g_masks"), 1)

            @block.vector
            def _(dve):
                link = linker(dve, "dve_link")
                chunks_of = lambda ap: ap[:, 0:SEQ].rearrange("p (n i) -> p n i", i=CH)
                seqs_of = lambda ap: ap[:, SEQ:TOK].rearrange("p (b t) -> p b t", t=DS)
                tt = nc.vector.tensor_tensor

                def log_sigmoid(h):
                    z = raw[:, 2, :]
                    dve.wait_ge(sem("raw_copied"), 3 * (h + 1))
                    nc.vector.scalar_tensor_tensor(out=ls[:, :], in0=z, scalar=-1.0, in1=z, op0=ALU.mult, op1=ALU.min)\
                        .then_inc(sem("minus_abs"), 1)
                    dve.wait_ge(sem("log1p_ready"), h + 1)
                    link(nc.vector.scalar_tensor_tensor(out=z, in0=z, scalar=0.0, in1=ls[:, :],
                                                        op0=ALU.min, op1=ALU.subtract))

                def elementwise(h):
                    if h >= 1:
                        dve.wait_ge(sem("su_done"), DB * h)
                    q, k, z = raw[:, 0, :], raw[:, 1, :], raw[:, 2, :]
                    nc.vector.tensor_tensor_scan(bsum[:, :], reset[:, :], z, 0.0, ALU.mult, ALU.add)\
                        .then_inc(sem("to_act"), 1)
                    dve.wait_ge(sem("to_act"), 2 * h + 1)
                    link(tt(chunks_of(ls), chunks_of(bsum)[:, :, CH - 1:CH].to_broadcast([P, NCH, CH]), chunks_of(bsum),
                            ALU.subtract))
                    tt(seqs_of(ls), seqs_of(bsum)[:, :, DS - 1:DS].to_broadcast([P, DB, DS]), seqs_of(bsum),
                       ALU.subtract).then_inc(sem("to_act"), 1)
                    dve.wait_ge(sem("from_act"), 3 * h + 1)
                    link(tt(qd[:, :], q, eb[:, :], ALU.mult))
                    dve.wait_ge(sem("from_act"), 3 * h + 2)
                    link(tt(kt[:, :], k, ls[:, :], ALU.mult))
                    dve.wait_ge(sem("from_act"), 3 * h + 3)
                    link(tt(diag(),
                            k[:, 0:SEQ].rearrange("p (t c i) -> p t c i", t=PT, c=4),
                            e1[:, 0:SEQ].rearrange("p (t c i) -> p t c i", t=PT, c=4), ALU.mult))
                    link(tt(kis[:, :], k[:, SEQ:TOK], e1[:, SEQ:TOK], ALU.mult))
                    kc4 = kt[:, 0:SEQ].rearrange("p (t c i) -> p t c i", t=PT, c=4)
                    for c in range(1, 5):
                        dst = Wk[:, :, c, :] if c < 4 else W4[:, :, :]
                        if c > 1:
                            w = CH * (c - 1)
                            link(tt(dst[:, :, 0:w], Wk[:, :, c - 1, 0:w],
                                    ebt[:, :, c - 1, CH - 1:CH].to_broadcast([P, PT, w]), ALU.mult))
                        link(nc.vector.tensor_copy(dst[:, :, CH * (c - 1):CH * c], kc4[:, :, c - 1, :]))
                        link(tt(dec[:, :, c:c + 1], dec[:, :, c - 1:c], ebt[:, :, c - 1, CH - 1:CH], ALU.mult))
                    dve.sem_inc(sem("elem_done"), 1)
                    link(tt(qi[:, :].rearrange("p (t c i) -> p t c i", t=PT, c=4),
                            qd[:, 0:SEQ].rearrange("p (t c i) -> p t c i", t=PT, c=4),
                            dec[:, :, 0:4].unsqueeze(3).to_broadcast([P, PT, 4, CH]), ALU.mult))
                    tt(Qm[:, :, :], qd[:, SEQ:TOK].unsqueeze(1).to_broadcast([P, DB, ST]), bmr[:, :, :], ALU.mult)\
                        .then_inc(sem("qi_ready"), 1)
                    dve.wait_ge(sem("qi_ready"), h + 1)

                def diag():
                    v = Wk[:, :, :, :].rearrange("p t c i -> p t (c i)")
                    return bass.AP(v.tensor, v.offset, [v.ap[0], [4 * P, PT], [P + CH, 4], [1, CH]])

                def core(h):
                    for j in range(2):
                        dve.wait_ge(sem("at_done"), 2 * h + j + 1)
                        tt(AT[:, 512 * j:512 * j + 512].rearrange("p (t i) -> p t i", t=4),
                           ps[:, j, :].rearrange("p (t i) -> p t i", t=4),
                           tri[:, :].unsqueeze(1).to_broadcast([P, 4, P]), ALU.mult).then_inc(sem("at_copied"), 1)
                    for t in range(PT):
                        c = PT * h + t
                        dve.wait_ge(sem("u_done"), c + 1)
                        dst, u = S[:, (t + 1) % 2, :], ps[:, 4 + t % 2, 0:DV]
                        if t >= 1:
                            dve.wait_ge(sem("go_done"), ncore * h + t)
                            dve.wait_ge(sem("S_ready"), c)
                            ins = nc.vector.scalar_tensor_tensor(out=dst, in0=S[:, t % 2, :], scalar=dec[:, t, 4:5],
                                                                 in1=u, op0=ALU.mult, op1=ALU.add)
                        else:
                            ins = nc.vector.tensor_copy(dst, u)
                        ins.then_inc(sem("S_ready"), 1)
                        if t == 0 and h >= 1:
                            dve.wait_ge(sem("pgla_stored"), 16 * h)
                    dve.wait_ge(sem("sA_done"), h + 1)
                    if h == 0:
                        dve.wait_ge(sem("g_masks"), 1)
                    link(tt(Km.rearrange("p (b c) -> p b c", b=DB), ps[0:ST, 2, 0:P].unsqueeze(1).to_broadcast([ST, DB, P]),
                            bmt[:, :].unsqueeze(2).to_broadcast([ST, DB, P]), ALU.mult))
                    tt(ATs[:, :], ps[0:ST, 0, 0:ST], tris[:, :], ALU.mult).then_inc(sem("sA_ready"), 1)
                    dve.wait_ge(sem("go_done"), ncore * (h + 1))
                    for b in range(DB):
                        dve.wait_ge(sem("su_done"), DB * h + b + 1)
                        nc.vector.scalar_tensor_tensor(out=S0[:, b, :], in0=S0[:, b, :],
                                                       scalar=eb[:, SEQ + DS * b + DS - 1:SEQ + DS * b + DS],
                                                       in1=ps[:, 4 + b % 2, 0:DV], op0=ALU.mult, op1=ALU.add)\
                            .then_inc(sem("sS_ready"), 1)

                dve.wait_ge(sem("g_masks"), 1)
                for h in range(GH):
                    log_sigmoid(h)
                    if h >= 1:
                        core(h - 1)
                    elementwise(h)
                core(GH - 1)

            @block.scalar
            def _(act):
                act.wait_ge(sem("vectors"), 16 * 6)

                def project(h):
                    if h >= 1:
                        act.wait_ge(sem("elem_done"), h)
                    for f in range(3):
                        act.wait_ge(sem("g_done"), 3 * h + f + 1)
                        if f < 2:
                            ins = nc.scalar.activation(split3(raw[:, f, :]), banks(f % 2), ACT.Copy,
                                                       scale=DK ** -0.5 if f == 0 else 1.0)
                        else:
                            ins = nc.scalar.activation(split3(raw[:, f, :]), banks(0), ACT.Identity,
                                                       bias=ab_col[:, h:h + 1])
                        ins.then_inc(sem("raw_copied"), 1)
                    act.wait_ge(sem("minus_abs"), h + 1)
                    nc.scalar.activation(ls[:, :], ls[:, :], ACT.Exp).then_inc(sem("act_link"), 1)
                    act.wait_ge(sem("act_link"), h + 1)
                    nc.scalar.activation(ls[:, :], ls[:, :], ACT.Ln, bias=1.0).then_inc(sem("log1p_ready"), 1)
                    for t in range(TILES):
                        n, c = rows_of(t), TILES * h + t
                        act.wait_ge(sem("gv_done"), c + 1)
                        nc.scalar.activation(vh[0:n, h % 2, t, :], ps[0:n, 6 + c % 2, 0:DV], ACT.Copy)\
                            .then_inc(sem("gv_copied"), 1)

                def elementwise(h):
                    act.wait_ge(sem("to_act"), 2 * h + 1)
                    nc.scalar.activation(eb[:, :], bsum[:, :], ACT.Exp, scale=1.0 / TAU).then_inc(sem("from_act"), 1)
                    act.wait_ge(sem("to_act"), 2 * h + 2)
                    nc.scalar.activation(ls[:, :], ls[:, :], ACT.Exp, scale=1.0 / TAU).then_inc(sem("from_act"), 1)
                    nc.scalar.activation(e1[:, :], bsum[:, :], ACT.Exp, scale=-1.0 / TAU).then_inc(sem("from_act"), 1)

                def core(h):
                    for j in range(2):
                        act.wait_ge(sem("w4_done"), 2 * h + j + 1)
                        nc.scalar.activation(k4[:, 512 * j:512 * j + 512], ps[:, 2 + j, :], ACT.Copy)\
                            .then_inc(sem("k4_copied"), 1)
                    for t in range(TILES):
                        n = rows_of(t)
                        act.wait_ge(sem("go_done"), ncore * h + t + 1)
                        nc.scalar.activation(og[0:n, t, DV * h:DV * h + DV], ps[0:n, 6 + t % 2, 0:DV], ACT.Copy)\
                            .then_inc(sem("go_copied"), 1)

                for h in range(GH):
                    project(h)
                    if h >= 1:
                        core(h - 1)
                    elementwise(h)
                core(GH - 1)

            @block.sync
            def _(sp):
                sp.dma_start(S0[:, :, :], a["state_gla"][0, :, 0].rearrange("b k v -> k b v")).then_inc(sem("S0_loaded"), 16)
                for h in range(GH):
                    if h == 0:
                        load_chunks(sp, "gqk2", "gqk2")
                        load_chunks(sp, "gv2", "gv2")
                    if h == 1:
                        load_chunks(sp, "gqk3", "gv3")
                    sp.wait_ge(sem("S_ready"), PT * (h + 1))
                    sp.dma_start(p_gla[0, 0, h], S[:, 0, :]).then_inc(sem("pgla_stored"), 16)
                    for b in range(0, DB, 2):
                        sp.wait_ge(sem("sS_ready"), DB * h + b + 2)
                        sp.dma_start(s_gla[0, b:b + 2, h].rearrange("b k v -> k b v"), S0[:, b:b + 2, :])\
                            .then_inc(sem("sgla_stored"), 16)
                    sp.wait_ge(sem("sgla_stored"), 8 * DB * (h + 1))
                    if h + 1 < GH:
                        sp.dma_start(S0[:, :, :], a["state_gla"][0, :, h + 1].rearrange("b k v -> k b v"))\
                            .then_inc(sem("S0_loaded"), 16)
                    if h == 1:
                        load_chunks(sp, "za0", "za1")
                load_chunks(sp, "zb0", "zb1")
                sp.wait_ge(sem("pgla_stored"), 16 * GH)
        s5.close()

        mixers = ExitStack()
        oT = sb(mixers, "oT", [P, 4, TOK])
        ogT = sb(mixers, "ogT", [P, KT, TOK])
        s6 = ExitStack()
        oN = sb(s6, "oN", [P, TILES, 512])
        zz = sb(s6, "zz", [P, 2, TOK])
        zg = sb(s6, "zg", [P, 2, TOK])
        junk = zg[:, 0, 0:DV]
        gss = sb(s6, "gss", [P, TILES * GH])
        grs = sb(s6, "grs", [P, TILES * GH])
        ogv = og[:, :, :].rearrange("p t (h v) -> p (t h) v", h=GH)
        NZ = 12
        with nc.Block() as block:
            @block.tensor
            def _(pe):
                def gates(f):
                    name = f"za{f // 2}" if f < 4 else f"zb{(f - 4) // 2}"
                    have(pe, name)
                    if f >= 2:
                        pe.wait_ge(sem("z_copied"), 2 * (f - 1))
                    w = slot(name)
                    feature_major(f % 2, lambda k: (w[:, k, P * (f % 2):P * (f % 2) + P], h_cols(k)), KT)\
                        .then_inc(sem("z_done"), 1)
                    released[number[name]] = (sem("z_done"), f + 1)

                def turn(f):
                    src = oN[:, :, P * f:P * f + P] if f < 4 else og[:, :, P * (f - 4):P * (f - 4) + P]
                    if f == 0:
                        pe.wait_ge(sem("oN_loaded"), 16 * (1 + DB))
                    if f == 4:
                        pe.wait_ge(sem("og_normed"), 2)
                    for j in range(3):
                        last = 3 * f + (0, -1, 1)[j]
                        if last > 0:
                            pe.wait_ge(sem("oT_copied"), last)
                        for t in range(4 * j, min(4 * j + 4, TILES)):
                            n = rows_of(t)
                            mm = nc.tensor.transpose(ps[:, 6 + j % 2, P * (t % 4):P * (t % 4) + n], src[0:n, t, :],
                                                     ident[0:n, 0:n])
                        mm.then_inc(sem("oT_done"), 1)

                for f in range(NZ):
                    gates(f)
                    if f >= 1:
                        turn(f - 1)
                turn(NZ - 1)

            @block.vector
            def _(dve):
                link = linker(dve, "dve_link")
                dve.wait_ge(sem("g_squares"), GH * TILES)
                link(nc.vector.tensor_scalar(grs[:, :], gss[:, :], 1.0 / DV, EPS, ALU.mult, ALU.add))
                dve.sem_inc(sem("g_var"), 1)
                dve.wait_ge(sem("g_sd"), 1)
                link(nc.vector.reciprocal(grs[:, :], gss[:, :]))
                NG = GH * PT
                nc.vector.tensor_tensor(ogv[:, 0:NG, :], ogv[:, 0:NG, :],
                                        grs[:, 0:NG].unsqueeze(2).to_broadcast([P, NG, DV]), ALU.mult)\
                    .then_inc(sem("og_normed"), 1)
                nc.vector.tensor_tensor(ogv[0:ST, NG:, :], ogv[0:ST, NG:, :],
                                        grs[0:ST, NG:].unsqueeze(2).to_broadcast([ST, GH, DV]), ALU.mult)\
                    .then_inc(sem("og_normed"), 1)
                for f in range(NZ):
                    dve.wait_ge(sem("z_copied"), 2 * (f + 1))
                    z = zz[:, f % 2, :]
                    link(nc.vector.tensor_tensor(z, z, zg[:, f % 2, :], ALU.mult))
                    for j in range(3):
                        dve.wait_ge(sem("oT_done"), 3 * f + j + 1)
                        w = min(512, TOK - 512 * j)
                        c = slice(512 * j, 512 * j + w)
                        src = ps[:, 6 + j % 2, 0:w]
                        if f < 4:
                            ins = nc.vector.tensor_tensor(oT[:, f, c], src, z[:, c], ALU.mult)
                        else:
                            ins = nc.vector.scalar_tensor_tensor(out=ogT[:, f - 4, c], in0=src,
                                                                 scalar=gn_col[:, f % 2:f % 2 + 1], in1=z[:, c],
                                                                 op0=ALU.mult, op1=ALU.mult)
                        ins.then_inc(sem("oT_copied"), 1)

            @block.gpsimd
            def _(pool):
                pool.memset(gss[:, :], 1.0).then_inc(sem("gss_ones"), 1)

            @block.scalar
            def _(act):
                act.wait_ge(sem("gss_ones"), 1)
                for t in range(TILES):
                    n = rows_of(t)
                    for h in range(GH):
                        c = GH * t + h
                        if c >= 1:
                            act.wait_ge(sem("g_squares"), c)
                        nc.scalar.activation(junk[0:n, :], og[0:n, t, DV * h:DV * h + DV], ACT.Square,
                                             accum_out=gss[0:n, c:c + 1]).then_inc(sem("g_squares"), 1)
                act.wait_ge(sem("g_var"), 1)
                act.wait_ge(sem("g_squares"), GH * TILES)
                nc.scalar.activation(gss[:, :], grs[:, :], ACT.Sqrt).then_inc(sem("g_sd"), 1)
                for f in range(NZ):
                    act.wait_ge(sem("z_done"), f + 1)
                    if f >= 2:
                        act.wait_ge(sem("oT_copied"), 3 * (f - 1))
                    nc.scalar.activation(split3(zz[:, f % 2, :]), banks(f % 2), ACT.Copy).then_inc(sem("z_copied"), 1)
                    nc.scalar.activation(split3(zg[:, f % 2, :]), banks(f % 2), ACT.Sigmoid).then_inc(sem("z_copied"), 1)

            @block.sync
            def _(sp):
                sp.dma_start(oN[:, 0:PT, :], o_spill).then_inc(sem("oN_loaded"), 16)
                for b in range(DB):
                    sp.dma_start(oN[DS * b:DS * b + DS, PT, :].rearrange("t (x d) -> t x d", d=HD),
                                 orow_spill[b].rearrange("x t d -> t x d")).then_inc(sem("oN_loaded"), 16)
                load_chunks(sp, "zb2", "wa0")
        s6.close()

        mixT = og[:, :, :].rearrange("p t c -> p (t c)")[:, 0:KT * TOK].rearrange("p (k c) -> p k c", k=KT)
        s7 = ExitStack()
        sg = sb(s7, "sg", [P, 4, TOK])
        ta = sb(s7, "ta", [P, 2, TOK])
        tb = sb(s7, "tb", [P, TOK])
        kinds = ("ma", "wa", "mb", "wb")
        steps = [(j, kind, s) for j in range(4) for kind in kinds for s in range(2)]
        with nc.Block() as block:
            def drained(n):
                j, kind, s = steps[n]
                who = "m_gated" if kind[0] == "m" else "m_merged"
                return sem(who), sum(1 for q in steps[:n + 1] if q[1][0] == kind[0])

            @block.tensor
            def _(pe):
                for n, (j, kind, s) in enumerate(steps):
                    name = f"{kind}{j}"
                    have(pe, name)
                    if n >= 2:
                        pe.wait_ge(*drained(n - 2))
                    w = slot(name)
                    if kind == "wa":
                        rhs = lambda k: (lambda i: oT[:, k, NF * i:NF * i + NF])
                    elif kind == "wb":
                        rhs = lambda k: (lambda i: ogT[:, k, NF * i:NF * i + NF])
                    else:
                        rhs = h_cols
                    feature_major(n % 2, lambda k: (w[:, k, P * s:P * s + P], rhs(k)), 4 if kind == "wa" else KT)\
                        .then_inc(sem("m_done"), 1)
                    released[number[name]] = (sem("m_done"), n + 1)

            @block.scalar
            def _(act):
                for n, (j, kind, s) in enumerate(steps):
                    if kind[0] != "m":
                        continue
                    act.wait_ge(sem("m_done"), n + 1)
                    i = s if kind == "ma" else 2 + s
                    if j >= 1:
                        act.wait_ge(*drained(steps.index((j - 1, "w" + kind[1], s))))
                    nc.scalar.activation(split3(sg[:, i, :]), banks(n % 2), ACT.Sigmoid).then_inc(sem("m_gated"), 1)

            @block.vector
            def _(dve):
                link = linker(dve, "dve_link")
                for n, (j, kind, s) in enumerate(steps):
                    if kind[0] != "w":
                        continue
                    dve.wait_ge(sem("m_done"), n + 1)
                    i = s if kind == "wa" else 2 + s
                    dve.wait_ge(*drained(steps.index((j, "m" + kind[1], s))))
                    dst = ta[:, s, :] if kind == "wa" else tb[:, :]
                    nc.vector.tensor_tensor(split3(dst), banks(n % 2), split3(sg[:, i, :]), ALU.mult)\
                        .then_inc(sem("m_merged"), 1)
                    if kind == "wb":
                        dve.wait_ge(*drained(n))
                        link(nc.vector.tensor_tensor(mixT[:, 2 * j + s, :], ta[:, s, :], tb[:, :], ALU.add))

            @block.sync
            def _(sp):
                load_chunks(sp, "mb0", "wo3")
        s7.close()
        mixers.close()

        s8 = ExitStack()
        FR = mybir.dt.float32r
        mH = sb(s8, "mH", [P, 2, KT, P], FR)
        mL = sb(s8, "mL", [P, 2, KT, P], FR)
        wH = sb(s8, "wH", [P, KT, D], FR)
        wL = sb(s8, "wL", [P, KT, D], FR)
        free = hT[:, :, :].rearrange("p k c -> p (k c)")
        xr = free[:, 0:3 * D].rearrange("p (n c) -> p n c", c=D)
        yy = free[:, 3 * D:6 * D].rearrange("p (n c) -> p n c", c=D)
        jk, fg = free[:, 6 * D:7 * D], free[:, 7 * D:8 * D]
        fst = sb(s8, "fst", [P, 2 * TILES])
        with nc.Block() as block:
            @block.tensor
            def _(pe):
                for t in range(TILES):
                    n = rows_of(t)
                    if t >= 4:
                        pe.wait_ge(sem("y_added"), t - 3)
                    pe.wait_ge(sem("mH_ready"), t + 1)
                    pe.wait_ge(sem("mL_ready"), t + 1)
                    width = 256 if t == 0 else 512
                    for c0 in range(0, D, width):
                        if t == 0:
                            pe.wait_ge(sem("wH_ready"), c0 // 256 + 1)
                            pe.wait_ge(sem("wL_ready"), c0 // 256 + 1)
                        for k in range(KT):
                            for i, (m, w) in enumerate(((mH, wH), (mH, wL), (mL, wH))):
                                mm = nc.tensor.matmul(
                                    ps[0:n, 2 * (t % 4) + c0 // 512, c0 % 512:c0 % 512 + width],
                                    m[:, t % 2, k, 0:n], w[:, k, c0:c0 + width],
                                    start=(k == 0 and i == 0), stop=(k == KT - 1 and i == 2))
                    mm.then_inc(sem("y_done"), 1)

            @block.vector
            def _(dve):
                link = linker(dve, "dve_link")

                def low_of_mix(t):
                    dve.wait_ge(sem("mH_ready"), t + 1)
                    if t >= 2:
                        dve.wait_ge(sem("y_done"), t - 1)
                    n = rows_of(t)
                    nc.vector.tensor_tensor(mL[:, t % 2, :, 0:n], mixT[:, :, P * t:P * t + n],
                                            mH[:, t % 2, :, 0:n].bitcast(F32), ALU.subtract)\
                        .then_inc(sem("mL_ready"), 1)

                low_of_mix(0)
                for j in range(4):
                    dve.wait_ge(sem("wH_ready"), j + 1)
                    c = slice(256 * j, 256 * j + 256)
                    nc.vector.tensor_tensor(wL[:, :, c], slot(f"wo{j}"), wH[:, :, c].bitcast(F32), ALU.subtract)\
                        .then_inc(sem("wL_ready"), 1)
                low_of_mix(1)
                dve.wait_ge(sem("fg_loaded"), 16)
                for t in range(TILES):
                    n = rows_of(t)
                    dve.wait_ge(sem("y_done"), t + 1)
                    if t + 2 < TILES:
                        low_of_mix(t + 2)
                    dve.wait_ge(sem(f"xr_loaded{t % 3}"), 16 * (t // 3 + 1))
                    if t >= 3:
                        dve.wait_ge(sem(f"y_stored{t % 3}"), 16 * (t // 3))
                    y = yy[0:n, t % 3, :]
                    nc.vector.tensor_tensor(y, ps[0:n, 2 * (t % 4):2 * (t % 4) + 2, :].rearrange("p a c -> p (a c)"),
                                            xr[0:n, t % 3, :], ALU.add).then_inc(sem("y_added"), 1)
                    ss, r = fst[0:n, 2 * t:2 * t + 1], fst[0:n, 2 * t + 1:2 * t + 2]
                    dve.wait_ge(sem("y_squared"), t + 1)
                    nc.vector.tensor_scalar(r, ss, 1.0 / D, EPS, ALU.mult, ALU.add).then_inc(sem("y_var"), 1)
                    dve.wait_ge(sem("y_sd"), t + 1)
                    link(nc.vector.reciprocal(r, ss))
                    nc.vector.scalar_tensor_tensor(out=y, in0=y, scalar=r, in1=fg[0:n, :], op0=ALU.mult, op1=ALU.mult)\
                        .then_inc(sem("y_ready"), 1)

            @block.scalar
            def _(act):
                def high_of_mix(t):
                    if t >= 2:
                        act.wait_ge(sem("y_done"), t - 1)
                        act.wait_ge(sem("mL_ready"), t - 1)
                    n = rows_of(t)
                    nc.scalar.activation(mH[:, t % 2, :, 0:n], mixT[:, :, P * t:P * t + n], ACT.Copy)\
                        .then_inc(sem("mH_ready"), 1)

                high_of_mix(0)
                for j in range(4):
                    have(act, f"wo{j}")
                    nc.scalar.activation(wH[:, :, 256 * j:256 * j + 256], slot(f"wo{j}"), ACT.Copy)\
                        .then_inc(sem("wH_ready"), 1)
                high_of_mix(1)
                for t in range(TILES):
                    if t + 2 < TILES:
                        high_of_mix(t + 2)
                    n = rows_of(t)
                    ss, r = fst[0:n, 2 * t:2 * t + 1], fst[0:n, 2 * t + 1:2 * t + 2]
                    act.wait_ge(sem("y_added"), t + 1)
                    if t >= 1:
                        act.wait_ge(sem("y_squared"), t)
                    nc.scalar.activation(jk[0:n, :], yy[0:n, t % 3, :], ACT.Square, accum_out=ss)\
                        .then_inc(sem("y_squared"), 1)
                    act.wait_ge(sem("y_var"), t + 1)
                    nc.scalar.activation(ss, r, ACT.Sqrt).then_inc(sem("y_sd"), 1)

            @block.sync
            def _(sp):
                sp.dma_start(fg[:, :], a["final_norm_g"].unsqueeze(0).to_broadcast([P, D])).then_inc(sem("fg_loaded"), 16)

                def load_x(t):
                    src = a["x_prompt"][0, P * t:P * t + P, :] if t < PT else \
                        a["x_sample"].rearrange("b s d -> (b s) d")
                    sp.dma_start(xr[0:rows_of(t), t % 3, :], src).then_inc(sem(f"xr_loaded{t % 3}"), 16)

                for t in range(3):
                    load_x(t)
                for t in range(TILES):
                    if t + 3 < TILES:
                        sp.wait_ge(sem("y_added"), t + 1)
                        load_x(t + 3)
                    sp.wait_ge(sem("y_ready"), t + 1)
                    dst = y_p[0, P * t:P * t + P, :] if t < PT else y_s.rearrange("b s d -> (b s) d")
                    sp.dma_start(dst, yy[0:rows_of(t), t % 3, :]).then_inc(sem(f"y_stored{t % 3}"), 16)
                for s in range(3):
                    sp.wait_ge(sem(f"y_stored{s}"), 16 * 3)
                sp.wait_ge(sem("stored"), 16 * out_count["stored"])
                sp.wait_ge(sem("sgla_stored"), 8 * DB * GH)
        s8.close()


_INS = ["x_prompt", "x_sample", "cache_k_cmp", "cache_v_cmp", "cache_k_slc", "cache_v_slc", "cache_k_win",
        "cache_v_win", "state_gla", "page_table", "norm_g", "w_in", "phi_k_pe", "phi_k_w1", "phi_k_w2",
        "phi_v_pe", "phi_v_w1", "phi_v_w2", "gla_alpha_up", "gla_alpha_b", "gla_norm_g", "w_branch_a",
        "w_branch_b", "w_out", "final_norm_g"]
_OUTS = ([(1, SEQ, D), (DB, DS, D)] + [(1, 1, SEQ, G, HD)] * 4 + [(1, 1, WIN, G, HD)] * 2 + [(1, 1, GH, DK, DV)]
         + [(1, DB, DS, G, HD)] * 4 + [(1, DB, WIN, G, HD)] * 2 + [(1, DB, GH, DK, DV)])


def kernel(**inputs):
    import numpy as _np
    import concourse.bacc as _bacc
    from concourse import mybir as _mybir
    from concourse.bass_utils import run_bass_kernel_spmd as _run

    nc = _bacc.Bacc("TRN2", target_bir_lowering=False, num_devices=1)
    arrays, args = {}, {}
    for name in _INS:
        x = _np.ascontiguousarray(inputs[name])
        arrays[f"in_{name}"] = x
        args[name] = nc.dram_tensor(f"in_{name}", x.shape, _mybir.dt.from_np(x.dtype), kind="ExternalInput").ap()
    outs = [nc.dram_tensor(f"out_{i}", shape, F32, kind="ExternalOutput").ap() for i, shape in enumerate(_OUTS)]
    hybrid_step(nc, args, outs)
    r = _run(nc, [arrays], core_ids=[0])
    return tuple(r.results[0][f"out_{i}"] for i in range(len(_OUTS)))
```
